# Optimizing a Trainium2 kernel written in Bass

```python
import math
import jax, jax.numpy as jnp
from jax import lax
import numpy as np

D_MODEL = 2048
BATCH = 1
SEQ = 256
DEPTH = 2

DIFF_HEADS = 8
DIFF_QK_DIM = 64
DIFF_V_DIM = 128
DIFF_WIDTH = DIFF_HEADS * DIFF_V_DIM
MLA_HEADS = 8
MLA_Q_RANK = 512
MLA_KV_RANK = 512
MLA_NOPE_DIM = 128
MLA_ROPE_DIM = 64
MLA_V_DIM = 128
MLA_WIDTH = MLA_HEADS * MLA_V_DIM
MIX_WIDTH = DIFF_WIDTH + MLA_WIDTH
IN_SIZES = (
    DIFF_HEADS * 2 * DIFF_QK_DIM,
    DIFF_HEADS * 2 * DIFF_QK_DIM,
    DIFF_WIDTH,
    DIFF_WIDTH,
    MLA_Q_RANK,
    MLA_KV_RANK,
    MLA_ROPE_DIM,
    MLA_WIDTH,
)
IN_WIDTH = sum(IN_SIZES)
ROPE_THETA = 10000.0
NUM_BUCKETS = 32
MAX_DISTANCE = 128
BLOCK_Q = 128
EPS = 1e-6
NEG_INF = -1e30


def _rms_norm(x, g):
    xf = x.astype(jnp.float32)
    y = xf * lax.rsqrt(jnp.mean(xf * xf, axis=-1, keepdims=True) + EPS)
    return (y * g.astype(jnp.float32)).astype(x.dtype)

def _rope_tables(seq):
    pos = jnp.arange(seq, dtype=jnp.float32)
    inv = 1.0 / (ROPE_THETA ** (jnp.arange(0, MLA_ROPE_DIM, 2, dtype=jnp.float32) / MLA_ROPE_DIM))
    ang = pos[:, None] * inv[None, :]
    ang = jnp.concatenate([ang, ang], axis=-1)
    return jnp.cos(ang), jnp.sin(ang)

def _apply_rope(x, cos, sin):
    half = x.shape[-1] // 2
    x1, x2 = x[..., :half], x[..., half:]
    rot = jnp.concatenate([-x2, x1], axis=-1)
    return x * cos.astype(x.dtype) + rot * sin.astype(x.dtype)

def _t5_bucket(dist):
    n = jnp.maximum(dist, 0)
    max_exact = NUM_BUCKETS // 2
    nf = jnp.maximum(n, 1).astype(jnp.float32)
    large = max_exact + (jnp.log(nf / max_exact) / math.log(MAX_DISTANCE / max_exact)
                         * (NUM_BUCKETS - max_exact)).astype(jnp.int32)
    large = jnp.minimum(large, NUM_BUCKETS - 1)
    return jnp.where(n < max_exact, n, large)

def _block_sweep(one_block, seq):
    starts = jnp.arange(seq // BLOCK_Q, dtype=jnp.int32) * BLOCK_Q
    out = lax.map(one_block, starts)
    out = jnp.moveaxis(out, 0, 1)
    b, nb, q, h, dv = out.shape
    return out.reshape(b, nb * q, h, dv)

def _diff_attention(q, k, v, lam, bias_table):
    seq = q.shape[1]
    kpos = jnp.arange(seq, dtype=jnp.int32)
    scale = DIFF_QK_DIM ** -0.5
    table = bias_table.astype(jnp.float32)

    def one_block(start):
        qb = lax.dynamic_slice_in_dim(q, start, BLOCK_Q, axis=1)
        s = jnp.einsum('bqhmd,bkhmd->bmhqk', qb, k).astype(jnp.float32) * scale
        dist = (start + jnp.arange(BLOCK_Q, dtype=jnp.int32))[:, None] - kpos[None, :]
        bias = jnp.transpose(table[_t5_bucket(dist)], (2, 0, 1))
        s = jnp.where((dist >= 0)[None, None, None], s + bias[None, None], NEG_INF)
        p = jax.nn.softmax(s, axis=-1)
        w = p[:, 0] - lam * p[:, 1]
        return jnp.einsum('bhqk,bkhd->bqhd', w.astype(v.dtype), v)

    return _block_sweep(one_block, seq)

def _mla_attention(q_nope, q_rope, k_nope, k_rope, v):
    seq = q_nope.shape[1]
    kpos = jnp.arange(seq, dtype=jnp.int32)
    scale = (MLA_NOPE_DIM + MLA_ROPE_DIM) ** -0.5

    def one_block(start):
        qn = lax.dynamic_slice_in_dim(q_nope, start, BLOCK_Q, axis=1)
        qr = lax.dynamic_slice_in_dim(q_rope, start, BLOCK_Q, axis=1)
        s = (jnp.einsum('bqhd,bkhd->bhqk', qn, k_nope)
             + jnp.einsum('bqhr,bkr->bhqk', qr, k_rope)).astype(jnp.float32) * scale
        dist = (start + jnp.arange(BLOCK_Q, dtype=jnp.int32))[:, None] - kpos[None, :]
        s = jnp.where((dist >= 0)[None, None], s, NEG_INF)
        p = jax.nn.softmax(s, axis=-1)
        return jnp.einsum('bhqk,bkhd->bqhd', p.astype(v.dtype), v)

    return _block_sweep(one_block, seq)

def first_inputs(seed: int = 0) -> dict:
    key = jax.random.key(seed)
    ks = jax.random.split(key, 12)
    f32 = jnp.float32
    x = jax.random.normal(ks[0], (BATCH, SEQ, D_MODEL), f32)
    norm_g = 1.0 + 0.02 * jax.random.normal(ks[1], (DEPTH, D_MODEL), f32)
    w_in = jax.random.normal(ks[2], (DEPTH, D_MODEL, IN_WIDTH), f32) * D_MODEL ** -0.5
    diff_lambda = 0.1 * jax.random.normal(ks[3], (DEPTH, 4, DIFF_QK_DIM), f32)
    diff_subln_g = 1.0 + 0.02 * jax.random.normal(ks[4], (DEPTH, DIFF_V_DIM), f32)
    rel_bias_table = 0.2 * jax.random.normal(ks[5], (NUM_BUCKETS, DIFF_HEADS), f32)
    mla_q_norm_g = 1.0 + 0.02 * jax.random.normal(ks[6], (DEPTH, MLA_Q_RANK), f32)
    w_uq = jax.random.normal(ks[7], (DEPTH, MLA_Q_RANK, MLA_HEADS * (MLA_NOPE_DIM + MLA_ROPE_DIM)), f32) * MLA_Q_RANK ** -0.5
    mla_kv_norm_g = 1.0 + 0.02 * jax.random.normal(ks[8], (DEPTH, MLA_KV_RANK), f32)
    w_ukv = jax.random.normal(ks[9], (DEPTH, MLA_KV_RANK, MLA_HEADS * (MLA_NOPE_DIM + MLA_V_DIM)), f32) * MLA_KV_RANK ** -0.5
    w_out = jax.random.normal(ks[10], (DEPTH, MIX_WIDTH, D_MODEL), f32) * MIX_WIDTH ** -0.5
    final_norm_g = 1.0 + 0.02 * jax.random.normal(ks[11], (D_MODEL,), f32)
    return {"x": x, "norm_g": norm_g, "w_in": w_in, "diff_lambda": diff_lambda,
            "diff_subln_g": diff_subln_g, "rel_bias_table": rel_bias_table,
            "mla_q_norm_g": mla_q_norm_g, "w_uq": w_uq, "mla_kv_norm_g": mla_kv_norm_g,
            "w_ukv": w_ukv, "w_out": w_out, "final_norm_g": final_norm_g}

def first_block(x, norm_g, w_in, diff_lambda, diff_subln_g, rel_bias_table,
              mla_q_norm_g, w_uq, mla_kv_norm_g, w_ukv, w_out, final_norm_g):
    b, seq, _ = x.shape
    cos, sin = _rope_tables(seq)
    split_points = [int(v) for v in np.cumsum(IN_SIZES)[:-1]]
    for l in range(DEPTH):
        h = _rms_norm(x, norm_g[l])
        proj = jnp.einsum('bsd,de->bse', h, w_in[l])
        q_a, k_a, v_a, z_a, c_q, c_kv, k_r, z_b = jnp.split(proj, split_points, axis=-1)

        lambda_init = 0.8 - 0.6 * math.exp(-0.3 * l)
        lp = diff_lambda[l].astype(jnp.float32)
        lam = (jnp.exp(jnp.sum(lp[0] * lp[1])) - jnp.exp(jnp.sum(lp[2] * lp[3])) + lambda_init)
        qa = q_a.reshape(b, seq, DIFF_HEADS, 2, DIFF_QK_DIM)
        ka = k_a.reshape(b, seq, DIFF_HEADS, 2, DIFF_QK_DIM)
        va = v_a.reshape(b, seq, DIFF_HEADS, DIFF_V_DIM)
        o_a = _diff_attention(qa, ka, va, lam, rel_bias_table)
        o_a = _rms_norm(o_a, diff_subln_g[l]) * (1.0 - lambda_init)
        o_a = o_a.reshape(b, seq, DIFF_WIDTH) * jax.nn.silu(z_a)

        q_b = jnp.einsum('bsr,re->bse', _rms_norm(c_q, mla_q_norm_g[l]), w_uq[l])
        q_b = q_b.reshape(b, seq, MLA_HEADS, MLA_NOPE_DIM + MLA_ROPE_DIM)
        q_nope, q_rope = q_b[..., :MLA_NOPE_DIM], q_b[..., MLA_NOPE_DIM:]
        q_rope = _apply_rope(q_rope, cos[:, None, :], sin[:, None, :])
        kv = jnp.einsum('bsr,re->bse', _rms_norm(c_kv, mla_kv_norm_g[l]), w_ukv[l])
        kv = kv.reshape(b, seq, MLA_HEADS, MLA_NOPE_DIM + MLA_V_DIM)
        k_nope, v_b = kv[..., :MLA_NOPE_DIM], kv[..., MLA_NOPE_DIM:]
        k_rope = _apply_rope(k_r, cos, sin)
        o_b = _mla_attention(q_nope, q_rope, k_nope, k_rope, v_b)
        o_b = o_b.reshape(b, seq, MLA_WIDTH) * jax.nn.silu(z_b)

        mixed = jnp.concatenate([o_a, o_b], axis=-1)
        x = x + jnp.einsum('bse,ed->bsd', mixed, w_out[l])
    return _rms_norm(x, final_norm_g)


DEPTH_2 = 1

HEAD_DIM = 64
ATTN_HEADS = D_MODEL // 128
KV_HEADS = ATTN_HEADS // 4
Q_DIM = ATTN_HEADS * HEAD_DIM
KV_DIM = KV_HEADS * HEAD_DIM
WINDOW = 128
ATTN_BLOCK = 128
D_INNER = D_MODEL
SSM_HEAD_DIM = 64
SSM_HEADS = D_INNER // SSM_HEAD_DIM
SSM_GROUPS = 4
D_STATE = 128
CONV_WIDTH = 4
CHUNK = 128
CONV_DIM = D_INNER + 2 * SSM_GROUPS * D_STATE
FFN_HIDDEN = -(-(8 * D_MODEL) // (3 * 256)) * 256
PLE_DIM = 256
IN_DIM = Q_DIM + 2 * KV_DIM + D_INNER + CONV_DIM + SSM_HEADS + 2 * D_MODEL
NORM_EPS = 1e-6
SSM_NORM_EPS = 1e-5


def rmsnorm(x, g, eps=NORM_EPS):
    xf = x.astype(jnp.float32)
    y = xf * lax.rsqrt(jnp.mean(xf * xf, axis=-1, keepdims=True) + eps)
    return (y * g.astype(jnp.float32)).astype(x.dtype)

def apply_rope(t, positions):
    half = HEAD_DIM // 2
    inv_freq = ROPE_THETA ** (-jnp.arange(half, dtype=jnp.float32) * 2.0 / HEAD_DIM)
    ang = positions.astype(jnp.float32)[..., None] * inv_freq
    cos, sin = jnp.cos(ang)[:, :, None, :], jnp.sin(ang)[:, :, None, :]
    t1, t2 = t[..., :half], t[..., half:]
    return jnp.concatenate([t1 * cos - t2 * sin, t2 * cos + t1 * sin], axis=-1)

def sliding_window_sink_attention(q, k, v, sinks):
    b, s = q.shape[0], q.shape[1]
    nb = s // ATTN_BLOCK
    grp = ATTN_HEADS // KV_HEADS
    qb = q.reshape(b, nb, ATTN_BLOCK, KV_HEADS, grp, HEAD_DIM)

    def banded(t):
        tb = t.reshape(b, nb, ATTN_BLOCK, KV_HEADS, HEAD_DIM)
        prev = jnp.pad(tb, ((0, 0), (1, 0), (0, 0), (0, 0), (0, 0)))[:, :-1]
        return jnp.concatenate([prev, tb], axis=2)

    kw, vw = banded(k), banded(v)
    scores = jnp.einsum('bnqhgd,bnkhd->bnhgqk', qb, kw) * (HEAD_DIM ** -0.5)
    qi = jnp.arange(ATTN_BLOCK)[:, None] + ATTN_BLOCK
    kj = jnp.arange(2 * ATTN_BLOCK)[None, :]
    dist = qi - kj
    key_pos = (jnp.arange(nb) * ATTN_BLOCK)[:, None, None] - ATTN_BLOCK + kj[None]
    valid = (dist >= 0)[None] & (dist < WINDOW)[None] & (key_pos >= 0)
    scores = jnp.where(valid[None, :, None, None], scores, -jnp.inf)
    sink = sinks.astype(jnp.float32).reshape(KV_HEADS, grp)[None, None, :, :, None]
    m = jnp.maximum(scores.max(axis=-1), sink)
    e = jnp.exp(scores - m[..., None])
    probs = e / (e.sum(axis=-1) + jnp.exp(sink - m))[..., None]
    out = jnp.einsum('bnhgqk,bnkhd->bnqhgd', probs, vw)
    return out.reshape(b, s, Q_DIM)

def causal_depthwise_conv(x, w, bias):
    out = lax.conv_general_dilated(
        x, w[:, None, :], window_strides=(1,), padding=[(CONV_WIDTH - 1, 0)],
        dimension_numbers=('NWC', 'WIO', 'NWC'), feature_group_count=x.shape[-1])
    return out + bias

def ssd_chunked(xh, dt, a_neg, bm, cm):
    b, s = xh.shape[0], xh.shape[1]
    nc = s // CHUNK
    e_per = SSM_HEADS // SSM_GROUPS
    xd = (xh * dt[..., None]).reshape(b, nc, CHUNK, SSM_GROUPS, e_per, SSM_HEAD_DIM)
    a = jnp.transpose((dt * a_neg).reshape(b, nc, CHUNK, SSM_GROUPS, e_per), (0, 1, 3, 4, 2))
    a_cs = jnp.cumsum(a, axis=-1)
    bc = bm.reshape(b, nc, CHUNK, SSM_GROUPS, D_STATE)
    cc = cm.reshape(b, nc, CHUNK, SSM_GROUPS, D_STATE)
    tril = jnp.tril(jnp.ones((CHUNK, CHUNK), dtype=bool))
    diff = a_cs[..., :, None] - a_cs[..., None, :]
    decay = jnp.where(tril, jnp.exp(jnp.where(tril, diff, 0.0)), 0.0)
    cb = jnp.einsum('bclgn,bcsgn->bcgls', cc, bc)
    y_diag = jnp.einsum('bcgels,bcsgep->bclgep', cb[:, :, :, None] * decay, xd)
    decay_states = jnp.exp(a_cs[..., -1:] - a_cs)
    states = jnp.einsum('bclgn,bcgel,bclgep->bcgepn', bc, decay_states, xd)
    chunk_decay = jnp.exp(a_cs[..., -1])

    def step(carry, inp):
        st, dec = inp
        return carry * dec[..., None, None] + st, carry

    init = jnp.zeros((b, SSM_GROUPS, e_per, SSM_HEAD_DIM, D_STATE), jnp.float32)
    _, prev = lax.scan(step, init, (jnp.moveaxis(states, 1, 0), jnp.moveaxis(chunk_decay, 1, 0)))
    prev = jnp.moveaxis(prev, 0, 1)
    y_off = jnp.einsum('bclgn,bcgepn,bcgel->bclgep', cc, prev, jnp.exp(a_cs))
    return (y_diag + y_off).reshape(b, s, SSM_HEADS, SSM_HEAD_DIM)

def _dense(key, shape, fan_in):
    return jax.random.normal(key, shape, jnp.float32) * (fan_in ** -0.5)

def second_inputs(seed: int = 0) -> dict:
    key = jax.random.key(seed)
    ks = jax.random.split(key, 24)
    L = DEPTH_2
    ones_noise = lambda k, shape: 1.0 + 0.05 * jax.random.normal(k, shape, jnp.float32)
    dt0 = jnp.exp(jax.random.uniform(ks[5], (L, SSM_HEADS), jnp.float32, np.log(1e-3), np.log(1e-1)))
    return {
        "x": jax.random.normal(ks[0], (BATCH, SEQ, D_MODEL), jnp.float32),
        "p": jax.random.normal(ks[1], (DEPTH_2, BATCH, SEQ, PLE_DIM), jnp.float32),
        "positions": jnp.tile(jnp.arange(SEQ, dtype=jnp.int32)[None], (BATCH, 1)),
        "g_mix": ones_noise(ks[2], (L, D_MODEL)),
        "w_in": _dense(ks[3], (L, D_MODEL, IN_DIM), D_MODEL),
        "conv_w": _dense(ks[4], (L, CONV_WIDTH, CONV_DIM), CONV_WIDTH),
        "conv_b": 0.02 * jax.random.normal(ks[6], (L, CONV_DIM), jnp.float32),
        "dt_bias": dt0 + jnp.log(-jnp.expm1(-dt0)),
        "a_log": jnp.log(jax.random.uniform(ks[7], (L, SSM_HEADS), jnp.float32, 1.0, 16.0)),
        "d_skip": ones_noise(ks[8], (L, SSM_HEADS)),
        "g_ssd": ones_noise(ks[9], (L, D_INNER)),
        "sinks": 0.5 * jax.random.normal(ks[10], (L, ATTN_HEADS), jnp.float32),
        "w_attn_br": _dense(ks[11], (L, Q_DIM, D_MODEL), Q_DIM),
        "w_ssd_br": _dense(ks[12], (L, D_INNER, D_MODEL), D_INNER),
        "w_o": _dense(ks[13], (L, D_MODEL, D_MODEL), D_MODEL),
        "g_ffn": ones_noise(ks[14], (L, D_MODEL)),
        "w_gate": _dense(ks[15], (L, D_MODEL, FFN_HIDDEN), D_MODEL),
        "w_up": _dense(ks[16], (L, D_MODEL, FFN_HIDDEN), D_MODEL),
        "w_down": _dense(ks[17], (L, FFN_HIDDEN, D_MODEL), FFN_HIDDEN),
        "g_ple": ones_noise(ks[18], (L, D_MODEL)),
        "w_ple_gate": _dense(ks[19], (L, D_MODEL, D_MODEL), D_MODEL),
        "w_ple_proj": _dense(ks[20], (L, PLE_DIM, D_MODEL), PLE_DIM),
        "g_final": ones_noise(ks[21], (D_MODEL,)),
    }

def second_block(x, p, positions, g_mix, w_in, conv_w, conv_b, dt_bias, a_log, d_skip, g_ssd,
              sinks, w_attn_br, w_ssd_br, w_o, g_ffn, w_gate, w_up, w_down, g_ple,
              w_ple_gate, w_ple_proj, g_final):
    b, s = x.shape[0], x.shape[1]
    f32 = jnp.float32
    sizes = [Q_DIM, KV_DIM, KV_DIM, D_INNER, CONV_DIM, SSM_HEADS, D_MODEL, D_MODEL]
    offsets = [int(o) for o in np.cumsum(sizes)[:-1]]
    h = x
    for i in range(DEPTH_2):
        u = rmsnorm(h, g_mix[i])
        proj = u @ w_in[i]
        q, k, v, z, xbc, dt_raw, g_a, g_s = jnp.split(proj, offsets, axis=-1)

        q = apply_rope(q.astype(f32).reshape(b, s, ATTN_HEADS, HEAD_DIM), positions)
        k = apply_rope(k.astype(f32).reshape(b, s, KV_HEADS, HEAD_DIM), positions)
        v = v.astype(f32).reshape(b, s, KV_HEADS, HEAD_DIM)
        attn = sliding_window_sink_attention(q, k, v, sinks[i]).astype(x.dtype)
        out_a = attn @ w_attn_br[i]

        xbc = jax.nn.silu(causal_depthwise_conv(xbc, conv_w[i], conv_b[i])).astype(f32)
        xs, bm, cm = jnp.split(xbc, [D_INNER, D_INNER + SSM_GROUPS * D_STATE], axis=-1)
        xh = xs.reshape(b, s, SSM_HEADS, SSM_HEAD_DIM)
        dt = jax.nn.softplus(dt_raw.astype(f32) + dt_bias[i].astype(f32))
        a_neg = -jnp.exp(a_log[i].astype(f32))
        y = ssd_chunked(xh, dt, a_neg,
                        bm.reshape(b, s, SSM_GROUPS, D_STATE),
                        cm.reshape(b, s, SSM_GROUPS, D_STATE))
        y = (y + d_skip[i].astype(f32)[:, None] * xh).reshape(b, s, D_INNER)
        y = rmsnorm(y * jax.nn.silu(z.astype(f32)), g_ssd[i], SSM_NORM_EPS).astype(x.dtype)
        out_s = y @ w_ssd_br[i]

        merged = jax.nn.sigmoid(g_a) * out_a + jax.nn.sigmoid(g_s) * out_s
        h = h + merged @ w_o[i]

        f = rmsnorm(h, g_ffn[i])
        h = h + (jax.nn.silu(f @ w_gate[i]) * (f @ w_up[i])) @ w_down[i]

        gate = jax.nn.sigmoid(rmsnorm(h, g_ple[i]) @ w_ple_gate[i])
        h = h + gate * (p[i] @ w_ple_proj[i])
    return rmsnorm(h, g_final)


def setup_inputs(seed=0):
    out = dict(first_inputs(seed))
    for name, value in second_inputs(seed + 1).items():
        if name != "x":
            out[name + "_2"] = value
    return out


def reference(
    x, norm_g, w_in, diff_lambda, diff_subln_g, rel_bias_table, mla_q_norm_g, w_uq,
    mla_kv_norm_g, w_ukv, w_out, final_norm_g, p_2, positions_2, g_mix_2, w_in_2, conv_w_2,
    conv_b_2, dt_bias_2, a_log_2, d_skip_2, g_ssd_2, sinks_2, w_attn_br_2, w_ssd_br_2, w_o_2,
    g_ffn_2, w_gate_2, w_up_2, w_down_2, g_ple_2, w_ple_gate_2, w_ple_proj_2, g_final_2,
):
    x = first_block(
        x, norm_g, w_in, diff_lambda, diff_subln_g, rel_bias_table, mla_q_norm_g, w_uq,
        mla_kv_norm_g, w_ukv, w_out, final_norm_g,
    )
    return second_block(
        x, p_2, positions_2, g_mix_2, w_in_2, conv_w_2, conv_b_2, dt_bias_2, a_log_2, d_skip_2,
        g_ssd_2, sinks_2, w_attn_br_2, w_ssd_br_2, w_o_2, g_ffn_2, w_gate_2, w_up_2, w_down_2,
        g_ple_2, w_ple_gate_2, w_ple_proj_2, g_final_2,
    )


_drawn_inputs = setup_inputs


def setup_inputs(seed=0):
    import zlib

    import numpy as np

    out = dict(_drawn_inputs(seed))
    spreads = {}
    factors = {'diff_lambda': 2.722,
     'diff_subln_g': 5.648,
     'mla_q_norm_g': 8.0,
     'mla_kv_norm_g': 8.0,
     'conv_b_2': 4.268,
     'd_skip_2': 3.262,
     'sinks_2': 8.0,
     'g_ple_2': 7.36}
    for name, (base, spread) in spreads.items():
        noise = np.random.default_rng([zlib.crc32(name.encode()), seed]).standard_normal(out[name].shape)
        drawn = base * np.exp(spread * noise) if base else spread * noise
        out[name] = __import__('jax').numpy.asarray(drawn.astype(out[name].dtype))
    for name, factor in factors.items():
        out[name] = (out[name] * factor).astype(out[name].dtype)
    return out
```

```python
import math
from contextlib import ExitStack

import concourse.bass as bass
import numpy as np
from concourse import mybir

F32 = mybir.dt.float32
F32R = mybir.dt.float32r
I32 = mybir.dt.int32
ALU = mybir.AluOpType
ACT = mybir.ActivationFunctionType
AX_X = mybir.AxisListType.X

P = 128
S = 256
NT = S // P
D = 2048
DC = D // P
DEPTH = 2
GW = 1024
RING = 4
LOOK = RING
NEG = -1e30

DH, MH = 8, 8
SWA_H, KV_H, HD = 16, 4, 64
SSM_H, SSM_G, SSM_N, SSM_P = 32, 4, 128, 64
TAPS = 4
FFN = 5632
HIDDEN_BLOCKS = FFN // 512
HB1 = 8
HB2 = HIDDEN_BLOCKS - HB1

LAYER_COLS = {}
BLOCK2_COLS = {}
CONST_COLS = {}


def _lay(table, widths):
    at = 0
    for name, w in widths:
        table[name] = (at, w)
        at += w
    return at


LAYER_W = _lay(LAYER_COLS, [("norm", DC), ("q_norm", 4), ("kv_norm", 4), ("lam_init", 1), ("one_minus", 1),
                            ("lambda", 256), ("subln", 128)])
BLOCK2_W = _lay(BLOCK2_COLS, [("mix", DC), ("ffn", DC), ("ple", DC), ("ssd", DC), ("conv_w", 24 * TAPS),
                              ("conv_b", 24), ("dt_bias", SSM_H), ("a_log", SSM_H), ("d_skip", SSM_H),
                              ("sinks", SWA_H), ("inv_freq", 1)])
CONST_W = _lay(CONST_COLS, [("ident", P), ("rot", P), ("tri", P), ("flip", P), ("causal", 384),
                            ("window", 384), ("cos", S), ("sin", S)])


def layer_plan():
    items, g, k, t, s = [], 0, 0, 0, 0

    def product(kind, n, granules, between=None):
        nonlocal g, k
        for i in range(granules):
            items.append(("gran", dict(kind=kind, n=n, i=i, of=granules, g=g, k=k)))
            g += 1
            if between:
                between(g)
        items.append(("evac", dict(kind=kind, n=n, g=g, k=k)))
        k += 1

    def turn(kind, n):
        nonlocal k, t
        items.append(("turn", dict(kind=kind, n=n, k=k, t=t)))
        k += 1
        t += 1

    def stats(kind):
        nonlocal s
        items.append(("stats", dict(kind=kind, s=s)))
        s += 1

    pending = []

    def heads(first, count, spacing, start):
        gap = start
        for h in range(first, first + count + 1):
            if h > first:
                pending.append((gap, ("head_turn", dict(h=h - 1))))
            if h < first + count:
                pending.append((gap, ("head_scores", dict(h=h))))
            if h > first:
                pending.append((gap + 1, ("head_out", dict(h=h - 1))))
            if h < first + count:
                pending.append((gap + 1, ("head_weights", dict(h=h))))
            gap += spacing

    def place(at):
        while pending and pending[0][0] <= at:
            items.append(pending.pop(0)[1])

    stats("x")
    for q in range(4):
        turn("x", q)
    for kind in ("q", "k"):
        for n in range(2):
            product(kind, n, 8)
    product("v", 0, 8)
    heads(0, DH, 3, g + 1)
    product("v", 1, 8, place)
    product("cq", 0, 8, place)
    stats("cq")
    product("ckv", 0, 8, place)
    turn("cq", 0)
    stats("ckv")
    product("kr", 0, 2, place)
    turn("ckv", 0)
    place(10 ** 6)
    items.append(("subln", dict(s=s)))
    s += 1
    for n in range(2):
        product("qn", n, 2)
    product("qr", 0, 2)
    for n in range(2):
        product("kn", n, 2)
    for n in range(2):
        product("vb", n, 2)
    heads(DH, MH, 2, g + 1)
    for n in range(2):
        product("z", n, 8, place)
    product("z", 2, 8, place)
    place(10 ** 6)
    product("z", 3, 8, place)
    for q in range(4):
        turn("o", q)
    for n in range(4):
        product("out", n, 8)
    return items, g, k, t, s


def block2_plan():
    items, g, k, t, s = [], 0, 0, 0, 0

    def product(kind, n, granules, between=None):
        nonlocal g, k
        for i in range(granules):
            items.append(("gran", dict(kind=kind, n=n, i=i, of=granules, g=g, k=k)))
            g += 1
            if between:
                between(g)
        items.append(("evac", dict(kind=kind, n=n, g=g, k=k)))
        k += 1

    def turn(kind, n):
        nonlocal k, t
        items.append(("turn", dict(kind=kind, n=n, k=k, t=t)))
        k += 1
        t += 1

    def back(n):
        nonlocal k
        items.append(("back", dict(n=n, k=k)))
        k += 1

    pending = []

    def place(at):
        while pending and pending[0][0] <= at:
            items.append(pending.pop(0)[1])

    items.append(("stats", dict(kind="u", s=s)))
    s += 1
    for q in range(4):
        turn("u", q)
    for n in range(2):
        product("q", n, 8)
    product("kv", 0, 8)
    gap = g + 5
    for h in range(SWA_H + 1):
        if h:
            pending.append((gap, ("head_turn", dict(h=h - 1))))
        if h < SWA_H:
            pending.append((gap, ("head_scores", dict(h=h))))
        if h:
            pending.append((gap + 1, ("head_out", dict(h=h - 1))))
        if h < SWA_H:
            pending.append((gap + 1, ("head_weights", dict(h=h))))
        gap += 2
    product("xbc", 0, 8, place)
    product("xbc", 1, 8, place)
    back(0)
    for n in range(2, 6):
        product("xbc", n, 8, place)
        if n > 2:
            back(n - 2)
    product("dt", 0, 1, place)
    back(4)
    place(10 ** 6)
    items.append(("decay", {}))
    gap = g + 4
    for grp in range(SSM_G):
        pending.append((gap, ("group_cb", dict(grp=grp))))
        pending.append((gap + 1, ("group_state", dict(grp=grp))))
        pending.append((gap + 2, ("group_off", dict(grp=grp))))
        gap += 3
        for c in range(NT):
            for half in range(2):
                u = (grp * NT + c) * 2 + half
                d = dict(u=u, grp=grp, c=c, h0=grp * 8 + half * 4)
                pending.append((gap, ("unit_rows", d)))
                pending.append((gap + 1, ("unit_mask", d)))
                pending.append((gap + 2, ("unit_out", d)))
                gap += 3
    for n in range(4):
        product("ga", n, 8, place)
    for n in range(4):
        product("gs", n, 8, place)
    place(10 ** 6)
    for n in range(4):
        product("z", n, 8)
    items.append(("stats", dict(kind="y", s=s)))
    s += 1
    for q in range(2):
        turn("attn", q)
    for n in range(4):
        product("attn_br", n, 4)
    for q in range(4):
        turn("y", q)
    for n in range(4):
        product("ssd_br", n, 8)
    for q in range(4):
        turn("merged", q)
    for n in range(4):
        product("w_o", n, 8)
    items.append(("stats", dict(kind="f", s=s)))
    s += 1
    for q in range(4):
        turn("f", q)
    return items, g, k, t, s


def freed(pair, k):
    return (k - pair) // 2 + 1


LAYER_ITEMS, LAYER_G, LAYER_K, LAYER_T, LAYER_S = layer_plan()
LAYER_STEP = {(d["kind"], d["n"]): d["k"] for what, d in LAYER_ITEMS if what in ("evac", "turn")}
B2_ITEMS, B2_G, B2_K, B2_T, B2_S = block2_plan()
B2_STEP = {(d["kind"], d["n"]): DEPTH * LAYER_K + d["k"] for what, d in B2_ITEMS if what in ("evac", "turn")}
BACK0 = DEPTH * LAYER_K + next(d["k"] for what, d in B2_ITEMS if what == "back")
G2 = DEPTH * LAYER_G
K2 = DEPTH * LAYER_K
T2 = DEPTH * LAYER_T
S2 = DEPTH * LAYER_S + 1
DG2 = DEPTH * 3
G_UP1 = G2 + B2_G
G_DN1 = G_UP1 + HB1 * 16
G_UP2 = G_DN1 + 4 * HB1 * 2
G_DN2 = G_UP2 + HB2 * 16
G_PLE = G_DN2 + 4 * HB2 * 2
G_ALL = G_PLE + 4 * 9
K_UP1 = K2 + B2_K
K_DN1 = K_UP1 + HB1 * 2
K_UP2 = K_DN1 + 4
K_DN2 = K_UP2 + HB2 * 2
K_PT = K_DN2 + 4
K_PLE = K_PT + 4
assert LAYER_G % RING == 0 and LAYER_K % 2 == 0
HEADS = DH + MH
GATE, UP = K_UP1 % 2, 1 - K_UP1 % 2
assert K_UP2 % 2 == GATE and K_PLE % 2 == GATE


def build(nc, wstream, x_in, p_in, positions, layer_small, block2_small, const_in, bias_rows, bias_onehot,
          gain_final1, gain_final2, out):
    rev = nc.dram_tensor("bias_by_distance", (DH, 384), F32, kind="Internal")
    spill = nc.dram_tensor("residual_spill", (S, D), F32, kind="Internal").ap()

    place = {"at": (nc.sbuf_base + 31) // 32 * 32}

    def sb(name, shape, dt=F32, at=None):
        size = 4 * int(np.prod(shape[1:]))
        where = place["at"] if at is None else at
        if at is None:
            place["at"] += (size + 31) // 32 * 32
        assert where + size <= 229344, name
        ends[0] = max(ends[0], where + size)
        return nc.alloc_sbuf_tensor_at(name, shape, dt, offset=where)

    ends = [0]

    ctx = ExitStack()
    with ctx:
        def psum(name, cols):
            return ctx.enter_context(nc.psum_tensor(name, [P, cols], F32))

        def sem(name):
            return ctx.enter_context(nc.semaphore(name))

        raw = sb("raw", [P, RING, GW])
        whi = sb("whi", [P, RING, GW], F32R)
        wlo = sb("wlo", [P, RING, GW], F32R)
        x = sb("x", [P, NT, D])
        xh = sb("xh", [P, DC, S], F32R)
        xl = sb("xl", [P, DC, S], F32R)
        const = sb("const", [P, CONST_W])
        cos2 = sb("cos2", [P, S])
        sin2 = sb("sin2", [P, S])
        lsmall = sb("lsmall", [P, DEPTH, LAYER_W])
        lcur = sb("lcur", [P, LAYER_W])
        bsmall = sb("bsmall", [P, BLOCK2_W])
        diag = sb("diag", [P, NT, P])
        act_out = sb("act_out", [P, NT, 512])
        gain = sb("gain", [P, D])
        stat = sb("stat", [P, 64])
        lam = sb("lam", [P, 8])
        subg = sb("subg", [P, P])
        negmax = sb("negmax", [P, 4])
        sums = sb("sums", [P, 4])
        rinv = sb("rinv", [P, 4])
        region = place["at"]

        bias = sb("bias", [P, DH, 256])
        qT = sb("qT", [P, 8, S])
        kT = sb("kT", [P, 8, S])
        v = sb("v", [P, NT, 1024])
        ch = sb("ch", [P, 8, S], F32R)
        cl = sb("cl", [P, 8, S], F32R)
        qr = sb("qr", [P, 4, S])
        kr = sb("kr", [P, S])
        o = sb("o", [P, NT, 2 * 1024])
        c_at = 1024
        unrot = sb("unrot", [P, 1024])
        prob = sb("prob", [P, 2, 384])
        probT = sb("probT", [P, 384])
        junk = sb("junk", [P, 1024])

        place["at"] = region
        xd_at = place["at"]
        xd = sb("xd", [P, NT, D])
        q2 = sb("q2", [P, 8, S], at=xd_at)
        kk2 = sb("kk2", [P, KV_H, S], at=xd_at + 8192)
        k2 = sb("k2", [P, 2, S], at=xd_at + 12288)
        v2 = sb("v2", [P, NT, 256], at=xd_at + 14336)
        ah = sb("ah", [P, 8, S], F32R, at=xd_at)
        al = sb("al", [P, 8, S], F32R, at=xd_at + 8192)
        junk2 = sb("junk2", [P, 1024], at=xd_at)
        bcT = sb("bcT", [P, 8, S])
        bt = sb("bt", [P, 512])
        ys = sb("ys", [P, NT, D])
        ga = sb("ga", [P, NT, D])
        attn = sb("attn", [P, NT, 1024])
        conv_at = place["at"]
        stage = sb("stage", [P, 4, S + TAPS - 1])
        conv = sb("conv", [P, 4, S])
        decay = sb("decay", [P, 2, 512], at=conv_at)
        xw = sb("xw", [P, 512], at=conv_at + 4160)
        state = sb("state", [P, 512], at=conv_at + 6208)
        cbm = sb("cbm", [P, NT, P])
        prob2 = sb("prob2", [P, 384])
        probT2 = sb("probT2", [P, 384])
        dts = sb("dts", [P, 12, 64])

        place["at"] = region
        fh = sb("fh", [P, 4 * HB1, S], F32R)
        fl = sb("fl", [P, 4 * HB1, S], F32R)
        junk3 = sb("junk3", [P, 1024])
        praw = sb("praw", [P, 2, S])
        ph = sb("ph", [P, 2, S], F32R)
        pl = sb("pl", [P, 2, S], F32R)
        pos_i = sb("pos_i", [P, S], I32, at=region + 8192)
        pos_t = sb("pos_t", [P, 3, S], at=region + 9216)

        acc = [psum("acc0", 1024), psum("acc1", 1024)]
        psS = psum("psS", 1024)
        psT = psum("psT", 512)
        psO = psum("psO", 512)

        def cst(name, rows=P):
            at, w = CONST_COLS[name]
            return const[0:rows, at:at + w]

        def lay(name, a=0, b=None):
            at, w = LAYER_COLS[name]
            return lcur[:, at + a:at + (w if b is None else b)]

        def par(name, a=0, b=None):
            at, w = BLOCK2_COLS[name]
            return bsmall[:, at + a:at + (w if b is None else b)]

        ident, rot, tri = cst("ident"), cst("rot"), cst("tri")

        w_loaded = [sem(f"w_loaded{i}") for i in range(RING)]
        hi_ready = sem("hi_ready")
        lo_ready = sem("lo_ready")
        w_used = sem("w_used")
        acc_free = [sem(f"acc_free{i}") for i in range(2)]
        act_read = sem("act_read")
        turned = sem("turned")
        turn_hi = sem("turn_hi")
        ms_ready = sem("ms_ready")
        root_ready = sem("root_ready")
        diag_ready = sem("diag_ready")
        rot_in = sem("rot_in")
        rot_done = sem("rot_done")
        rot_read = sem("rot_read")
        scores_ready = sem("scores_ready")
        negmax_ready = sem("negmax_ready")
        exp_ready = sem("exp_ready")
        weights_ready = sem("weights_ready")
        probT_in_psum = sem("probT_in_psum")
        probT_ready = sem("probT_ready")
        pv_ready = sem("pv_ready")
        head_read = sem("head_read")
        small_loaded = sem("small_loaded")
        x_loaded = sem("x_loaded")
        bias_loaded = sem("bias_loaded")
        bias_ps = sem("bias_ps")
        bias_sb = sem("bias_sb")
        bias_out = sem("bias_out")
        bias_in = sem("bias_in")
        bias_flip = sem("bias_flip")
        bias_done = sem("bias_done")
        pos_loaded = sem("pos_loaded")
        angle_ready = sem("angle_ready")
        table_ready = sem("table_ready")
        lam_in = sem("lam_in")
        lam_exp = sem("lam_exp")
        layer_small_ready = sem("layer_small_ready")
        final1_ready = sem("final1_ready")
        spilled = sem("spilled")
        refetched = sem("refetched")
        gain2_loaded = sem("gain2_loaded")
        k_spread = sem("k_spread")
        conv_sum = sem("conv_sum")
        conv_done = sem("conv_done")
        back_ready = sem("back_ready")
        dt_step = sem("dt_step")
        dt_act = sem("dt_act")
        acs_ready = sem("acs_ready")
        decay_in = sem("decay_in")
        decay_ready = sem("decay_ready")
        cb_ready = sem("cb_ready")
        xw_ready = sem("xw_ready")
        cb_read = sem("cb_read")
        state_ps = sem("state_ps")
        state_ready = sem("state_ready")
        off_ready = sem("off_ready")
        off_read = sem("off_read")
        rows_ready = sem("rows_ready")
        diff_ready = sem("diff_ready")
        unit_exp = sem("unit_exp")
        unit_ready = sem("unit_ready")
        diag_out = sem("diag_out")
        diag_read = sem("diag_read")
        merged_free = sem("merged_free")
        p_loaded = sem("p_loaded")
        p_hi = sem("p_hi")
        p_lo = sem("p_lo")
        result_ready = sem("result_ready")
        stored = sem("stored")

        block = ctx.enter_context(nc.Block())

        def moved(eng, k, more=0):
            eng.wait_ge(acc_free[k % 2], more + (k // 2 + 1))

        def wait(eng, signal, value):
            if not (isinstance(value, int) and value <= 0):
                eng.wait_ge(signal, value)

        @block.sync
        def _(sp):
            sp.dma_start(x[:, :, :], x_in.rearrange("(t p) d -> p t d", p=P)).then_inc(x_loaded, 16)
            sp.dma_start(const[:, :], const_in).then_inc(small_loaded, 16)
            sp.dma_start(lsmall[:, :, :], layer_small.rearrange("l p w -> p l w")).then_inc(small_loaded, 16)
            sp.dma_start(bsmall[:, :], block2_small).then_inc(small_loaded, 16)
            sp.dma_start(bias[0:33, 0, 0:DH], bias_rows).then_inc(bias_loaded, 16)
            sp.dma_start(bias[0:33, 2:4, :].rearrange("p a b -> p (a b)")[:, 0:384], bias_onehot).then_inc(bias_loaded, 16)
            sp.dma_start(gain[:, :], gain_final1).then_inc(small_loaded, 16)
            sp.dma_start(pos_i[:, :], positions.partition_broadcast(P)).then_inc(pos_loaded, 16)

            for g in range(RING):
                sp.dma_start(raw[:, g, :], wstream[g, :, :]).then_inc(w_loaded[g], 16)
            with sp.Fori(1, G_ALL // RING) as i:
                for j in range(RING):
                    sp.wait_ge(lo_ready, RING * i + (j + 1 - RING))
                    sp.dma_start(raw[:, j, :], wstream[bass.ds(RING * i + j, 1), :, :]
                                 .rearrange("a p n -> p (a n)")).then_inc(w_loaded[j], 16)
            for g in range(G_ALL // RING * RING, G_ALL):
                sp.wait_ge(lo_ready, g + 1 - RING)
                sp.dma_start(raw[:, g % RING, :], wstream[g, :, :]).then_inc(w_loaded[g % RING], 16)
            sp.wait_ge(result_ready, NT)
            sp.dma_start(out.rearrange("(t p) d -> p t d", p=P), x[:, :, :]).then_inc(stored, 16)
            sp.wait_ge(stored, 16)

        @block.gpsimd
        def _(pool):
            def rest(g, j, first):
                pool.wait_ge(hi_ready, g + 1)
                if not first:
                    pool.wait_ge(w_used, g + 1 - RING)
                pool.tensor_tensor(wlo[:, j, :], raw[:, j, :], whi[:, j, :].bitcast(F32),
                                   ALU.subtract).then_inc(lo_ready, 1)

            for g in range(RING):
                rest(g, g, True)
            with pool.Fori(1, G_ALL // RING) as i:
                for j in range(RING):
                    rest(RING * i + j, j, False)
            for g in range(G_ALL // RING * RING, G_ALL):
                rest(g, g % RING, False)

        def turn_of(kind, n):
            if kind == "x":
                return x, 4 * n, xh, xl, 4 * n, (lay, "norm", 4 * n)
            if kind == "cq":
                return o, c_at // P, ch, cl, 0, (lay, "q_norm", 0)
            if kind == "ckv":
                return o, c_at // P + 4, ch, cl, 4, (lay, "kv_norm", 0)
            if kind == "o":
                return o, 4 * n, xh, xl, 4 * n, None
            if kind == "u":
                return x, 4 * n, xh, xl, 4 * n, (par, "mix", 4 * n)
            if kind == "attn":
                return attn, 4 * n, ah, al, 4 * n, None
            if kind == "y":
                return ys, 4 * n, xh, xl, 4 * n, (par, "ssd", 4 * n)
            if kind == "merged":
                return ga, 4 * n, xh, xl, 4 * n, None
            if kind == "f":
                return x, 4 * n, xh, xl, 4 * n, (par, "ffn", 4 * n)
            if kind == "ple":
                return x, 4 * n, xh, xl, 4 * n, (par, "ple", 4 * n)
            raise ValueError(kind)

        @block.tensor
        def _(pe):
            def claim(k):
                wait(pe, acc_free[k_slot(k)], k_use(k))

            def granule(g, slot, out_ps, form, ah_, al_, chunk0, chunks, first, last_one, width=512):
                pe.wait_ge(lo_ready, g + 1)
                per = GW // chunks
                wh = whi[:, slot, :].rearrange("p (c n) -> p c n", c=chunks)
                wl = wlo[:, slot, :].rearrange("p (c n) -> p c n", c=chunks)
                m = None
                for c in range(chunks):
                    begin = first and c == 0
                    end = last_one and c == chunks - 1
                    kc = chunk0 + c
                    if form in ("B", "KV", "KR"):
                        for j in range({"B": 4, "KV": 2, "KR": 1}[form]):
                            dst = out_ps[:, 256 * j:256 * j + 256]
                            js = slice(128 * j, 128 * j + 128)
                            pe.matmul(dst, wh[:, c, js], ah_[:, kc, :], start=begin and j % 2 == 0, stop=False,
                                      skip_group_check=True)
                            pe.matmul(dst, wh[:, c, js], al_[:, kc, :], start=False, stop=False,
                                      skip_group_check=True)
                            m = pe.matmul(dst, wl[:, c, js], ah_[:, kc, :], start=False, stop=end,
                                          skip_group_check=True)
                    if form in ("A", "KV"):
                        for t in range(NT):
                            lo, step = (0, 512) if form == "A" else (512, 256)
                            dst = out_ps[:, lo + step * t:lo + step * t + width]
                            cols = slice(0, width) if form == "A" else slice(256, 512)
                            ts = slice(P * t, P * t + P)
                            shared = form == "KV"
                            pe.matmul(dst, ah_[:, kc, ts], wh[:, c, cols], start=begin and not (shared and t),
                                      stop=False, skip_group_check=shared)
                            pe.matmul(dst, ah_[:, kc, ts], wl[:, c, cols], start=False, stop=False,
                                      skip_group_check=shared)
                            m = pe.matmul(dst, al_[:, kc, ts], wh[:, c, cols], start=False, stop=end,
                                          skip_group_check=shared)
                m.then_inc(w_used, 1)

            def turn(kind, n, k):
                src, c0, _, _, _, g = turn_of(kind, n)
                claim(k)
                for j in range(4):
                    for t in range(NT):
                        a = src[:, t, (c0 + j) * P:(c0 + j + 1) * P]
                        dst = acc[k % 2][:, 256 * j + P * t:256 * j + P * t + P]
                        if g is None:
                            m = pe.transpose(dst, a, ident)
                        else:
                            m = pe.matmul(dst, a, diag[:, t, :], start=True, stop=True)
                m.then_inc(turned, 1)

            FORMS = dict(q="B", k="B", v="A", cq="A", ckv="A", kr="KR", qn="B", qr="B", kn="B", vb="A",
                         z="A", out="A", kv="KV", xbc="B", dt="A", ga="A", gs="A", attn_br="A", ssd_br="A", w_o="A")

            def scores(hh, tiles, depth):
                wait(pe, negmax_ready, hh)
                for n, parts in enumerate(tiles):
                    base = 512 * n
                    for part, (qa, ka) in enumerate(parts):
                        one = dict(start=part == 0, stop=part == len(parts) - 1)
                        m = pe.matmul(psS[:, base:base + 256], qa[:, P:S], ka[:, 0:S], **one)
                    for part, (qa, ka) in enumerate(parts):
                        one = dict(start=part == 0, stop=part == len(parts) - 1)
                        m = pe.matmul(psS[:, base + 256:base + 384], qa[:, 0:P], ka[:, 0:P], **one)
                m.then_inc(scores_ready, 1)

            def head_turn(hh, src, weights_signal, weights_value):
                pe.wait_ge(weights_signal, weights_value)
                for j in range(3):
                    m = pe.transpose(psT[:, P * j:P * j + P], src[:, P * j:P * j + P], ident)
                m.then_inc(probT_in_psum, 1)

            def head_out(hh, pt, vv, w):
                pe.wait_ge(probT_ready, hh + 1)
                wait(pe, head_read, hh)
                pe.matmul(psO[:, w:2 * w], pt[:, 0:P], vv(0), start=True, stop=False)
                pe.matmul(psO[:, w:2 * w], pt[:, P:2 * P], vv(1), start=False, stop=True)
                m = pe.matmul(psO[:, 0:w], pt[:, 2 * P:3 * P], vv(0), start=True, stop=True)
                m.then_inc(pv_ready, 1)

            pe.wait_ge(bias_loaded, 32)
            pe.wait_ge(small_loaded, 64)
            pe.matmul(psT[0:DH, 0:384], bias[0:33, 0, 0:DH],
                      bias[0:33, 2:4, :].rearrange("p a b -> p (a b)")[:, 0:384], start=True, stop=True)\
                .then_inc(bias_ps, 1)
            pe.wait_ge(bias_in, 16)
            for j in range(4):
                if j >= 2:
                    pe.wait_ge(bias_done, j - 1)
                pe.matmul(psS[:, 512 * (j % 2):512 * (j % 2) + 512], cst("flip"), o[:, 0, 512 * j:512 * j + 512],
                          start=True, stop=True).then_inc(bias_flip, 1)

            def in_sbuf(l, step):
                for b in range(2):
                    pe.wait_ge(acc_free[b], l * (LAYER_K // 2) + freed(b, LAYER_STEP[step]))

            with pe.Fori(0, DEPTH) as l:
                k_slot = lambda k: k % 2
                k_use = lambda k: l * (LAYER_K // 2) + k // 2
                for what, d in LAYER_ITEMS:
                    if what == "gran":
                        kind, n, i = d["kind"], d["n"], d["i"]
                        if i == 0:
                            claim(d["k"])
                            need = {"q": ("x", 3), "qn": ("cq", 0), "kn": ("ckv", 0), "out": ("o", 3)}.get(kind)
                            if need and n == 0:
                                in_sbuf(l, need)
                        a, b, c0 = xh, xl, 2 * i
                        chunks = 8 if kind == "kr" else 2
                        if kind == "kr":
                            c0 = 8 * i
                        if kind in ("qn", "qr"):
                            a, b = ch, cl
                        if kind in ("kn", "vb"):
                            a, b, c0 = ch, cl, 4 + 2 * i
                        granule(l * LAYER_G + d["g"], d["g"] % RING, acc[d["k"] % 2], FORMS[kind], a, b, c0,
                                chunks, i == 0, i == d["of"] - 1)
                    elif what == "turn":
                        kind, n = d["kind"], d["n"]
                        if n == 0:
                            if kind in ("x", "cq", "ckv"):
                                pe.wait_ge(diag_ready, l * 3 + {"x": 1, "cq": 2, "ckv": 3}[kind])
                            else:
                                pe.wait_ge(act_read, l * 4 + 4)
                        turn(kind, n, d["k"])
                    elif what == "evac" and d["kind"] in ("kr", "qr"):
                        r = 0 if d["kind"] == "kr" else 1
                        pe.wait_ge(rot_in, l * 2 + r + 1)
                        halves = 1 if r == 0 else 4
                        for j in range(halves):
                            m = pe.matmul(acc[d["k"] % 2][:, 256 * j:256 * j + 256], rot,
                                          unrot[:, 256 * j:256 * j + 256], start=True, stop=True)
                        m.then_inc(rot_done, 1)
                    elif what == "head_scores":
                        h = d["h"]
                        if h < DH:
                            if h == 0:
                                in_sbuf(l, ("k", 1))
                            scores(l * HEADS + h, [[(qT[64 * m:64 * m + 64, h, :], kT[64 * m:64 * m + 64, h, :])]
                                                   for m in range(2)], 64)
                        else:
                            e = h - DH
                            if e == 0:
                                in_sbuf(l, ("vb", 1))
                            half = slice(64 * (e % 2), 64 * (e % 2) + 64)
                            scores(l * HEADS + h, [[(qT[:, e, :], kT[:, e, :]), (qr[half, e // 2, :], kr[half, :])]], 0)
                    elif what == "head_turn":
                        h = d["h"]
                        if h < DH:
                            head_turn(l * HEADS + h, prob[:, 0, :], weights_ready, l * DH + h + 1)
                        else:
                            head_turn(l * HEADS + h, prob[:, 0, :], exp_ready, l * HEADS + h + 1)
                    elif what == "head_out":
                        h = d["h"]
                        e = h % DH
                        if h in (0, 4):
                            in_sbuf(l, ("v", h // 4))
                        head_out(l * HEADS + h, probT, lambda c, e=e: v[:, c, e * P:e * P + P], P)

            def both_moved(k):
                for b in range(2):
                    pe.wait_ge(acc_free[b], freed(b, k))

            k_slot = lambda k: (K2 + k) % 2
            k_use = lambda k: (K2 + k) // 2
            HB = DEPTH * HEADS
            for what, d in B2_ITEMS:
                if what == "gran":
                    kind, n, i = d["kind"], d["n"], d["i"]
                    if i == 0:
                        claim(d["k"])
                        need = {"q": ("u", 3), "attn_br": ("attn", 1), "ssd_br": ("y", 3), "w_o": ("merged", 3)}.get(kind)
                        if need and n == 0:
                            both_moved(B2_STEP[need])
                    a, b = (ah, al) if kind == "attn_br" else (xh, xl)
                    chunks = 16 if kind == "dt" else 2
                    granule(G2 + d["g"], (G2 + d["g"]) % RING, acc[d["k"] % 2], FORMS[kind], a, b, 2 * i,
                            chunks, i == 0, i == d["of"] - 1, width={"dt": SSM_H, "kv": 256}.get(kind, 512))
                elif what == "turn":
                    kind, n = d["kind"], d["n"]
                    if n == 0:
                        if kind in ("u", "y", "f", "attn"):
                            pe.wait_ge(diag_ready, DG2 + {"u": 1, "attn": 2, "y": 2, "f": 3}[kind])
                        if kind == "merged":
                            for b in range(2):
                                pe.wait_ge(acc_free[b], freed(b, K2 + d["k"] - 1))
                    turn(kind, n, d["k"])
                elif what == "evac" and d["kind"] in ("q", "kv"):
                    r = DEPTH * 2 + (d["n"] if d["kind"] == "q" else 2)
                    pe.wait_ge(rot_in, r + 1)
                    for j in range(4 if d["kind"] == "q" else 2):
                        m = pe.matmul(acc[d["k"] % 2][:, 256 * j:256 * j + 256], rot,
                                      attn[:, 0, 256 * j:256 * j + 256], start=True, stop=True)
                    m.then_inc(rot_done, 1)
                elif what == "back":
                    n = d["n"]
                    claim(d["k"])
                    pe.wait_ge(conv_done, 1 if n == 0 else n + 2)
                    for c in range(1 if n == 0 else NT):
                        for j in range(4):
                            src = bcT[:, j, 0:P] if n == 0 else conv[:, j, P * c:P * c + P]
                            m = pe.transpose(acc[d["k"] % 2][:, 512 * c + P * j:512 * c + P * j + P], src, ident)
                    m.then_inc(back_ready, 1)
                elif what == "head_scores":
                    h = d["h"]
                    if h == 0:
                        pe.wait_ge(k_spread, 16 * KV_H * 2)
                    half = slice(64 * (h % 2), 64 * (h % 2) + 64)
                    scores(HB + h, [[(q2[half, h // 2, :], kk2[half, h // (SWA_H // KV_H), :])]], 64)
                elif what == "head_turn":
                    head_turn(HB + d["h"], prob2[:, :], exp_ready, HB + d["h"] + 1)
                elif what == "head_out":
                    h = d["h"]
                    kvh = h // (SWA_H // KV_H)
                    head_out(HB + h, probT2, lambda c, e=kvh: v2[:, c, e * HD:e * HD + HD], HD)
                elif what == "decay":
                    pe.wait_ge(dt_step, 3)
                    wait(pe, head_read, HB + SWA_H)
                    pe.matmul(psO[:, 0:64], tri, dts[:, 6, :], start=True, stop=True)
                    pe.matmul(psO[:, 64:128], tri[:, P - 1:P].to_broadcast([P, P]), dts[:, 6, :], start=True,
                              stop=True).then_inc(acs_ready, 1)
                elif what == "group_cb":
                    grp = d["grp"]
                    if grp == 0:
                        wait(pe, negmax_ready, HB + SWA_H)
                        pe.wait_ge(conv_done, 6)
                    wait(pe, cb_read, grp)
                    for c in range(NT):
                        m = pe.matmul(psS[:, P * c:P * c + P], bcT[:, grp, P * c:P * c + P],
                                      bcT[:, 4 + grp, P * c:P * c + P], start=True, stop=True)
                    m.then_inc(cb_ready, 1)
                elif what == "group_state":
                    grp = d["grp"]
                    pe.wait_ge(xw_ready, grp + 1)
                    if grp == 0:
                        moved(pe, BACK0)
                    wait(pe, off_read, grp)
                    pe.matmul(psS[:, 512:1024], bt[:, P * grp:P * grp + P], xw[:, :], start=True, stop=True)\
                        .then_inc(state_ps, 1)
                elif what == "group_off":
                    grp = d["grp"]
                    pe.wait_ge(state_ready, grp + 1)
                    pe.matmul(psS[:, 512:1024], bcT[:, 4 + grp, P:S], state[:, :], start=True, stop=True)\
                        .then_inc(off_ready, 1)
                elif what == "unit_rows":
                    u, c, h0 = d["u"], d["c"], d["h0"]
                    if u == 0:
                        wait(pe, probT_ready, HB + SWA_H)
                    wait(pe, diff_ready, u)
                    for j in range(4):
                        a = dts[:, 6, 32 * c + h0 + j:32 * c + h0 + j + 1].to_broadcast([P, P])
                        m = pe.matmul(psT[:, P * j:P * j + P], a, tri, start=True, stop=True)
                    m.then_inc(rows_ready, 1)
                elif what == "unit_out":
                    u, c, h0 = d["u"], d["c"], d["h0"]
                    pe.wait_ge(unit_ready, u + 1)
                    wait(pe, diag_read, u)
                    if u == 0:
                        pe.wait_ge(decay_in, 1)
                    for j in range(4):
                        m = pe.matmul(psO[:, 64 * j:64 * j + 64], decay[:, u % 2, P * j:P * j + P],
                                      xd[:, c, 64 * (h0 + j):64 * (h0 + j) + 64], start=True, stop=True)
                    m.then_inc(diag_out, 1)

            for part, (g_up, k_up, hbs, g_dn, k_dn) in enumerate(
                    [(G_UP1, K_UP1, HB1, G_DN1, K_DN1), (G_UP2, K_UP2, HB2, G_DN2, K_DN2)]):
                if part == 0:
                    both_moved(K_UP1 - 1)
                with pe.Fori(0, hbs) as i:
                    for side in range(2):
                        k = k_up + side
                        pe.wait_ge(acc_free[k % 2], k // 2 + i)
                        for j in range(8):
                            granule(g_up + 16 * i + 8 * side + j, (g_up + 8 * side + j) % RING, acc[k % 2], "B",
                                    xh, xl, 2 * j, 2, j == 0, j == 7)
                pe.wait_ge(act_read, DEPTH * 4 + 4 + (HB1 if part == 0 else HIDDEN_BLOCKS))
                per = 2 * hbs
                with pe.Fori(0, 2) as i:
                    for side in range(2):
                        k = k_dn + side
                        pe.wait_ge(acc_free[k % 2], k // 2 + i)
                        for j in range(per):
                            granule(g_dn + 2 * per * i + per * side + j, (g_dn + per * side + j) % RING, acc[k % 2],
                                    "A", fh, fl, 2 * j, 2, j == 0, j == per - 1)
            pe.wait_ge(diag_ready, DG2 + B2_S + 1)
            k_slot = lambda k: k % 2
            k_use = lambda k: k // 2
            for n in range(4):
                turn("ple", n, K_PT + n)
            both_moved(K_PLE - 1)
            pe.wait_ge(p_lo, 1)
            for n in range(4):
                for side in range(2):
                    claim(K_PLE + 2 * n + side)
                    g = G_PLE + 9 * n + 8 * side
                    for j in range(8 if side == 0 else 1):
                        granule(g + j, (g + j) % RING, acc[(GATE + side) % 2], "A", *((xh, xl) if side == 0 else (ph, pl)),
                                2 * j, 2, j == 0, j == (7 if side == 0 else 0))

        @block.scalar
        def _(act):
            def upper(g, slot, first=False):
                act.wait_ge(w_loaded[slot], 16 * (g // RING + 1))
                if not first:
                    act.wait_ge(w_used, g + 1 - RING)
                act.activation(whi[:, slot, :], raw[:, slot, :], ACT.Copy).then_inc(hi_ready, 1)

            def ahead(g_static, g=None):
                if g is None:
                    g = g_static
                if isinstance(g, int) and g + LOOK >= G_ALL:
                    return
                upper(g + LOOK, g_static % RING)

            def turn_round(kind, n, k, t_value):
                src, c0, dh, dl, dc, g = turn_of(kind, n)
                act.wait_ge(turned, t_value + 1)
                for j in range(4):
                    a = acc[k % 2][:, 256 * j:256 * j + 256]
                    if g is None:
                        m = act.activation(dh[:, dc + j, :], a, ACT.Copy)
                    else:
                        m = act.activation(dh[:, dc + j, :], a, ACT.Copy, scale=g[0](g[1], g[2] + j, g[2] + j + 1))
                m.then_inc(turn_hi, 1)

            def root(s_value):
                act.wait_ge(ms_ready, s_value + 1)
                act.activation(stat[:, 32:48], stat[:, 16:32], ACT.Sqrt).then_inc(root_ready, 1)

            def exps(hh, pr, maps, scale=1.0):
                act.wait_ge(negmax_ready, hh + 1)
                for m in range(maps):
                    act.activation(pr(m)[:, 0:256], pr(m)[:, 0:256], ACT.Exp, bias=negmax[:, m:m + 1],
                                   accum_out=sums[:, m:m + 1])
                    z = act.activation(pr(m)[:, 256:384], pr(m)[:, 256:384], ACT.Exp, bias=negmax[:, 2 + m:3 + m],
                                       accum_out=sums[:, 2 + m:3 + m])
                return z

            def copy_probT(hh, pt):
                act.wait_ge(probT_in_psum, hh + 1)
                act.activation(pt[:, :], psT[:, 0:384], ACT.Copy).then_inc(probT_ready, 1)

            def silu_out(k, g_value, func, uses):
                act.wait_ge(w_used, g_value)
                wait(act, act_read, uses)
                act.activation(act_out[:, :, :], acc[k % 2][:, :].rearrange("p (t n) -> p t n", t=NT), func)\
                    .then_inc(acc_free[k % 2], 1)

            for g in range(RING):
                upper(g, g, first=True)
            act.wait_ge(angle_ready, 1)
            act.activation(sin2[:, :], pos_t[:, 1, :], ACT.Sin)
            act.activation(cos2[:, :], pos_t[:, 2, :], ACT.Sin).then_inc(table_ready, 1)
            act.wait_ge(bias_sb, 1)
            act.dma_start(rev.ap(), o[0:DH, 1, 0:384]).then_inc(bias_out, 16)
            act.wait_ge(bias_out, 16)
            act.dma_start(o[:, 0, :].rearrange("p (h n) -> p h n", h=DH),
                          bass.AP(rev, 0, [[1, P], [384, DH], [1, 256]])).then_inc(bias_in, 16)

            with act.Fori(0, DEPTH) as l:
                base = l * LAYER_G
                for what, d in LAYER_ITEMS:
                    if what == "gran":
                        g = d["g"]
                        act.wait_ge(w_loaded[g % RING], 16 * (l * (LAYER_G // RING) + (g + LOOK) // RING + 1))
                        act.wait_ge(w_used, base + (g + 1))
                        act.activation(whi[:, g % RING, :], raw[:, g % RING, :], ACT.Copy).then_inc(hi_ready, 1)
                    elif what == "turn":
                        turn_round(d["kind"], d["n"], d["k"], l * LAYER_T + d["t"])
                    elif what in ("stats", "subln"):
                        root(l * LAYER_S + d["s"])
                        if d.get("kind") == "x":
                            act.wait_ge(lam_in, l + 1)
                            act.activation(lam[:, 2:4], lam[:, 0:2], ACT.Exp).then_inc(lam_exp, 1)
                    elif what == "head_scores":
                        h = d["h"]
                        exps(l * HEADS + h, lambda m: prob[:, m, :], 2 if h < DH else 1).then_inc(exp_ready, 1)
                    elif what == "head_turn":
                        copy_probT(l * HEADS + d["h"], probT)
                    elif what == "evac" and d["kind"] == "z":
                        silu_out(d["k"], base + d["g"], ACT.Silu, l * 4 + d["n"])

            HB = DEPTH * HEADS
            root(DEPTH * LAYER_S)
            act.wait_ge(final1_ready, 1)
            act.dma_start(gain[:, :], gain_final2).then_inc(gain2_loaded, 16)
            act.dma_start(spill.rearrange("(t p) d -> p t d", p=P), x[:, :, :]).then_inc(spilled, 16)
            uses = DEPTH * 4
            for what, d in B2_ITEMS:
                if what == "gran":
                    ahead(G2 + d["g"])
                elif what == "turn":
                    turn_round(d["kind"], d["n"], d["k"], T2 + d["t"])
                elif what == "stats":
                    root(S2 + d["s"])
                elif what == "head_scores":
                    h = d["h"]
                    exps(HB + h, lambda m: prob2[:, :], 1)
                    act.activation(sums[:, 3:4], par("sinks", h, h + 1), ACT.Exp, bias=negmax[:, 2:3])
                    act.activation(sums[:, 1:2], par("sinks", h, h + 1), ACT.Exp, bias=negmax[:, 0:1])\
                        .then_inc(exp_ready, 1)
                elif what == "head_turn":
                    copy_probT(HB + d["h"], probT2)
                elif what == "evac" and d["kind"] == "kv":
                    moved(act, K2 + d["k"])
                    for i in range(KV_H):
                        for half in range(2):
                            act.dma_start(kk2[64 * half:64 * half + 64, i, :],
                                          k2[64 * (i % 2):64 * (i % 2) + 64, i // 2, :]).then_inc(k_spread, 16)
                elif what == "evac" and d["kind"] == "xbc":
                    n = d["n"]
                    act.wait_ge(w_used, G2 + d["g"])
                    wait(act, conv_sum, n)
                    act.activation(stage[:, :, TAPS - 1:], acc[d["k"] % 2][:, :].rearrange("p (j s) -> p j s", j=4),
                                   ACT.Copy).then_inc(acc_free[d["k"] % 2], 1)
                    act.wait_ge(conv_sum, n + 1)
                    dst = bcT[:, 4 * n:4 * n + 4, :] if n < 2 else conv[:, :, :]
                    act.activation(dst, conv[:, :, :], ACT.Silu).then_inc(conv_done, 1)
                elif what == "evac" and d["kind"] in ("ga", "gs"):
                    act.wait_ge(w_used, G2 + d["g"])
                    if d["kind"] == "gs" and d["n"] == 0:
                        act.wait_ge(spilled, 16)
                    dst = (ga if d["kind"] == "ga" else x)[:, :, 512 * d["n"]:512 * d["n"] + 512]
                    act.activation(dst, acc[d["k"] % 2][:, :].rearrange("p (t n) -> p t n", t=NT), ACT.Sigmoid)\
                        .then_inc(acc_free[d["k"] % 2], 1)
                elif what == "evac" and d["kind"] == "z":
                    silu_out(d["k"], G2 + d["g"], ACT.Silu, uses)
                    uses += 1
                elif what == "evac" and d["kind"] == "dt":
                    act.wait_ge(dt_step, 1)
                    act.activation(dts[:, 8, 0:SSM_H], par("a_log"), ACT.Exp)
                    act.activation(dts[:, 2, :], dts[:, 1, :], ACT.Exp).then_inc(dt_act, 1)
                    act.wait_ge(dt_step, 2)
                    act.activation(dts[:, 4, :], dts[:, 3, :], ACT.Ln).then_inc(dt_act, 1)
                elif what == "decay":
                    act.wait_ge(decay_in, 1)
                    act.activation(dts[:, 9, :], dts[:, 10, :], ACT.Exp).then_inc(decay_ready, 1)
                elif what == "group_state":
                    grp = d["grp"]
                    act.wait_ge(state_ps, grp + 1)
                    act.activation(state[:, :], psS[:, 512:1024], ACT.Copy).then_inc(state_ready, 1)
                elif what == "unit_rows":
                    u = d["u"]
                    act.wait_ge(diff_ready, u + 1)
                    act.activation(decay[:, u % 2, :], decay[:, u % 2, :], ACT.Exp).then_inc(unit_exp, 1)
                elif what == "evac" and d["kind"] == "ssd_br" and d["n"] == 3:
                    act.wait_ge(merged_free, 1)
                    act.dma_start(x[:, :, :], spill.rearrange("(t p) d -> p t d", p=P)).then_inc(refetched, 16)
            assert uses == DEPTH * 4 + 4
            for k in (K_UP1 - 2, K_UP1 - 1):
                moved(act, k)
            act.dma_start(praw[:, :, :], p_in).then_inc(p_loaded, 16)
            act.wait_ge(p_loaded, 16)
            act.activation(ph[:, :, :], praw[:, :, :], ACT.Copy).then_inc(p_hi, 1)

            for part, (g_up, k_up, hbs, g_dn, k_dn) in enumerate(
                    [(G_UP1, K_UP1, HB1, G_DN1, K_DN1), (G_UP2, K_UP2, HB2, G_DN2, K_DN2)]):
                def stream(g_static, i, stride, many):
                    for j in range(many):
                        g = g_static + j
                        act.wait_ge(w_loaded[g % RING], 16 * (stride // RING * i + (g + LOOK) // RING + 1))
                        act.wait_ge(w_used, stride * i + (g + 1))
                        act.activation(whi[:, g % RING, :], raw[:, g % RING, :], ACT.Copy).then_inc(hi_ready, 1)

                done = 0 if part == 0 else HB1
                with act.Fori(0, hbs) as i:
                    stream(g_up, i, 16, 8)
                    act.wait_ge(w_used, 16 * i + (g_up + 8))
                    act.wait_ge(act_read, i + (uses + done))
                    act.activation(act_out[:, :, :].rearrange("p t n -> p (t n)"), acc[GATE][:, :], ACT.Silu)\
                        .then_inc(acc_free[GATE], 1)
                    stream(g_up + 8, i, 16, 8)
                    moved(act, k_up + 1, i)
                    act.activation(fh[:, bass.ds(4 * i, 4), :].rearrange("p c s -> p (c s)"),
                                   act_out[:, :, :].rearrange("p t n -> p (t n)"), ACT.Copy).then_inc(turn_hi, 1)
                per = 2 * hbs
                with act.Fori(0, 2) as i:
                    stream(g_dn, i, 2 * per, 2 * per)
            root(S2 + B2_S)
            for n in range(4):
                turn_round("ple", n, K_PT + n, T2 + B2_T + n)
            uses2 = uses + HIDDEN_BLOCKS
            for n in range(4):
                for j in range(8):
                    ahead(G_PLE + 9 * n + j)
                silu_out(K_PLE + 2 * n, G_PLE + 9 * n + 8, ACT.Sigmoid, uses2 + n)
                ahead(G_PLE + 9 * n + 8)
            root(S2 + B2_S + 1)

        @block.vector
        def _(dve):
            def sync():
                dve.drain()

            def mean_squares(parts, width, eps, s_value):
                n = len(parts(0))
                for t in range(NT):
                    for i, a in enumerate(parts(t)):
                        w = a.shape[-1]
                        dve.tensor_tensor_reduce(out=jk[:, 0:w], in0=a, in1=a, scale=1.0, scalar=0.0, op0=ALU.mult,
                                                 op1=ALU.add, accum_out=stat[:, NT * i + t:NT * i + t + 1])
                        sync()
                if n == 2:
                    dve.tensor_tensor(stat[:, 0:NT], stat[:, 0:NT], stat[:, NT:2 * NT], ALU.add)
                    sync()
                dve.tensor_scalar(stat[:, 16:16 + NT], stat[:, 0:NT], 1.0 / width, eps, ALU.mult, ALU.add)\
                    .then_inc(ms_ready, 1)
                dve.wait_ge(root_ready, s_value + 1)
                dve.reciprocal(stat[:, 48:48 + NT], stat[:, 32:32 + NT])
                sync()

            def make_diag():
                for t in range(NT):
                    m = dve.tensor_scalar(diag[:, t, :], ident, stat[:, 48 + t:49 + t], None, ALU.mult)
                m.then_inc(diag_ready, 1)

            def turn_rest(kind, n, k, t_value):
                src, c0, dh, dl, dc, g = turn_of(kind, n)
                dve.wait_ge(turn_hi, t_value + 1)
                if g is None:
                    m = dve.tensor_tensor(dl[:, dc:dc + 4, :].rearrange("p c s -> p (c s)"), acc[k % 2][:, :],
                                          dh[:, dc:dc + 4, :].rearrange("p c s -> p (c s)").bitcast(F32), ALU.subtract)
                else:
                    for j in range(4):
                        m = dve.scalar_tensor_tensor(dl[:, dc + j, :], acc[k % 2][:, 256 * j:256 * j + 256],
                                                     g[0](g[1], g[2] + j, g[2] + j + 1), dh[:, dc + j, :].bitcast(F32),
                                                     ALU.mult, ALU.subtract)
                m.then_inc(acc_free[k % 2], 1)

            def rotate(dst, cos, sin, k, r, tiles, raw_t):
                w = 256 * tiles
                dve.tensor_copy(raw_t[:, 0:w], acc[k % 2][:, 0:w]).then_inc(rot_in, 1)
                dve.wait_ge(rot_done, r + 1)
                ps = acc[k % 2][:, 0:w].rearrange("p (j s) -> p j s", j=tiles)
                rw = raw_t[:, 0:w].rearrange("p (j s) -> p j s", j=tiles)
                cb = cos.unsqueeze(1).broadcast_to([P, tiles, S])
                sb_ = sin.unsqueeze(1).broadcast_to([P, tiles, S])
                dve.tensor_tensor(dst, ps, sb_, ALU.mult)
                dve.tensor_tensor(rw, rw, cb, ALU.mult)
                sync()
                return dve.tensor_tensor(dst, dst, rw, ALU.add)

            def masked(hh, pr, mask, scale):
                dve.wait_ge(scores_ready, hh + 1)
                dve.scalar_tensor_tensor(pr, psS[:, 0:384], scale, mask, ALU.mult, ALU.add)
                sync()
                dve.tensor_reduce(negmax[:, 0:1], pr[:, 0:256], AX_X, ALU.max, negate=True)
                return dve.tensor_reduce(negmax[:, 2:3], pr[:, 256:384], AX_X, ALU.max, negate=True)

            dve.memset(stat[:, :], 1.0)
            dve.wait_ge(bias_ps, 1)
            dve.tensor_copy(o[0:DH, 1, 0:384], psT[0:DH, 0:384]).then_inc(bias_sb, 1)
            dve.wait_ge(pos_loaded, 16)
            dve.wait_ge(small_loaded, 64)
            TWO_PI = 2 * math.pi
            magic = 1.5 * 2.0 ** 23
            c1 = 6.28125
            c2 = float(np.float32((TWO_PI - c1) * 2 ** 19 // 1 / 2 ** 19))
            c3 = TWO_PI - c1 - c2
            ang = junk[:, 0:256]
            turns = junk[:, 256:512]
            dve.tensor_copy(ang, pos_i[:, :])
            sync()
            dve.tensor_scalar(ang, ang, par("inv_freq"), None, ALU.mult)
            sync()
            for which, shift in ((1, 0.0), (2, 0.25)):
                r = pos_t[:, which, :]
                dve.tensor_scalar(turns, ang, 1.0 / TWO_PI, shift, ALU.mult, ALU.add)
                sync()
                dve.tensor_scalar(turns, turns, magic, None, ALU.add)
                sync()
                dve.tensor_scalar(turns, turns, magic, None, ALU.subtract)
                sync()
                dve.scalar_tensor_tensor(r, turns, -c1, ang, ALU.mult, ALU.add)
                sync()
                dve.scalar_tensor_tensor(r, turns, -c2, r, ALU.mult, ALU.add)
                sync()
                dve.scalar_tensor_tensor(r, turns, -c3, r, ALU.mult, ALU.add)
                sync()
                if shift:
                    dve.tensor_scalar(r, r, math.pi / 2, None, ALU.add)
                    sync()
                m = dve.tensor_scalar(r, r, 3.1415925, -3.1415925, ALU.min, ALU.max)
            m.then_inc(angle_ready, 1)
            dve.wait_ge(table_ready, 1)
            for j in range(4):
                dve.wait_ge(bias_flip, j + 1)
                dve.tensor_copy(bias[:, 2 * j:2 * j + 2, :].rearrange("p a b -> p (a b)"),
                                psS[:, 512 * (j % 2):512 * (j % 2) + 512]).then_inc(bias_done, 1)
            dve.wait_ge(x_loaded, 16)

            halves_of_x = lambda t: [x[:, t, 0:1024], x[:, t, 1024:2048]]
            jk = junk
            with dve.Fori(0, DEPTH) as l:
                dve.tensor_copy(lcur[:, :], lsmall[:, bass.ds(l, 1), :].rearrange("p a w -> p (a w)"))
                sync()
                for i in range(2):
                    dve.tensor_tensor_reduce(out=jk[:, 64 * i:64 * i + 64], in0=lay("lambda", 128 * i, 128 * i + 64),
                                             in1=lay("lambda", 128 * i + 64, 128 * i + 128), scale=1.0, scalar=0.0,
                                             op0=ALU.mult, op1=ALU.add, accum_out=lam[:, i:i + 1])
                sync()
                dve.tensor_scalar(subg[:, :], lay("subln"), lay("one_minus"), None, ALU.mult).then_inc(lam_in, 1)
                for what, d in LAYER_ITEMS:
                    if what == "stats":
                        kind = d["kind"]
                        if kind == "x":
                            mean_squares(lambda t: [x[:, t, 0:1024], x[:, t, 1024:2048]], D, 1e-6, l * LAYER_S + d["s"])
                            make_diag()
                            dve.wait_ge(lam_exp, l + 1)
                            dve.tensor_tensor(lam[:, 4:5], lam[:, 3:4], lam[:, 2:3], ALU.subtract)
                            sync()
                            dve.tensor_tensor(lam[:, 5:6], lam[:, 4:5], lay("lam_init"), ALU.subtract)
                            sync()
                        else:
                            a = c_at if kind == "cq" else c_at + 512
                            mean_squares(lambda t: [o[:, t, a:a + 512]], 512, 1e-6, l * LAYER_S + d["s"])
                            make_diag()
                    elif what == "turn":
                        turn_rest(d["kind"], d["n"], d["k"], l * LAYER_T + d["t"])
                    elif what == "evac":
                        kind, n, k = d["kind"], d["n"], d["k"]
                        ps = acc[k % 2]
                        two = ps[:, :].rearrange("p (t n) -> p t n", t=NT)
                        cols = slice(512 * n, 512 * n + 512)
                        if kind in ("kr", "qr"):
                            sync()
                        if kind != "z":
                            dve.wait_ge(w_used, l * LAYER_G + d["g"])
                        if kind in ("q", "qn"):
                            dve.tensor_copy(qT[:, 4 * n:4 * n + 4, :].rearrange("p c s -> p (c s)"), ps[:, :])\
                                .then_inc(acc_free[k % 2], 1)
                        elif kind in ("k", "kn"):
                            dve.tensor_copy(kT[:, 4 * n:4 * n + 4, :].rearrange("p c s -> p (c s)"), ps[:, :])\
                                .then_inc(acc_free[k % 2], 1)
                        elif kind in ("v", "vb"):
                            dve.tensor_copy(v[:, :, cols], two).then_inc(acc_free[k % 2], 1)
                        elif kind in ("cq", "ckv"):
                            a = c_at if kind == "cq" else c_at + 512
                            dve.tensor_copy(o[:, :, a:a + 512], two).then_inc(acc_free[k % 2], 1)
                            sync()
                        elif kind == "kr":
                            rotate(kr[:, :].unsqueeze(1), cst("cos"), cst("sin"), k, l * 2, 1, unrot)\
                                .then_inc(acc_free[k % 2], 1)
                        elif kind == "qr":
                            rotate(qr[:, :, :], cst("cos"), cst("sin"), k, l * 2 + 1, 4, unrot)\
                                .then_inc(acc_free[k % 2], 1)
                        elif kind == "z":
                            moved(dve, k, l * (LAYER_K // 2))
                            dve.tensor_tensor(o[:, :, cols], o[:, :, cols], act_out[:, :, :], ALU.mult)\
                                .then_inc(act_read, 1)
                        elif kind == "out":
                            dve.tensor_tensor(x[:, :, cols], x[:, :, cols], two, ALU.add)\
                                .then_inc(acc_free[k % 2], 1)
                            if n == 3:
                                sync()
                    elif what == "head_scores":
                        h = d["h"]
                        hh = l * HEADS + h
                        if h < DH:
                            dve.wait_ge(scores_ready, hh + 1)
                            pss = psS[:, :].rearrange("p (m n) -> p m n", m=2)
                            b_all = bias[:, h, :].unsqueeze(1).broadcast_to([P, 2, 256])
                            b_diag = bias[:, h, 128:256].unsqueeze(1).broadcast_to([P, 2, 128])
                            dve.scalar_tensor_tensor(prob[:, :, 0:256], pss[:, :, 0:256], 64 ** -0.5, b_all,
                                                     ALU.mult, ALU.add)
                            dve.scalar_tensor_tensor(prob[:, :, 256:384], pss[:, :, 256:384], 64 ** -0.5, b_diag,
                                                     ALU.mult, ALU.add)
                            sync()
                            dve.tensor_reduce(negmax[:, 0:2], prob[:, :, 0:256], AX_X, ALU.max, negate=True)
                            dve.tensor_reduce(negmax[:, 2:4], prob[:, :, 256:384], AX_X, ALU.max, negate=True)\
                                .then_inc(negmax_ready, 1)
                        else:
                            masked(hh, prob[:, 0, :], cst("causal"), 192 ** -0.5).then_inc(negmax_ready, 1)
                    elif what == "head_weights":
                        h = d["h"]
                        sync()
                        dve.wait_ge(exp_ready, l * HEADS + h + 1)
                        if h < DH:
                            dve.reciprocal(rinv[:, :], sums[:, :])
                            sync()
                            for j in (1, 3):
                                dve.tensor_scalar(rinv[:, j:j + 1], rinv[:, j:j + 1], lam[:, 5:6], None, ALU.mult)
                            sync()
                            parts = ((0, 256, 0), (256, 384, 2))
                            for a, b, j in parts:
                                dve.tensor_scalar(prob[:, 1, a:b], prob[:, 1, a:b], rinv[:, j + 1:j + 2], None, ALU.mult)
                            sync()
                            for a, b, j in parts:
                                m = dve.scalar_tensor_tensor(prob[:, 0, a:b], prob[:, 0, a:b], rinv[:, j:j + 1],
                                                             prob[:, 1, a:b], ALU.mult, ALU.add)
                            m.then_inc(weights_ready, 1)
                        else:
                            for j in (0, 2):
                                dve.reciprocal(rinv[:, j:j + 1], sums[:, j:j + 1])
                            sync()
                    elif what == "head_out":
                        h = d["h"]
                        dve.wait_ge(pv_ready, l * HEADS + h + 1)
                        pso = psO[:, 0:256].rearrange("p (t n) -> p t n", t=NT)
                        if h < DH:
                            dve.tensor_copy(o[:, :, P * h:P * h + P], pso).then_inc(head_read, 1)
                        else:
                            dve.tensor_scalar(o[:, 0, P * h:P * h + P], pso[:, 0, :], rinv[:, 2:3], None, ALU.mult)
                            dve.tensor_scalar(o[:, 1, P * h:P * h + P], pso[:, 1, :], rinv[:, 0:1], None, ALU.mult)\
                                .then_inc(head_read, 1)
                    elif what == "subln":
                        sync()
                        for t in range(NT):
                            oa = o[:, t, 0:1024]
                            dve.tensor_tensor(jk[:, :], oa, oa, ALU.mult)
                            sync()
                            dve.tensor_reduce(stat[:, 8 * t:8 * t + 8], jk[:, :].rearrange("p (h n) -> p h n", h=DH),
                                              AX_X, ALU.add)
                            sync()
                        dve.tensor_scalar(stat[:, 16:32], stat[:, 0:16], 1.0 / P, 1e-6, ALU.mult, ALU.add)\
                            .then_inc(ms_ready, 1)
                        dve.wait_ge(root_ready, l * LAYER_S + d["s"] + 1)
                        dve.reciprocal(stat[:, 48:64], stat[:, 32:48])
                        sync()
                        for t in range(NT):
                            oa = o[:, t, 0:1024].rearrange("p (h n) -> p h n", h=DH)
                            dve.tensor_tensor(oa, oa, stat[:, 48 + 8 * t:56 + 8 * t].unsqueeze(2).to_broadcast([P, DH, P]),
                                              ALU.mult)
                        sync()
                        for t in range(NT):
                            oa = o[:, t, 0:1024].rearrange("p (h n) -> p h n", h=DH)
                            dve.tensor_tensor(oa, oa, subg[:, :].unsqueeze(1).broadcast_to([P, DH, P]), ALU.mult)
                        sync()
            mean_squares(halves_of_x, D, 1e-6, DEPTH * LAYER_S)
            for t in range(NT):
                m = dve.scalar_tensor_tensor(x[:, t, :], x[:, t, :], stat[:, 48 + t:49 + t], gain[:, :],
                                             ALU.mult, ALU.mult)
            m.then_inc(final1_ready, 1)
            sync()

            HB = DEPTH * HEADS
            jk = junk2
            dve.memset(stage[:, :, 0:TAPS - 1], 0.0)
            by_head = lambda a, n=SSM_P: a.rearrange("p (h n) -> p h n", n=n)
            for what, d in B2_ITEMS:
                if what == "stats":
                    kind = d["kind"]
                    src = ys if kind == "y" else x
                    mean_squares(lambda t: [src[:, t, 0:1024], src[:, t, 1024:2048]], D,
                                 1e-5 if kind == "y" else 1e-6, S2 + d["s"])
                    make_diag()
                elif what == "turn":
                    turn_rest(d["kind"], d["n"], d["k"], T2 + d["t"])
                elif what == "evac":
                    kind, n, k = d["kind"], d["n"], d["k"]
                    ps = acc[k % 2]
                    two = ps[:, :].rearrange("p (t n) -> p t n", t=NT)
                    cols = slice(512 * n, 512 * n + 512)
                    if kind in ("q", "kv", "ssd_br"):
                        sync()
                    if kind in ("q", "kv", "dt", "attn_br", "ssd_br", "w_o"):
                        dve.wait_ge(w_used, G2 + d["g"])
                    if kind == "q":
                        rotate(q2[:, 4 * n:4 * n + 4, :], cos2[:, :], sin2[:, :], k, DEPTH * 2 + n, 4, attn[:, 0, :])\
                            .then_inc(acc_free[k % 2], 1)
                    elif kind == "kv":
                        dve.tensor_copy(v2[:, :, :], ps[:, 512:1024].rearrange("p (t n) -> p t n", t=NT))
                        rotate(k2[:, :, :], cos2[:, :], sin2[:, :], k, DEPTH * 2 + 2, 2, attn[:, 0, :])\
                            .then_inc(acc_free[k % 2], 1)
                    elif kind == "xbc":
                        moved(dve, K2 + k)
                        if n >= 1:
                            dve.wait_ge(conv_done, n)
                        if n >= 3:
                            dve.wait_ge(back_ready, n - 1)
                        for tap in range(TAPS):
                            for j in range(4):
                                w = par("conv_w", (4 * n + j) * TAPS + tap, (4 * n + j) * TAPS + tap + 1)
                                a = stage[:, j, tap:tap + S]
                                if tap == 0:
                                    m = dve.tensor_scalar(conv[:, j, :], a, w, par("conv_b", 4 * n + j, 4 * n + j + 1),
                                                          ALU.mult, ALU.add)
                                else:
                                    m = dve.scalar_tensor_tensor(conv[:, j, :], a, w, conv[:, j, :], ALU.mult, ALU.add)
                            if tap < TAPS - 1:
                                sync()
                        m.then_inc(conv_sum, 1)
                    elif kind == "dt":
                        dve.tensor_tensor(dts[:, 0, :].rearrange("p (t n) -> p t n", t=NT), two[:, :, 0:SSM_H],
                                          par("dt_bias").unsqueeze(1).broadcast_to([P, NT, SSM_H]), ALU.add)\
                            .then_inc(acc_free[k % 2], 1)
                        sync()
                        dve.tensor_scalar(dts[:, 1, :], dts[:, 0, :], -1.0, None, ALU.mult)
                        sync()
                        dve.tensor_tensor(dts[:, 1, :], dts[:, 1, :], dts[:, 0, :], ALU.min).then_inc(dt_step, 1)
                        dve.wait_ge(dt_act, 1)
                        dve.tensor_scalar(dts[:, 3, :], dts[:, 2, :], 1.0, None, ALU.add).then_inc(dt_step, 1)
                        sync()
                        dve.tensor_scalar(dts[:, 9, :], dts[:, 3, :], 1.0, None, ALU.subtract)
                        sync()
                        dve.tensor_scalar(dts[:, 10, :], dts[:, 9, :], 1e-30, None, ALU.max)
                        dve.tensor_scalar(dts[:, 11, :], dts[:, 9, :], 0.0, None, ALU.is_equal)
                        sync()
                        dve.reciprocal(dts[:, 10, :], dts[:, 10, :])
                        dve.tensor_tensor(dts[:, 11, :], dts[:, 11, :], dts[:, 2, :], ALU.mult)
                        dve.wait_ge(dt_act, 2)
                        dve.tensor_tensor(dts[:, 9, :], dts[:, 4, :], dts[:, 2, :], ALU.mult)
                        sync()
                        dve.tensor_tensor(dts[:, 9, :], dts[:, 9, :], dts[:, 10, :], ALU.mult)
                        sync()
                        dve.tensor_tensor(dts[:, 9, :], dts[:, 9, :], dts[:, 11, :], ALU.add)
                        sync()
                        dve.scalar_tensor_tensor(dts[:, 5, :], dts[:, 0, :], 0.0, dts[:, 9, :], ALU.max, ALU.add)
                        sync()
                        dve.scalar_tensor_tensor(dts[:, 6, :].rearrange("p (t n) -> p t n", t=NT),
                                                 dts[:, 5, :].rearrange("p (t n) -> p t n", t=NT), -1.0,
                                                 dts[:, 8, 0:SSM_H].unsqueeze(1).broadcast_to([P, NT, SSM_H]),
                                                 ALU.mult, ALU.mult).then_inc(dt_step, 1)
                    elif kind == "z":
                        moved(dve, K2 + k)
                        dve.tensor_tensor(ys[:, :, cols], ys[:, :, cols], act_out[:, :, :], ALU.mult).then_inc(act_read, 1)
                        if n == 3:
                            sync()
                    elif kind == "attn_br":
                        dve.tensor_tensor(ga[:, :, cols], ga[:, :, cols], two, ALU.mult).then_inc(acc_free[k % 2], 1)
                    elif kind == "ssd_br":
                        m = dve.tensor_tensor(act_out[:, :, :], x[:, :, cols], two, ALU.mult)
                        if n == 3:
                            m.then_inc(merged_free, 1)
                        sync()
                        dve.tensor_tensor(ga[:, :, cols], ga[:, :, cols], act_out[:, :, :], ALU.add)\
                            .then_inc(acc_free[k % 2], 1)
                    elif kind == "w_o":
                        if n == 0:
                            dve.wait_ge(refetched, 16)
                        dve.tensor_tensor(x[:, :, cols], x[:, :, cols], two, ALU.add).then_inc(acc_free[k % 2], 1)
                        if n == 3:
                            sync()
                elif what == "back":
                    n, k = d["n"], d["k"]
                    dve.wait_ge(back_ready, n + 1)
                    if n == 0:
                        m = dve.tensor_copy(bt[:, :], acc[k % 2][:, 0:512])
                    else:
                        m = dve.tensor_copy(ys[:, :, 512 * (n - 1):512 * n],
                                            acc[k % 2][:, :].rearrange("p (t n) -> p t n", t=NT))
                    m.then_inc(acc_free[k % 2], 1)
                elif what == "head_scores":
                    dve.wait_ge(scores_ready, HB + d["h"] + 1)
                    dve.scalar_tensor_tensor(prob2[:, :], psS[:, 0:384], HD ** -0.5, cst("window"), ALU.mult, ALU.add)
                    sync()
                    dve.tensor_reduce(negmax[:, 1:2], prob2[:, 0:256], AX_X, ALU.max)
                    dve.tensor_reduce(negmax[:, 3:4], prob2[:, 256:384], AX_X, ALU.max)
                    sync()
                    sink = par("sinks", d["h"], d["h"] + 1)
                    dve.tensor_scalar(negmax[:, 0:1], negmax[:, 1:2], sink, -1.0, ALU.max, ALU.mult)
                    dve.tensor_scalar(negmax[:, 2:3], negmax[:, 3:4], sink, -1.0, ALU.max, ALU.mult)\
                        .then_inc(negmax_ready, 1)
                elif what == "head_weights":
                    dve.wait_ge(exp_ready, HB + d["h"] + 1)
                    sync()
                    for j in (0, 2):
                        dve.tensor_tensor(rinv[:, j:j + 1], sums[:, j:j + 1], sums[:, j + 1:j + 2], ALU.add)
                    sync()
                    for j in (0, 2):
                        dve.reciprocal(rinv[:, j:j + 1], rinv[:, j:j + 1])
                    sync()
                elif what == "head_out":
                    h = d["h"]
                    dve.wait_ge(pv_ready, HB + h + 1)
                    dve.tensor_scalar(attn[:, 0, HD * h:HD * h + HD], psO[:, 0:HD], rinv[:, 2:3], None, ALU.mult)
                    dve.tensor_scalar(attn[:, 1, HD * h:HD * h + HD], psO[:, HD:2 * HD], rinv[:, 0:1], None, ALU.mult)\
                        .then_inc(head_read, 1)
                elif what == "decay":
                    dve.wait_ge(acs_ready, 1)
                    dve.tensor_copy(dts[:, 7, :], psO[:, 0:64])
                    sync()
                    dve.tensor_tensor(dts[:, 10, 0:32], psO[:, 64:96], dts[:, 7, 0:32], ALU.subtract)
                    dve.tensor_copy(dts[:, 10, 32:64], psO[:, 32:64]).then_inc(decay_in, 1)
                    for c in range(NT):
                        dve.tensor_tensor(by_head(xd[:, c, :]), by_head(ys[:, c, :]),
                                          dts[:, 5, 32 * c:32 * c + 32].unsqueeze(2).to_broadcast([P, SSM_H, SSM_P]),
                                          ALU.mult)
                    sync()
                    for c in range(NT):
                        dve.tensor_tensor(by_head(ys[:, c, :]), by_head(ys[:, c, :]),
                                          par("d_skip").unsqueeze(2).to_broadcast([P, SSM_H, SSM_P]), ALU.mult)
                    dve.wait_ge(decay_ready, 1)
                    sync()
                elif what == "group_cb":
                    grp = d["grp"]
                    dve.wait_ge(cb_ready, grp + 1)
                    dve.tensor_tensor(cbm[:, :, :], psS[:, 0:256].rearrange("p (c n) -> p c n", c=NT),
                                      tri.unsqueeze(1).broadcast_to([P, NT, P]), ALU.mult).then_inc(cb_read, 1)
                    wait(dve, state_ps, grp)
                    dve.tensor_tensor(by_head(xw[:, :]), by_head(xd[:, 0, 512 * grp:512 * grp + 512]),
                                      dts[:, 9, 8 * grp:8 * grp + 8].unsqueeze(2).to_broadcast([P, 8, SSM_P]),
                                      ALU.mult).then_inc(xw_ready, 1)
                elif what == "group_off":
                    grp = d["grp"]
                    dve.wait_ge(off_ready, grp + 1)
                    dve.tensor_tensor(by_head(act_out[:, 0, :]), by_head(psS[:, 512:1024]),
                                      dts[:, 9, 32 + 8 * grp:40 + 8 * grp].unsqueeze(2).to_broadcast([P, 8, SSM_P]),
                                      ALU.mult).then_inc(off_read, 1)
                    sync()
                    y1 = ys[:, 1, 512 * grp:512 * grp + 512]
                    dve.tensor_tensor(y1, y1, act_out[:, 0, :], ALU.add)
                    sync()
                elif what == "unit_rows":
                    u, c, h0 = d["u"], d["c"], d["h0"]
                    dve.wait_ge(rows_ready, u + 1)
                    if u >= 2:
                        dve.wait_ge(diag_out, u - 1)
                    for j in range(4):
                        col = 32 * c + h0 + j
                        m = dve.tensor_scalar(decay[:, u % 2, P * j:P * j + P], psT[:, P * j:P * j + P],
                                              dts[:, 7, col:col + 1], 0.0, ALU.subtract, ALU.min)
                    m.then_inc(diff_ready, 1)
                elif what == "unit_mask":
                    u, c = d["u"], d["c"]
                    dve.wait_ge(unit_exp, u + 1)
                    dd = decay[:, u % 2, :].rearrange("p (j n) -> p j n", j=4)
                    dve.tensor_tensor(dd, dd, cbm[:, c, :].unsqueeze(1).broadcast_to([P, 4, P]), ALU.mult)\
                        .then_inc(unit_ready, 1)
                elif what == "unit_out":
                    u, c, h0 = d["u"], d["c"], d["h0"]
                    dve.wait_ge(diag_out, u + 1)
                    yy = ys[:, c, 64 * h0:64 * h0 + 256]
                    dve.tensor_tensor(yy, yy, psO[:, 0:256], ALU.add).then_inc(diag_read, 1)
                    if u == 15:
                        sync()

            dve.wait_ge(p_hi, 1)
            dve.tensor_tensor(pl[:, :, :], praw[:, :, :], ph[:, :, :].bitcast(F32), ALU.subtract).then_inc(p_lo, 1)
            flat = act_out[:, :, :].rearrange("p t n -> p (t n)")
            for part, (g_up, k_up, hbs, g_dn, k_dn) in enumerate(
                    [(G_UP1, K_UP1, HB1, G_DN1, K_DN1), (G_UP2, K_UP2, HB2, G_DN2, K_DN2)]):
                done = 0 if part == 0 else HB1
                with dve.Fori(0, hbs) as i:
                    moved(dve, k_up, i)
                    dve.wait_ge(w_used, 16 * i + (g_up + 16))
                    dve.tensor_tensor(flat, flat, acc[UP][:, :], ALU.mult).then_inc(acc_free[UP], 1)
                    dve.wait_ge(turn_hi, i + (T2 + B2_T + done + 1))
                    dve.tensor_tensor(fl[:, bass.ds(4 * i, 4), :].rearrange("p c s -> p (c s)"), flat,
                                      fh[:, bass.ds(4 * i, 4), :].rearrange("p c s -> p (c s)").bitcast(F32),
                                      ALU.subtract).then_inc(act_read, 1)
                per = 2 * hbs
                with dve.Fori(0, 2) as i:
                    for side in range(2):
                        xc = x[:, :, bass.ds(1024 * i + 512 * side, 512)]
                        dve.wait_ge(w_used, 2 * per * i + (g_dn + per * (side + 1)))
                        dve.tensor_tensor(xc, xc, acc[(k_dn + side) % 2][:, :].rearrange("p (t n) -> p t n", t=NT),
                                          ALU.add).then_inc(acc_free[(k_dn + side) % 2], 1)
                sync()

            jk = junk3
            mean_squares(halves_of_x, D, 1e-6, S2 + B2_S)
            make_diag()
            for n in range(4):
                turn_rest("ple", n, K_PT + n, T2 + B2_T + HIDDEN_BLOCKS + n)
            for n in range(4):
                cols = slice(512 * n, 512 * n + 512)
                moved(dve, K_PLE + 2 * n)
                dve.wait_ge(w_used, G_PLE + 9 * n + 9)
                dve.tensor_tensor(flat, flat, acc[UP][:, :], ALU.mult).then_inc(acc_free[UP], 1)
                sync()
                dve.tensor_tensor(x[:, :, cols], x[:, :, cols], act_out[:, :, :], ALU.add).then_inc(act_read, 1)
            sync()
            mean_squares(halves_of_x, D, 1e-6, S2 + B2_S + 1)
            dve.wait_ge(gain2_loaded, 16)
            for t in range(NT):
                dve.scalar_tensor_tensor(x[:, t, :], x[:, t, :], stat[:, 48 + t:49 + t], gain[:, :],
                                         ALU.mult, ALU.mult).then_inc(result_ready, 1)


def _pack(table, width, parts, rows=P):
    a = np.zeros((rows, width), np.float32)
    for name, v in parts.items():
        at, w = table[name]
        a[:, at:at + w] = v
    return a


def _columns(v):
    return np.asarray(v).reshape(-1, P).T


def _granules(w, cols, chunks=2):
    w = w[:, cols]
    k, n = w.shape
    return w.reshape(k // P // chunks, chunks, P, n).transpose(0, 2, 1, 3).reshape(-1, P, chunks * n)


def _constants():
    i = np.arange(P)
    rot = np.zeros((P, P), np.float32)
    for d in range(P):
        if d % 64 < 32:
            rot[d + 32, d] = -1.0
        else:
            rot[d - 32, d] = 1.0
    diag = np.where(i[None, :] > i[:, None], NEG, 0.0)
    none = np.zeros((P, P))
    near = np.where(i[None, :] > i[:, None], 0.0, NEG)
    inv = (1.0 / (np.float32(10000.0) ** (np.arange(0, 64, 2, dtype=np.float32) / np.float32(64)))).astype(np.float32)
    ang = (np.arange(S, dtype=np.float32)[None, :] * inv[i % 32][:, None]).astype(np.float32).astype(np.float64)
    return _pack(CONST_COLS, CONST_W, dict(
        ident=np.eye(P), rot=rot, tri=(i[:, None] <= i[None, :]), flip=np.eye(P)[::-1],
        causal=np.concatenate([none, diag, diag], 1), window=np.concatenate([near, diag, diag], 1),
        cos=np.cos(ang), sin=np.sin(ang)))


def _bias_onehot():
    dist = 255 - np.arange(383)
    n = np.maximum(dist, 0)
    nf = np.maximum(n, 1).astype(np.float32)
    large = 16 + (np.log(nf / np.float32(16)) / np.float32(math.log(8)) * np.float32(16)).astype(np.int32)
    bucket = np.where(n < 16, n, np.minimum(large, 31))
    a = np.zeros((33, 384), np.float32)
    a[bucket[dist >= 0], np.nonzero(dist >= 0)[0]] = 1.0
    a[32, :383] = np.where(dist < 0, NEG, 0.0)
    return a


def _weights(i):
    blocks = []
    add = lambda w, cols, chunks=2: blocks.append(_granules(w, cols, chunks))
    span = lambda a, n=512: np.arange(a, a + n)
    for l in range(DEPTH):
        w = i["w_in"][l]
        for at in (0, 512, 1024, 1536, 2048, 2560, 4096, 4608):
            add(w, span(at))
        add(w, np.concatenate([span(5120, 64)] * 2), 8)
        uq, ukv = i["w_uq"][l], i["w_ukv"][l]
        for half in range(2):
            add(uq, np.concatenate([span(192 * h, 128) for h in range(4 * half, 4 * half + 4)]))
        add(uq, np.concatenate([span(192 * h + 128, 64) for h in range(MH)]))
        for off in (0, 128):
            for half in range(2):
                add(ukv, np.concatenate([span(256 * h + off, 128) for h in range(4 * half, 4 * half + 4)]))
        for at in (3072, 3584, 5184, 5696):
            add(w, span(at))
        for n in range(4):
            add(i["w_out"][l], span(512 * n))
    w = i["w_in_2"][0]
    for at in (0, 512, 1024, 5632, 6144, 3584, 4096, 4608, 5120):
        add(w, span(at))
    dt = np.zeros((D, 64), np.float32)
    dt[:, :SSM_H] = w[:, 6656:6688]
    add(dt, span(0, 64), 16)
    for first in (6688, 8736, 1536):
        for n in range(4):
            add(w, span(first + 512 * n))
    for name in ("w_attn_br_2", "w_ssd_br_2", "w_o_2"):
        for n in range(4):
            add(i[name][0], span(512 * n))
    for a, b in ((0, HB1), (HB1, HIDDEN_BLOCKS)):
        for hb in range(a, b):
            add(i["w_gate_2"][0], span(512 * hb))
            add(i["w_up_2"][0], span(512 * hb))
        for n in range(4):
            add(i["w_down_2"][0][512 * a:512 * b], span(512 * n))
    for n in range(4):
        add(i["w_ple_gate_2"][0], span(512 * n))
        add(i["w_ple_proj_2"][0], span(512 * n))
    return np.concatenate(blocks, 0)


def kernel(**inputs):
    import concourse.bacc as bacc
    from concourse.bass_utils import run_bass_kernel_spmd

    i = {k: np.asarray(v) for k, v in inputs.items()}
    row = lambda v: np.broadcast_to(np.asarray(v).reshape(1, -1), (P, np.asarray(v).size))
    layer_small = []
    for l in range(DEPTH):
        lambda_init = 0.8 - 0.6 * math.exp(-0.3 * l)
        layer_small.append(_pack(LAYER_COLS, LAYER_W, {
            "norm": _columns(i["norm_g"][l]), "q_norm": _columns(i["mla_q_norm_g"][l]),
            "kv_norm": _columns(i["mla_kv_norm_g"][l]), "lam_init": lambda_init, "one_minus": 1.0 - lambda_init,
            "lambda": row(i["diff_lambda"][l]), "subln": row(i["diff_subln_g"][l])}))
    order = np.concatenate([np.arange(2048, 3072), np.arange(0, 2048)])
    conv_w = i["conv_w_2"][0][:, order].reshape(TAPS, 24, P).transpose(2, 1, 0).reshape(P, 24 * TAPS)
    inv = (np.float32(10000.0) ** (-np.arange(32, dtype=np.float32) * np.float32(2.0) / np.float32(64))).astype(np.float32)
    block2_small = _pack(BLOCK2_COLS, BLOCK2_W, {
        "mix": _columns(i["g_mix_2"][0]), "ffn": _columns(i["g_ffn_2"][0]), "ple": _columns(i["g_ple_2"][0]),
        "ssd": _columns(i["g_ssd_2"][0]), "conv_w": conv_w, "conv_b": _columns(i["conv_b_2"][0][order]),
        "dt_bias": row(i["dt_bias_2"][0]), "a_log": row(i["a_log_2"][0]), "d_skip": row(i["d_skip_2"][0]),
        "sinks": row(i["sinks_2"][0]), "inv_freq": inv[np.arange(P) % 32][:, None]})
    bias_rows = np.concatenate([i["rel_bias_table"], np.ones((1, DH), np.float32)], 0)
    arrays = {
        "wstream": _weights(i), "x_in": np.ascontiguousarray(i["x"][0]),
        "p_in": np.ascontiguousarray(i["p_2"][0, 0].T.reshape(2, P, S).transpose(1, 0, 2)),
        "positions": np.ascontiguousarray(i["positions_2"].reshape(S)),
        "layer_small": np.stack(layer_small), "block2_small": block2_small, "const_in": _constants(),
        "bias_rows": bias_rows, "bias_onehot": _bias_onehot(),
        "gain_final1": np.ascontiguousarray(row(i["final_norm_g"])),
        "gain_final2": np.ascontiguousarray(row(i["g_final_2"])),
    }
    nc = bacc.Bacc("TRN2", target_bir_lowering=False, num_devices=1)
    args = [nc.dram_tensor(n, a.shape, mybir.dt.from_np(a.dtype), kind="ExternalInput").ap()
            for n, a in arrays.items()]
    args.append(nc.dram_tensor("out", (S, D), F32, kind="ExternalOutput").ap())
    build(nc, *args)
    r = run_bass_kernel_spmd(nc, [arrays], core_ids=[0])
    return r.results[0]["out"].reshape(1, S, D)
```

```python
import math
from contextlib import ExitStack

import concourse.bass as bass
import numpy as np
from concourse import mybir

F32 = mybir.dt.float32
F32R = mybir.dt.float32r
I32 = mybir.dt.int32
ALU = mybir.AluOpType
ACT = mybir.ActivationFunctionType
AX_X = mybir.AxisListType.X

P = 128
S = 256
NT = S // P
D = 2048
DC = D // P
DEPTH = 2
GW = 1024
RING = 4
LOOK = RING
NEG = -1e30

DH, MH = 8, 8
SWA_H, KV_H, HD = 16, 4, 64
SSM_H, SSM_G, SSM_N, SSM_P = 32, 4, 128, 64
TAPS = 4
FFN = 5632
HIDDEN_BLOCKS = FFN // 512
PARTS = (4, 4, 3)
PAIRS = DC // 2

LAYER_COLS = {}
BLOCK2_COLS = {}
CONST_COLS = {}


def _lay(table, widths):
    at = 0
    for name, w in widths:
        table[name] = (at, w)
        at += w
    return at


LAYER_W = _lay(LAYER_COLS, [("norm", DC), ("next_norm", DC), ("q_norm", 4), ("kv_norm", 4), ("lam_init", 1), ("one_minus", 1),
                            ("lambda", 256), ("subln", 128)])
BLOCK2_W = _lay(BLOCK2_COLS, [("final1", DC), ("mix", DC), ("ffn", DC), ("ple", DC), ("ssd", DC), ("conv_w", 24 * TAPS),
                              ("conv_b", 24), ("dt_bias", SSM_H), ("a_log", SSM_H), ("d_skip", SSM_H),
                              ("sinks", SWA_H), ("inv_freq", 1)])
CONST_W = _lay(CONST_COLS, [("ident", P), ("rot", P), ("tri", P), ("flip", P), ("causal", 384),
                            ("cos", S), ("sin", S), ("near", P)])
RESIDENT = CONST_W - P
LAYER_OWN = LAYER_COLS["lambda"][0]


class Plan:

    def __init__(self):
        self.items, self.later = [], []
        self.g = self.k = self.t = 0

    def item(self, what, **d):
        self.items.append((what, d))

    def at(self, when, what, **d):
        self.later.append((when, what, d))
        self.later.sort(key=lambda x: x[0])

    def flush(self, upto=10 ** 9):
        while self.later and self.later[0][0] <= upto:
            _, what, d = self.later.pop(0)
            if what == "turn":
                self.turn(**d)
            else:
                self.item(what, **d)

    def turn(self, kind, m):
        self.item("turn", kind=kind, m=m, t=self.t)
        self.t += 1

    def product(self, kind, n, granules, evac_after=0):
        d = dict(kind=kind, n=n, of=granules, k=self.k)
        end = self.g + granules
        for i in range(granules):
            self.item("gran", i=i, g=self.g, **d)
            self.g += 1
            self.flush(self.g)
        if evac_after:
            self.at(end + evac_after, "evac", g=end, **d)
        else:
            self.item("evac", g=end, **d)
        self.k += 1

    def step(self, what, **d):
        self.item(what, k=self.k, **d)
        self.k += 1

    def heads(self, first, count, spacing, start):
        for h in range(first, first + count + 1):
            gap = start + spacing * (h - first)
            if h > first:
                self.at(gap, "head_turn", h=h - 1)
            if h < first + count:
                self.at(gap, "head_scores", h=h)
            if h > first:
                self.at(gap + 1, "head_out", h=h - 1)
            if h < first + count:
                self.at(gap + 1, "head_weights", h=h)


def layer_plan():
    p = Plan()
    p.item("root", kind="x")
    p.at(1, "turn", kind="x_last", m=6)
    p.at(3, "turn", kind="x_last", m=7)
    p.at(5, "spread", kind="x")
    for kind in ("q", "k"):
        for n in range(2):
            p.product(kind, n, 8)
    p.product("v", 0, 8)
    p.heads(0, DH, 3, p.g + 1)
    p.product("v", 1, 8)
    p.product("cq", 0, 8)
    p.item("cstats", kind="cq", c=0)
    p.product("ckv", 0, 8)
    p.step("cturn", kind="cq", c=0)
    p.item("cstats", kind="ckv", c=1)
    p.product("kr", 0, 2)
    p.flush()
    p.step("cturn", kind="ckv", c=1)
    p.item("subln")
    for n in range(2):
        p.product("qn", n, 2)
    p.product("qr", 0, 2)
    for n in range(2):
        p.product("kn", n, 2)
    for n in range(2):
        p.product("vb", n, 2)
    p.heads(DH, MH, 2, p.g + 1)
    for n in range(4):
        if n == 3:
            p.flush()
        p.product("z", n, 8)
        p.at(p.g + 2, "turn", kind="o", m=2 * n)
        p.at(p.g + 4, "turn", kind="o", m=2 * n + 1)
    for n in range(4):
        p.product("out", n, 8)
        if n < 3:
            p.at(p.g + 2, "turn", kind="x_next", m=2 * n)
            p.at(p.g + 4, "turn", kind="x_next", m=2 * n + 1)
    assert not p.later
    return p


def block2_plan():
    p = Plan()
    p.item("root", kind="x1")
    p.at(1, "turn", kind="u_last", m=6)
    p.at(3, "turn", kind="u_last", m=7)
    p.at(4, "second_norm")
    p.at(9, "spread", kind="u")
    p.product("q", 0, 8, evac_after=2)
    p.product("q", 1, 8)
    p.product("kv", 0, 8)
    p.heads(0, SWA_H, 2, p.g + 5)
    p.product("xbc", 0, 8)
    p.product("xbc", 1, 8)
    p.step("back", n=0)
    for n in range(2, 6):
        p.product("xbc", n, 8)
        if n > 2:
            p.step("back", n=n - 2)
    p.product("dt", 0, 1)
    p.step("back", n=4)
    p.flush()
    p.item("decay")
    gap = p.g + 4
    for grp in range(SSM_G):
        p.at(gap, "group_cb", grp=grp)
        p.at(gap + 1, "group_state", grp=grp)
        p.at(gap + 2, "group_off", grp=grp)
        gap += 3
        for c in range(NT):
            for half in range(2):
                u = (grp * NT + c) * 2 + half
                d = dict(u=u, grp=grp, c=c, h0=grp * 8 + half * 4)
                p.at(gap, "unit_rows", **d)
                p.at(gap + 1, "unit_mask", **d)
                p.at(gap + 2, "unit_out", **d)
                gap += 3
    for n in range(4):
        p.product("ga", n, 8)
    for n in range(4):
        p.product("gs", n, 8)
    p.flush()
    for n in range(4):
        if n < 2:
            p.at(p.g + 6, "turn", kind="attn", m=2 * n)
            p.at(p.g + 7, "turn", kind="attn", m=2 * n + 1)
        p.product("z", n, 8)
        p.at(p.g + 2, "turn", kind="y", m=2 * n)
        p.at(p.g + 4, "turn", kind="y", m=2 * n + 1)
    p.item("root", kind="y")
    for n in range(4):
        p.product("attn_br", n, 4)
    p.flush()
    for n in range(4):
        p.product("ssd_br", n, 8)
        p.at(p.g + 2, "turn", kind="merged", m=2 * n)
        p.at(p.g + 4, "turn", kind="merged", m=2 * n + 1)
    for n in range(4):
        p.product("w_o", n, 8)
        if n < 3:
            p.at(p.g + 2, "turn", kind="f", m=2 * n)
            p.at(p.g + 4, "turn", kind="f", m=2 * n + 1)
    p.item("root", kind="f")
    for m in (6, 7):
        p.turn("f", m)
    p.item("spread", kind="f")
    assert not p.later
    return p


def down_plan():
    p = Plan()
    for n in range(4):
        p.product("down", n, 2 * PARTS[-1])
        if n < 3:
            p.at(p.g + 2, "turn", kind="ple", m=2 * n)
            p.at(p.g + 4, "turn", kind="ple", m=2 * n + 1)
    return p


def embedding_plan():
    p = Plan()
    p.item("root", kind="ple")
    p.at(1, "turn", kind="ple", m=6)
    p.at(3, "turn", kind="ple", m=7)
    for n in range(4):
        p.product("gate", n, 8)
        p.product("proj", n, 1)
    return p


def freed(pair, k):
    return (k - pair) // 2 + 1


LAYER, B2, DOWN, PLE = layer_plan(), block2_plan(), down_plan(), embedding_plan()
LAYER_STEP = {(d["kind"], d["n"]): d["k"] for what, d in LAYER.items if what == "evac"}
LAYER_STEP.update({(d["kind"], "turn"): d["k"] for what, d in LAYER.items if what == "cturn"})
BACK0 = DEPTH * LAYER.k + next(d["k"] for what, d in B2.items if what == "back")
PRO_T = 6
G2 = DEPTH * LAYER.g
K2 = DEPTH * LAYER.k
T2 = PRO_T + DEPTH * LAYER.t
LAYER_S = 4
S2 = DEPTH * LAYER_S
G_FFN, K_FFN = G2 + B2.g, K2 + B2.k
FFN_PARTS = []
_g, _k, _b = G_FFN, K_FFN, 0
for _hbs in PARTS:
    FFN_PARTS.append(dict(g_up=_g, k_up=_k, hbs=_hbs, g_dn=_g + 16 * _hbs, k_dn=_k + 2 * _hbs, done=_b))
    _g += 16 * _hbs + 8 * _hbs
    _k += 2 * _hbs + 4
    _b += _hbs
G_PLE, K_PLE = _g, _k
G_ALL = G_PLE + PLE.g
T_DOWN = T2 + B2.t
T_PLE = T_DOWN + DOWN.t
assert LAYER.g % RING == 0 and LAYER.k % 2 == 0
HEADS = DH + MH
B2_STEP = {(d["kind"], d["n"]): d["k"] for what, d in B2.items if what == "evac"}
TURN = {(name, d["kind"], d["m"]): d["t"] for name, plan in (("layer", LAYER), ("block2", B2))
        for what, d in plan.items if what == "turn"}
DG2 = DEPTH * 3
G_DOWN, K_DOWN = FFN_PARTS[-1]["g_dn"], FFN_PARTS[-1]["k_dn"]
GATE, UP = K_FFN % 2, 1 - K_FFN % 2
assert all(p["k_up"] % 2 == GATE for p in FFN_PARTS) and K_PLE % 2 == GATE


def build(nc, wstream, x_in, p_in, positions, layer_small, block2_small, const_in, bias_rows, bias_onehot,
          gain_final1, gain_final2, out):
    rev = nc.dram_tensor("bias_by_distance", (DH, 384), F32, kind="Internal")
    spill = nc.dram_tensor("residual_spill", (S, D), F32, kind="Internal").ap()

    place = {"at": (nc.sbuf_base + 31) // 32 * 32}

    def sb(name, shape, dt=F32, at=None):
        size = 4 * int(np.prod(shape[1:]))
        where = place["at"] if at is None else at
        if at is None:
            place["at"] += (size + 31) // 32 * 32
        assert where + size <= 229344, name
        ends[0] = max(ends[0], where + size)
        return nc.alloc_sbuf_tensor_at(name, shape, dt, offset=where)

    ends = [0]

    ctx = ExitStack()
    with ctx:
        def psum(name, cols):
            return ctx.enter_context(nc.psum_tensor(name, [P, cols], F32))

        def sem(name):
            return ctx.enter_context(nc.semaphore(name))

        raw = sb("raw", [P, RING, GW])
        whi = sb("whi", [P, RING, GW], F32R)
        wlo = sb("wlo", [P, RING, GW], F32R)
        x = sb("x", [P, NT, D])
        xh = sb("xh", [P, DC, S], F32R)
        xl = sb("xl", [P, DC, S], F32R)
        const = sb("const", [P, RESIDENT])
        cos2 = sb("cos2", [P, S])
        sin2 = sb("sin2", [P, S])
        lsmall = sb("lsmall", [P, DEPTH, LAYER_W])
        lcur = sb("lcur", [P, LAYER_OWN])
        bsmall = sb("bsmall", [P, BLOCK2_W])
        diag = sb("diag", [P, NT, P])
        act_out = sb("act_out", [P, NT, 512])
        rs = sb("rs", [P, 8])
        rbc = sb("rbc", [P, 1, S])
        stat = sb("stat", [P, 64])
        lam = sb("lam", [P, 8])
        subg = sb("subg", [P, P])
        negmax = sb("negmax", [P, 4])
        sums = sb("sums", [P, 4])
        rinv = sb("rinv", [P, 4])
        region = place["at"]

        K = 1024
        at = lambda kib: region + kib * K
        bh = sb("bh", [P, DC, S], F32R, at=at(16))
        bl = sb("bl", [P, DC, S], F32R, at=at(32))
        bias = sb("bias", [P, DH, 256], at=at(0))
        v = sb("v", [P, NT, 1024], at=at(8))
        ch = sb("ch", [P, 8, S], F32R, at=at(16))
        cl = sb("cl", [P, 8, S], F32R, at=at(32))
        qT = sb("qT", [P, 8, S], at=at(24))
        kT = sb("kT", [P, 8, S], at=at(40))
        qr = sb("qr", [P, 4, S], at=at(48))
        kr = sb("kr", [P, S], at=at(52))
        o = sb("o", [P, NT, 2 * 1024], at=at(53))
        c_at = 1024
        unrot = sb("unrot", [P, 1024], at=at(69))
        prob = sb("prob", [P, 2, 384], at=at(73))
        probT = sb("probT", [P, 384], at=at(76))
        pos_i = sb("pos_i", [P, S], I32, at=at(73))
        pos_t = sb("pos_t", [P, 3, S], at=at(74))
        gain1 = sb("gain1", [P, D], at=at(80))
        junk = sb("junk", [P, 1024], at=at(88))

        xd = sb("xd", [P, NT, D], at=at(0))
        q2 = sb("q2", [P, 8, S], at=at(0))
        kk2 = sb("kk2", [P, KV_H, S], at=at(8))
        k2 = sb("k2", [P, 2, S], at=at(12))
        v2 = sb("v2", [P, NT, 256], at=at(14))
        ah = sb("ah", [P, 8, S], F32R, at=at(0))
        al = sb("al", [P, 8, S], F32R, at=at(8))
        bcT = sb("bcT", [P, 8, S], at=at(16))
        stage = sb("stage", [P, 4, S + TAPS - 1], at=at(24))
        conv = sb("conv", [P, 4, S], at=at(28) + 64)
        decay = sb("decay", [P, 2, 512], at=at(24))
        xw = sb("xw", [P, 512], at=at(28))
        state = sb("state", [P, 512], at=at(30))
        bt = sb("bt", [P, 512], at=at(33))
        cbm = sb("cbm", [P, NT, P], at=at(35))
        prob2 = sb("prob2", [P, 384], at=at(36))
        probT2 = sb("probT2", [P, 384], at=at(38))
        dts = sb("dts", [P, 12, 64], at=at(40))
        ys = sb("ys", [P, NT, D], at=at(48))
        attn = sb("attn", [P, NT, 1024], at=at(64))
        ga = sb("ga", [P, NT, D], at=at(72))

        gain2 = sb("gain2", [P, D], at=at(0))
        fh = sb("fh", [P, 4 * max(PARTS), S], F32R, at=at(48))
        fl = sb("fl", [P, 4 * max(PARTS), S], F32R, at=at(64))
        praw = sb("praw", [P, 2, S], at=at(80))
        ph = sb("ph", [P, 2, S], F32R, at=at(82))
        pl = sb("pl", [P, 2, S], F32R, at=at(84))

        acc = [psum("acc0", 1024), psum("acc1", 1024)]
        psS = psum("psS", 1024)
        psT = psum("psT", 512)
        psO = psum("psO", 512)

        def cst(name, rows=P):
            at, w = CONST_COLS[name]
            return const[0:rows, at:at + w]

        def lay(name, a=0, b=None):
            at, w = LAYER_COLS[name]
            return lcur[:, at + a:at + (w if b is None else b)]

        def par(name, a=0, b=None):
            at, w = BLOCK2_COLS[name]
            return bsmall[:, at + a:at + (w if b is None else b)]

        ident, rot, tri = cst("ident"), cst("rot"), cst("tri")

        w_loaded = [sem(f"w_loaded{i}") for i in range(RING)]
        hi_ready = sem("hi_ready")
        lo_ready = sem("lo_ready")
        w_used = sem("w_used")
        acc_free = [sem(f"acc_free{i}") for i in range(2)]
        act_read = sem("act_read")
        negmax_ready = sem("negmax_ready")
        head_read = sem("head_read")
        turned = sem("turned")
        turn_hi = sem("turn_hi")
        turn_lo = sem("turn_lo")
        cturned = sem("cturned")
        cturn_hi = sem("cturn_hi")
        ms_ready = sem("ms_ready")
        root_ready = sem("root_ready")
        r_ready = sem("r_ready")
        diag_ready = sem("diag_ready")
        row_ready = sem("row_ready")
        rot_in = sem("rot_in")
        rot_done = sem("rot_done")
        scores_ready = sem("scores_ready")
        exp_ready = sem("exp_ready")
        weights_ready = sem("weights_ready")
        probT_in_psum = sem("probT_in_psum")
        probT_ready = sem("probT_ready")
        pv_ready = sem("pv_ready")
        const_loaded = sem("const_loaded")
        masks_loaded = sem("masks_loaded")
        lsmall_loaded = sem("lsmall_loaded")
        bsmall_loaded = sem("bsmall_loaded")
        gain1_loaded = sem("gain1_loaded")
        x_loaded = [sem(f"x_loaded{i}") for i in range(2)]
        bias_loaded = sem("bias_loaded")
        bias_ps = sem("bias_ps")
        bias_sb = sem("bias_sb")
        bias_out = sem("bias_out")
        bias_in = sem("bias_in")
        bias_flip = sem("bias_flip")
        bias_done = sem("bias_done")
        pos_loaded = sem("pos_loaded")
        angle_ready = sem("angle_ready")
        table_ready = sem("table_ready")
        lam_in = sem("lam_in")
        lam_exp = sem("lam_exp")
        final1_ready = sem("final1_ready")
        spilled = sem("spilled")
        near_loaded = sem("near_loaded")
        refetched = sem("refetched")
        gain2_loaded = sem("gain2_loaded")
        k_spread = sem("k_spread")
        conv_sum = sem("conv_sum")
        conv_done = sem("conv_done")
        back_ready = sem("back_ready")
        dt_step = sem("dt_step")
        dt_act = sem("dt_act")
        acs_ready = sem("acs_ready")
        decay_in = sem("decay_in")
        decay_ready = sem("decay_ready")
        cb_ready = sem("cb_ready")
        xw_ready = sem("xw_ready")
        cb_read = sem("cb_read")
        state_ps = sem("state_ps")
        state_ready = sem("state_ready")
        off_ready = sem("off_ready")
        off_read = sem("off_read")
        rows_ready = sem("rows_ready")
        diff_ready = sem("diff_ready")
        unit_exp = sem("unit_exp")
        unit_ready = sem("unit_ready")
        diag_out = sem("diag_out")
        diag_read = sem("diag_read")
        merged_free = sem("merged_free")
        gate_done = sem("gate_done")
        hid_ready = sem("hid_ready")
        hid_hi = sem("hid_hi")
        hid_lo = sem("hid_lo")
        p_loaded = sem("p_loaded")
        p_hi = sem("p_hi")
        p_lo = sem("p_lo")
        result_ready = [sem(f"result_ready{t}") for t in range(NT)]
        stored = sem("stored")

        block = ctx.enter_context(nc.Block())

        def moved(eng, k, more=0):
            eng.wait_ge(acc_free[k % 2], more + (k // 2 + 2))

        def wait(eng, signal, value):
            if not (isinstance(value, int) and value <= 0):
                eng.wait_ge(signal, value)

        @block.sync
        def _(sp):
            def load(g, slot):
                sp.dma_start(raw[:, slot, :], wstream[g, :, :]).then_inc(w_loaded[slot], 16)

            sp.dma_start(bias[0:33, 0, 0:DH], bias_rows).then_inc(bias_loaded, 16)
            sp.dma_start(bias[0:33, 2:4, :].rearrange("p a b -> p (a b)")[:, 0:384], bias_onehot).then_inc(bias_loaded, 16)
            sp.dma_start(const[:, 0:4 * P], const_in[:, 0:4 * P]).then_inc(const_loaded, 16)
            for half in range(2):
                cols = slice(1024 * half, 1024 * half + 1024)
                sp.dma_start(x[:, :, cols], x_in.rearrange("(t p) d -> p t d", p=P)[:, :, cols])\
                    .then_inc(x_loaded[half], 16)
                if half == 0:
                    sp.dma_start(lsmall[:, :, :], layer_small.rearrange("l p w -> p l w")).then_inc(lsmall_loaded, 16)
                load(2 * half, 2 * half)
                load(2 * half + 1, 2 * half + 1)
            sp.dma_start(bsmall[:, :], block2_small).then_inc(bsmall_loaded, 16)
            sp.dma_start(pos_i[:, :], positions.partition_broadcast(P)).then_inc(pos_loaded, 16)
            sp.wait_ge(bias_sb, 1)
            sp.dma_start(rev.ap(), o[0:DH, 1, 0:384]).then_inc(bias_out, 16)
            sp.wait_ge(bias_out, 16)
            sp.dma_start(o[:, 0, :].rearrange("p (h n) -> p h n", h=DH),
                         bass.AP(rev, 0, [[1, P], [384, DH], [1, 256]])).then_inc(bias_in, 16)
            sp.dma_start(const[:, 4 * P:], const_in[:, 4 * P:RESIDENT]).then_inc(masks_loaded, 16)
            sp.dma_start(gain1[:, :], gain_final1).then_inc(gain1_loaded, 16)

            with sp.Fori(1, G_ALL // RING) as i:
                for j in range(RING):
                    sp.wait_ge(lo_ready, RING * i + (j + 1 - RING))
                    sp.dma_start(raw[:, j, :], wstream[bass.ds(RING * i + j, 1), :, :]
                                 .rearrange("a p n -> p (a n)")).then_inc(w_loaded[j], 16)
            for g in range(G_ALL // RING * RING, G_ALL):
                sp.wait_ge(lo_ready, g + 1 - RING)
                load(g, g % RING)
            for t in range(NT):
                sp.wait_ge(result_ready[t], 1)
                sp.dma_start(out[P * t:P * t + P, :], x[:, t, :]).then_inc(stored, 16)
            sp.wait_ge(stored, 16 * NT)

        @block.gpsimd
        def _(pool):
            def rest(g, j, first):
                pool.wait_ge(hi_ready, g + 1)
                if not first:
                    pool.wait_ge(w_used, g + 1 - RING)
                pool.tensor_tensor(wlo[:, j, :], raw[:, j, :], whi[:, j, :].bitcast(F32),
                                   ALU.subtract).then_inc(lo_ready, 1)

            for g in range(RING):
                rest(g, g, True)
            with pool.Fori(1, G_ALL // RING) as i:
                for j in range(RING):
                    rest(RING * i + j, j, False)
            for g in range(G_ALL // RING * RING, G_ALL):
                rest(g, g % RING, False)

        def turn_of(kind):
            return {
                "x": (x, xh, xl, lambda c: lsmall[:, 0, c:c + 1]),
                "x_last": (x, xh, xl, lambda c: lay("norm", c, c + 1)),
                "x_next": (x, xh, xl, lambda c: lay("next_norm", c, c + 1)),
                "u_last": (x, xh, xl, lambda c: par("mix", c, c + 1)),
                "o": (o, bh, bl, None),
                "attn": (attn, ah, al, None),
                "y": (ys, bh, bl, lambda c: par("ssd", c, c + 1)),
                "merged": (ga, xh, xl, None),
                "f": (x, bh, bl, lambda c: par("ffn", c, c + 1)),
                "ple": (x, xh, xl, lambda c: par("ple", c, c + 1)),
            }[kind]

        def turn_bank(kind, m):
            b = 1 if kind == "o" else m % 2
            return psS[:, 512 * b:512 * b + 512]

        @block.tensor
        def _(pe):
            def claim(k, more=0):
                pe.wait_ge(acc_free[k % 2], more + (k // 2 + 1))

            def granule(g, slot, out_ps, form, ah_, al_, chunk0, chunks, first, last_one, width=512):
                pe.wait_ge(lo_ready, g + 1)
                per = GW // chunks
                wh = whi[:, slot, :].rearrange("p (c n) -> p c n", c=chunks)
                wl = wlo[:, slot, :].rearrange("p (c n) -> p c n", c=chunks)
                m = None
                for c in range(chunks):
                    begin = first and c == 0
                    end = last_one and c == chunks - 1
                    kc = chunk0 + c
                    if form in ("B", "KV", "KR"):
                        for j in range({"B": 4, "KV": 2, "KR": 1}[form]):
                            dst = out_ps[:, 256 * j:256 * j + 256]
                            js = slice(128 * j, 128 * j + 128)
                            pe.matmul(dst, wh[:, c, js], ah_[:, kc, :], start=begin and j % 2 == 0, stop=False,
                                      skip_group_check=True)
                            pe.matmul(dst, wh[:, c, js], al_[:, kc, :], start=False, stop=False,
                                      skip_group_check=True)
                            m = pe.matmul(dst, wl[:, c, js], ah_[:, kc, :], start=False, stop=end,
                                          skip_group_check=True)
                    if form in ("A", "KV"):
                        for t in range(NT):
                            lo, step = (0, 512) if form == "A" else (512, 256)
                            dst = out_ps[:, lo + step * t:lo + step * t + width]
                            cols = slice(0, width) if form == "A" else slice(256, 512)
                            ts = slice(P * t, P * t + P)
                            shared = form == "KV"
                            pe.matmul(dst, ah_[:, kc, ts], wh[:, c, cols], start=begin and not (shared and t),
                                      stop=False, skip_group_check=shared)
                            pe.matmul(dst, ah_[:, kc, ts], wl[:, c, cols], start=False, stop=False,
                                      skip_group_check=shared)
                            m = pe.matmul(dst, al_[:, kc, ts], wh[:, c, cols], start=False, stop=end,
                                          skip_group_check=shared)
                m.then_inc(w_used, 1)

            def turn(kind, m, t_value):
                src = turn_of(kind)[0]
                wait(pe, turn_lo, t_value if kind == "o" else t_value - 1)
                bank = turn_bank(kind, m)
                for j in range(2):
                    for t in range(NT):
                        c = 2 * m + j
                        z = pe.transpose(bank[:, 256 * j + P * t:256 * j + P * t + P], src[:, t, c * P:c * P + P], ident)
                z.then_inc(turned, 1)

            def spread():
                for t in range(NT):
                    m = pe.matmul(psT[:, P * t:P * t + P], tri[:, P - 1:P].to_broadcast([P, P]), diag[:, t, :],
                                  start=True, stop=True)
                m.then_inc(row_ready, 1)

            FORMS = dict(q="B", k="B", v="A", cq="A", ckv="A", kr="KR", qn="B", qr="B", kn="B", vb="A",
                         z="A", out="A", kv="KV", xbc="B", dt="A", ga="A", gs="A", attn_br="A", ssd_br="A", w_o="A")

            def scores(hh, tiles):
                pe.wait_ge(negmax_ready, hh + 1)
                for n, parts in enumerate(tiles):
                    base = 512 * n
                    for part, (qa, ka) in enumerate(parts):
                        one = dict(start=part == 0, stop=part == len(parts) - 1)
                        m = pe.matmul(psS[:, base:base + 256], qa[:, P:S], ka[:, 0:S], **one)
                    for part, (qa, ka) in enumerate(parts):
                        one = dict(start=part == 0, stop=part == len(parts) - 1)
                        m = pe.matmul(psS[:, base + 256:base + 384], qa[:, 0:P], ka[:, 0:P], **one)
                m.then_inc(scores_ready, 1)

            def head_turn(src):
                for j in range(3):
                    m = pe.transpose(psT[:, P * j:P * j + P], src[:, P * j:P * j + P], ident)
                m.then_inc(probT_in_psum, 1)

            def head_out(hh, pt, vv, w):
                pe.wait_ge(probT_ready, hh + 1)
                pe.wait_ge(head_read, hh + 1)
                pe.matmul(psO[:, w:2 * w], pt[:, 0:P], vv(0), start=True, stop=False)
                pe.matmul(psO[:, w:2 * w], pt[:, P:2 * P], vv(1), start=False, stop=True)
                m = pe.matmul(psO[:, 0:w], pt[:, 2 * P:3 * P], vv(0), start=True, stop=True)
                m.then_inc(pv_ready, 1)

            pe.wait_ge(bias_loaded, 32)
            pe.matmul(psT[0:DH, 0:384], bias[0:33, 0, 0:DH],
                      bias[0:33, 2:4, :].rearrange("p a b -> p (a b)")[:, 0:384], start=True, stop=True)\
                .then_inc(bias_ps, 1)
            pe.wait_ge(const_loaded, 16)
            pe.wait_ge(x_loaded[0], 16)
            for m in range(PRO_T):
                if m == 4:
                    pe.wait_ge(x_loaded[1], 16)
                turn("x", m, m)
            pe.wait_ge(bias_in, 16)
            for j in range(4):
                if j >= 2:
                    pe.wait_ge(bias_done, j - 1)
                pe.matmul((psO, psT)[j % 2][:, 0:512], cst("flip"), o[:, 0, 512 * j:512 * j + 512],
                          start=True, stop=True).then_inc(bias_flip, 1)
            pe.wait_ge(bias_done, 4)

            with pe.Fori(0, DEPTH) as l:
                uses = l * (LAYER.k // 2)
                tb = l * LAYER.t + PRO_T

                def read_upto(step):
                    for b in range(2):
                        pe.wait_ge(acc_free[b], uses + (1 + freed(b, LAYER_STEP[step])))

                for what, d in LAYER.items:
                    if what == "gran":
                        kind, n, i = d["kind"], d["n"], d["i"]
                        if i == 0:
                            claim(d["k"], uses)
                            if kind in ("qn", "kn") and n == 0:
                                moved(pe, LAYER_STEP[("cq" if kind == "qn" else "ckv", "turn")], uses)
                        if kind == "q" and n == 0:
                            pe.wait_ge(turn_lo, tb + (i - 5))
                        if kind == "out" and n == 0:
                            pe.wait_ge(turn_lo, tb + (TURN["layer", "o", i] + 1))
                        a, b, c0 = xh, xl, 2 * i
                        chunks = 8 if kind == "kr" else 2
                        if kind == "kr":
                            c0 = 8 * i
                        if kind in ("qn", "qr"):
                            a, b = ch, cl
                        if kind in ("kn", "vb"):
                            a, b, c0 = ch, cl, 4 + 2 * i
                        if kind == "out":
                            a, b = bh, bl
                        granule(l * LAYER.g + d["g"], d["g"] % RING, acc[d["k"] % 2], FORMS[kind], a, b, c0,
                                chunks, i == 0, i == d["of"] - 1)
                    elif what == "turn":
                        kind, m = d["kind"], d["m"]
                        if kind == "x_last":
                            pe.wait_ge(acc_free[1], uses + 1)
                        elif kind == "o":
                            pe.wait_ge(act_read, l * 4 + (m // 2 + 2))
                        else:
                            moved(pe, LAYER_STEP["out", m // 2], uses)
                            if m == 0:
                                pe.wait_ge(negmax_ready, l * HEADS + (HEADS + 1))
                        turn(kind, m, tb + d["t"])
                    elif what == "spread":
                        pe.wait_ge(diag_ready, l * 3 + 1)
                        spread()
                    elif what == "cturn":
                        c, k = d["c"], d["k"]
                        claim(k, uses)
                        pe.wait_ge(diag_ready, l * 3 + (c + 2))
                        for j in range(4):
                            for t in range(NT):
                                at_ = c_at + 512 * c + P * j
                                m = pe.matmul(acc[k % 2][:, 256 * j + P * t:256 * j + P * t + P], o[:, t, at_:at_ + P],
                                              diag[:, t, :], start=True, stop=True)
                        m.then_inc(cturned, 1)
                    elif what == "evac" and d["kind"] in ("kr", "qr"):
                        r = 0 if d["kind"] == "kr" else 1
                        pe.wait_ge(rot_in, l * 2 + r + 1)
                        for j in range(1 if r == 0 else 4):
                            m = pe.matmul(acc[d["k"] % 2][:, 256 * j:256 * j + 256], rot,
                                          unrot[:, 256 * j:256 * j + 256], start=True, stop=True)
                        m.then_inc(rot_done, 1)
                    elif what == "head_scores":
                        h = d["h"]
                        if h < DH:
                            if h == 0:
                                read_upto(("k", 1))
                            scores(l * HEADS + h, [[(qT[64 * m:64 * m + 64, h, :], kT[64 * m:64 * m + 64, h, :])]
                                                   for m in range(2)])
                        else:
                            e = h - DH
                            if e == 0:
                                read_upto(("vb", 1))
                            half = slice(64 * (e % 2), 64 * (e % 2) + 64)
                            scores(l * HEADS + h, [[(qT[:, e, :], kT[:, e, :]), (qr[half, e // 2, :], kr[half, :])]])
                    elif what == "head_turn":
                        h = d["h"]
                        if h < DH:
                            pe.wait_ge(weights_ready, l * DH + h + 1)
                        else:
                            pe.wait_ge(exp_ready, l * HEADS + h + 1)
                        head_turn(prob[:, 0, :])
                    elif what == "head_out":
                        h = d["h"]
                        e = h % DH
                        if h in (0, 4):
                            read_upto(("v", h // 4))
                        head_out(l * HEADS + h, probT, lambda c, e=e: v[:, c, e * P:e * P + P], P)

            HB = DEPTH * HEADS
            for what, d in B2.items:
                if what == "gran":
                    kind, n, i = d["kind"], d["n"], d["i"]
                    if i == 0:
                        claim(K2 + d["k"])
                    if n == 0 and kind == "q":
                        pe.wait_ge(turn_lo, T2 + i - 5)
                    operand = {"attn_br": "attn", "ssd_br": "y", "w_o": "merged"}.get(kind)
                    if n == 0 and operand:
                        pe.wait_ge(turn_lo, T2 + TURN["block2", operand, i] + 1)
                    a, b = {"attn_br": (ah, al), "ssd_br": (bh, bl)}.get(kind, (xh, xl))
                    chunks = 16 if kind == "dt" else 2
                    granule(G2 + d["g"], (G2 + d["g"]) % RING, acc[d["k"] % 2], FORMS[kind], a, b, 2 * i,
                            chunks, i == 0, i == d["of"] - 1, width={"dt": SSM_H, "kv": 256}.get(kind, 512))
                elif what == "turn":
                    kind, m = d["kind"], d["m"]
                    if kind == "u_last":
                        moved(pe, K2 - 1)
                    elif kind == "attn":
                        if m == 0:
                            pe.wait_ge(head_read, HB + SWA_H + 1)
                            pe.wait_ge(cb_read, SSM_G)
                            pe.wait_ge(off_read, SSM_G)
                    elif kind == "y":
                        pe.wait_ge(act_read, DEPTH * 4 + m // 2 + 2)
                    else:
                        moved(pe, K2 + B2_STEP["ssd_br" if kind == "merged" else "w_o", m // 2])
                    turn(kind, m, T2 + d["t"])
                elif what == "spread":
                    pe.wait_ge(diag_ready, DG2 + (1 if d["kind"] == "u" else 2))
                    spread()
                elif what == "evac" and d["kind"] in ("q", "kv"):
                    r = DEPTH * 2 + (d["n"] if d["kind"] == "q" else 2)
                    pe.wait_ge(rot_in, r + 1)
                    for j in range(4 if d["kind"] == "q" else 2):
                        m = pe.matmul(acc[d["k"] % 2][:, 256 * j:256 * j + 256], rot,
                                      attn[:, 0, 256 * j:256 * j + 256], start=True, stop=True)
                    m.then_inc(rot_done, 1)
                elif what == "back":
                    n = d["n"]
                    claim(K2 + d["k"])
                    pe.wait_ge(conv_done, 1 if n == 0 else n + 2)
                    for c in range(1 if n == 0 else NT):
                        for j in range(4):
                            src = bcT[:, j, 0:P] if n == 0 else conv[:, j, P * c:P * c + P]
                            m = pe.transpose(acc[d["k"] % 2][:, 512 * c + P * j:512 * c + P * j + P], src, ident)
                    m.then_inc(back_ready, 1)
                elif what == "head_scores":
                    h = d["h"]
                    if h == 0:
                        pe.wait_ge(k_spread, 16 * KV_H * 2)
                    half = slice(64 * (h % 2), 64 * (h % 2) + 64)
                    scores(HB + h, [[(q2[half, h // 2, :], kk2[half, h // (SWA_H // KV_H), :])]])
                elif what == "head_turn":
                    pe.wait_ge(exp_ready, HB + d["h"] + 1)
                    head_turn(prob2[:, :])
                elif what == "head_out":
                    h = d["h"]
                    kvh = h // (SWA_H // KV_H)
                    head_out(HB + h, probT2, lambda c, e=kvh: v2[:, c, e * HD:e * HD + HD], HD)
                elif what == "decay":
                    pe.wait_ge(dt_step, 3)
                    pe.wait_ge(head_read, HB + SWA_H + 1)
                    pe.matmul(psO[:, 0:64], tri, dts[:, 6, :], start=True, stop=True)
                    pe.matmul(psO[:, 64:128], tri[:, P - 1:P].to_broadcast([P, P]), dts[:, 6, :], start=True,
                              stop=True).then_inc(acs_ready, 1)
                elif what == "group_cb":
                    grp = d["grp"]
                    if grp == 0:
                        pe.wait_ge(negmax_ready, HB + SWA_H + 1)
                        pe.wait_ge(conv_done, 6)
                    wait(pe, cb_read, grp)
                    for c in range(NT):
                        m = pe.matmul(psS[:, P * c:P * c + P], bcT[:, grp, P * c:P * c + P],
                                      bcT[:, 4 + grp, P * c:P * c + P], start=True, stop=True)
                    m.then_inc(cb_ready, 1)
                elif what == "group_state":
                    grp = d["grp"]
                    pe.wait_ge(xw_ready, grp + 1)
                    if grp == 0:
                        moved(pe, BACK0)
                    wait(pe, off_read, grp)
                    pe.matmul(psS[:, 512:1024], bt[:, P * grp:P * grp + P], xw[:, :], start=True, stop=True)\
                        .then_inc(state_ps, 1)
                elif what == "group_off":
                    grp = d["grp"]
                    pe.wait_ge(state_ready, grp + 1)
                    pe.matmul(psS[:, 512:1024], bcT[:, 4 + grp, P:S], state[:, :], start=True, stop=True)\
                        .then_inc(off_ready, 1)
                elif what == "unit_rows":
                    u, c, h0 = d["u"], d["c"], d["h0"]
                    if u == 0:
                        pe.wait_ge(probT_ready, HB + SWA_H)
                    wait(pe, diff_ready, u)
                    for j in range(4):
                        a = dts[:, 6, 32 * c + h0 + j:32 * c + h0 + j + 1].to_broadcast([P, P])
                        m = pe.matmul(psT[:, P * j:P * j + P], a, tri, start=True, stop=True)
                    m.then_inc(rows_ready, 1)
                elif what == "unit_out":
                    u, c, h0 = d["u"], d["c"], d["h0"]
                    pe.wait_ge(unit_ready, u + 1)
                    wait(pe, diag_read, u)
                    if u == 0:
                        pe.wait_ge(decay_in, 1)
                    for j in range(4):
                        m = pe.matmul(psO[:, 64 * j:64 * j + 64], decay[:, u % 2, P * j:P * j + P],
                                      xd[:, c, 64 * (h0 + j):64 * (h0 + j) + 64], start=True, stop=True)
                    m.then_inc(diag_out, 1)

            pe.wait_ge(turn_lo, T_DOWN)
            for f in FFN_PARTS:
                with pe.Fori(0, f["hbs"]) as i:
                    for side in range(2):
                        claim(f["k_up"] + side, i)
                        for j in range(8):
                            g = f["g_up"] + 8 * side + j
                            granule(16 * i + g, g % RING, acc[(GATE, UP)[side]], "B", bh, bl, 2 * j, 2, j == 0, j == 7)
                pe.wait_ge(hid_lo, f["done"] + f["hbs"])
                per = 2 * f["hbs"]
                if f is FFN_PARTS[-1]:
                    continue
                with pe.Fori(0, 2) as i:
                    for side in range(2):
                        k = f["k_dn"] + side
                        claim(k, i)
                        for j in range(per):
                            g = f["g_dn"] + per * side + j
                            granule(2 * per * i + g, g % RING, acc[k % 2], "A", fh, fl, 2 * j, 2, j == 0, j == per - 1)
            for what, d in DOWN.items:
                if what == "gran":
                    k, g, i = K_DOWN + d["k"], G_DOWN + d["g"], d["i"]
                    if i == 0:
                        claim(k)
                    granule(g, g % RING, acc[k % 2], "A", fh, fl, 2 * i, 2, i == 0, i == d["of"] - 1)
                elif what == "turn":
                    moved(pe, K_DOWN + d["m"] // 2)
                    turn("ple", d["m"], T_DOWN + d["t"])
            for what, d in PLE.items:
                if what == "gran":
                    k, g, i = K_PLE + d["k"], G_PLE + d["g"], d["i"]
                    if i == 0:
                        claim(k)
                    if d["kind"] == "gate" and d["n"] == 0:
                        pe.wait_ge(turn_lo, T_PLE + i - 5)
                    if d["kind"] == "proj" and d["n"] == 0:
                        pe.wait_ge(p_lo, 1)
                    a, b = (xh, xl) if d["kind"] == "gate" else (ph, pl)
                    granule(g, g % RING, acc[k % 2], "A", a, b, 2 * i, 2, i == 0, i == d["of"] - 1)
                elif what == "turn":
                    moved(pe, K_DOWN + 3)
                    turn("ple", d["m"], T_PLE + d["t"])

        @block.scalar
        def _(act):
            def upper(g, slot, first=False):
                act.wait_ge(w_loaded[slot], 16 * (g // RING + 1))
                if not first:
                    act.wait_ge(w_used, g + 1 - RING)
                act.activation(whi[:, slot, :], raw[:, slot, :], ACT.Copy).then_inc(hi_ready, 1)

            def ahead(g):
                if g + LOOK < G_ALL:
                    upper(g + LOOK, g % RING)

            def turn_round(kind, m, t_value):
                _, dh, _, gain = turn_of(kind)
                act.wait_ge(turned, t_value + 1)
                bank = turn_bank(kind, m)
                if gain is None:
                    z = act.activation(dh[:, 2 * m:2 * m + 2, :].rearrange("p c s -> p (c s)"), bank, ACT.Copy)
                else:
                    for j in range(2):
                        z = act.activation(dh[:, 2 * m + j, :], bank[:, 256 * j:256 * j + 256], ACT.Copy,
                                           scale=gain(2 * m + j))
                z.then_inc(turn_hi, 1)

            def root(s_value):
                act.wait_ge(ms_ready, s_value + 1)
                act.activation(stat[:, 32:48], stat[:, 16:32], ACT.Sqrt).then_inc(root_ready, 1)

            def exps(hh, pr, maps, scale=1.0):
                act.wait_ge(negmax_ready, hh + 2)
                for m in range(maps):
                    act.activation(pr(m)[:, 0:256], pr(m)[:, 0:256], ACT.Exp, bias=negmax[:, m:m + 1],
                                   accum_out=sums[:, m:m + 1])
                    z = act.activation(pr(m)[:, 256:384], pr(m)[:, 256:384], ACT.Exp, bias=negmax[:, 2 + m:3 + m],
                                       accum_out=sums[:, 2 + m:3 + m])
                return z

            def copy_probT(hh, pt):
                act.wait_ge(probT_in_psum, hh + 1)
                act.activation(pt[:, :], psT[:, 0:384], ACT.Copy).then_inc(probT_ready, 1)

            def scaled(dst, k, g_value, func):
                act.wait_ge(w_used, g_value)
                for t in range(NT):
                    z = act.activation(dst[:, t, :], acc[k % 2][:, 512 * t:512 * t + 512], func, scale=rs[:, t:t + 1])
                z.then_inc(acc_free[k % 2], 1)

            for g in range(2):
                upper(g, g, first=True)
            for m in range(PRO_T):
                if m == 0:
                    act.wait_ge(lsmall_loaded, 16)
                turn_round("x", m, m)
                if m == 1:
                    upper(2, 2, first=True)
                if m == 3:
                    upper(3, 3, first=True)
            act.wait_ge(angle_ready, 1)
            act.activation(sin2[:, :], pos_t[:, 1, :], ACT.Sin)
            act.activation(cos2[:, :], pos_t[:, 2, :], ACT.Sin).then_inc(table_ready, 1)

            with act.Fori(0, DEPTH) as l:
                base = l * LAYER.g
                tb = l * LAYER.t + PRO_T
                for what, d in LAYER.items:
                    if what == "gran":
                        g = d["g"]
                        act.wait_ge(w_loaded[g % RING], 16 * (l * (LAYER.g // RING) + (g + LOOK) // RING + 1))
                        act.wait_ge(w_used, base + (g + 1))
                        act.activation(whi[:, g % RING, :], raw[:, g % RING, :], ACT.Copy).then_inc(hi_ready, 1)
                    elif what == "turn":
                        turn_round(d["kind"], d["m"], tb + d["t"])
                    elif what == "cturn":
                        c, name = d["c"], {"cq": "q_norm", "ckv": "kv_norm"}[d["kind"]]
                        act.wait_ge(cturned, l * 2 + (c + 1))
                        for j in range(4):
                            z = act.activation(ch[:, 4 * c + j, :], acc[d["k"] % 2][:, 256 * j:256 * j + 256], ACT.Copy,
                                               scale=lay(name, j, j + 1))
                        z.then_inc(cturn_hi, 1)
                    elif what == "root":
                        root(l * LAYER_S)
                        act.wait_ge(lam_in, l + 1)
                        act.activation(lam[:, 2:4], lam[:, 0:2], ACT.Exp).then_inc(lam_exp, 1)
                    elif what == "cstats":
                        root(l * LAYER_S + (1 + d["c"]))
                    elif what == "subln":
                        root(l * LAYER_S + 3)
                    elif what == "head_scores":
                        h = d["h"]
                        exps(l * HEADS + h, lambda m: prob[:, m, :], 2 if h < DH else 1).then_inc(exp_ready, 1)
                    elif what == "head_turn":
                        copy_probT(l * HEADS + d["h"], probT)
                    elif what == "evac" and d["kind"] == "z":
                        act.wait_ge(act_read, l * 4 + (d["n"] + 1))
                        act.wait_ge(r_ready, l + 1)
                        scaled(act_out, d["k"], base + d["g"], ACT.Silu)

            HB = DEPTH * HEADS
            for what, d in B2.items:
                kind = d.get("kind")
                if what == "gran":
                    ahead(G2 + d["g"])
                elif what == "turn":
                    turn_round(kind, d["m"], T2 + d["t"])
                elif what == "root":
                    root(S2 + {"x1": 0, "y": 2, "f": 3}[kind])
                elif what == "second_norm":
                    act.wait_ge(final1_ready, 1)
                    act.dma_start(spill.rearrange("(t p) d -> p t d", p=P), x[:, :, :]).then_inc(spilled, 16)
                    act.dma_start(cst("causal")[:, 0:P], const_in[:, RESIDENT:]).then_inc(near_loaded, 16)
                    root(S2 + 1)
                elif what == "head_scores":
                    h = d["h"]
                    exps(HB + h, lambda m: prob2[:, :], 1)
                    act.activation(sums[:, 3:4], par("sinks", h, h + 1), ACT.Exp, bias=negmax[:, 2:3])
                    act.activation(sums[:, 1:2], par("sinks", h, h + 1), ACT.Exp, bias=negmax[:, 0:1])\
                        .then_inc(exp_ready, 1)
                elif what == "head_turn":
                    copy_probT(HB + d["h"], probT2)
                elif what == "evac" and kind == "kv":
                    moved(act, K2 + d["k"])
                    for i in range(KV_H):
                        for half in range(2):
                            act.dma_start(kk2[64 * half:64 * half + 64, i, :],
                                          k2[64 * (i % 2):64 * (i % 2) + 64, i // 2, :]).then_inc(k_spread, 16)
                elif what == "evac" and kind == "xbc":
                    n = d["n"]
                    act.wait_ge(conv_sum, n + 1)
                    dst = bcT[:, 4 * n:4 * n + 4, :] if n < 2 else conv[:, :, :]
                    act.activation(dst, conv[:, :, :], ACT.Silu).then_inc(conv_done, 1)
                elif what == "evac" and kind in ("ga", "gs"):
                    if d["n"] == 0:
                        act.wait_ge(r_ready, DEPTH + 1)
                        if kind == "gs":
                            act.wait_ge(spilled, 16)
                    cols = slice(512 * d["n"], 512 * d["n"] + 512)
                    scaled((ga if kind == "ga" else x)[:, :, cols], d["k"], G2 + d["g"], ACT.Sigmoid)
                elif what == "evac" and kind == "z":
                    act.wait_ge(act_read, DEPTH * 4 + d["n"] + 1)
                    scaled(act_out, d["k"], G2 + d["g"], ACT.Silu)
                elif what == "evac" and kind == "dt":
                    act.wait_ge(dt_step, 1)
                    act.activation(dts[:, 8, 0:SSM_H], par("a_log"), ACT.Exp)
                    act.activation(dts[:, 2, :], dts[:, 1, :], ACT.Exp).then_inc(dt_act, 1)
                    act.wait_ge(dt_step, 2)
                    act.activation(dts[:, 4, :], dts[:, 3, :], ACT.Ln).then_inc(dt_act, 1)
                elif what == "decay":
                    act.wait_ge(decay_in, 1)
                    act.activation(dts[:, 9, :], dts[:, 10, :], ACT.Exp).then_inc(decay_ready, 1)
                elif what == "group_state":
                    grp = d["grp"]
                    act.wait_ge(state_ps, grp + 1)
                    act.activation(state[:, :], psS[:, 512:1024], ACT.Copy).then_inc(state_ready, 1)
                elif what == "unit_rows":
                    u = d["u"]
                    act.wait_ge(diff_ready, u + 1)
                    act.activation(decay[:, u % 2, :], decay[:, u % 2, :], ACT.Exp).then_inc(unit_exp, 1)
                elif what == "evac" and kind == "ssd_br" and d["n"] == 3:
                    act.wait_ge(merged_free, 1)
                    act.dma_start(x[:, :, :], spill.rearrange("(t p) d -> p t d", p=P)).then_inc(refetched, 16)
            act.dma_start(praw[:, :, :], p_in).then_inc(p_loaded, 16)
            act.dma_start(gain2[:, :], gain_final2).then_inc(gain2_loaded, 16)

            for f in FFN_PARTS:
                def stream(g_static, i, stride, many):
                    for j in range(many):
                        g = g_static + j
                        act.wait_ge(w_loaded[g % RING], 16 * (stride // RING * i + (g + LOOK) // RING + 1))
                        act.wait_ge(w_used, stride * i + (g + 1))
                        act.activation(whi[:, g % RING, :], raw[:, g % RING, :], ACT.Copy).then_inc(hi_ready, 1)

                flat = act_out[:, :, :].rearrange("p t n -> p (t n)")
                with act.Fori(0, f["hbs"]) as i:
                    stream(f["g_up"], i, 16, 8)
                    moved(act, f["k_up"], i)
                    act.activation(flat, flat, ACT.Silu).then_inc(gate_done, 1)
                    stream(f["g_up"] + 8, i, 16, 8)
                    act.wait_ge(hid_ready, i + (f["done"] + 1))
                    act.activation(fh[:, bass.ds(4 * i, 4), :].rearrange("p c s -> p (c s)"), flat, ACT.Copy)\
                        .then_inc(hid_hi, 1)
                if f is FFN_PARTS[0]:
                    act.wait_ge(p_loaded, 16)
                    act.activation(ph[:, :, :], praw[:, :, :], ACT.Copy).then_inc(p_hi, 1)
                per = 2 * f["hbs"]
                if f is not FFN_PARTS[-1]:
                    with act.Fori(0, 2) as i:
                        stream(f["g_dn"], i, 2 * per, 2 * per)
            for what, d in DOWN.items:
                if what == "gran":
                    ahead(G_DOWN + d["g"])
                elif what == "turn":
                    turn_round("ple", d["m"], T_DOWN + d["t"])
            for what, d in PLE.items:
                if what == "gran":
                    ahead(G_PLE + d["g"])
                elif what == "turn":
                    turn_round("ple", d["m"], T_PLE + d["t"])
                elif what == "root":
                    root(S2 + 4)
                elif what == "evac" and d["kind"] == "gate":
                    act.wait_ge(act_read, DEPTH * 4 + 4 + d["n"] + 1)
                    act.wait_ge(r_ready, DEPTH + 3)
                    scaled(act_out, K_PLE + d["k"], G_PLE + d["g"], ACT.Sigmoid)
            root(S2 + 5)
            act.wait_ge(r_ready, DEPTH + 4)
            act.activation(x[:, 0, :], x[:, 0, :], ACT.Copy, scale=rs[:, 0:1]).then_inc(result_ready[0], 1)

        @block.vector
        def _(dve):
            def sync():
                dve.drain()

            def squares(src, n):
                sync()
                for t in range(NT):
                    a = src[:, t, 512 * n:512 * n + 512]
                    m = dve.tensor_tensor_reduce(out=junk[:, 512 * t:512 * t + 512], in0=a, in1=a, scale=1.0, scalar=0.0,
                                                 op0=ALU.mult, op1=ALU.add, accum_out=stat[:, 4 * t + n:4 * t + n + 1])
                return m

            def mean_of_quarters(eps):
                sync()
                dve.tensor_reduce(stat[:, 8:10], stat[:, 0:8].rearrange("p (t n) -> p t n", t=NT), AX_X, ALU.add)
                sync()
                dve.tensor_scalar(stat[:, 16:18], stat[:, 8:10], 1.0 / D, eps, ALU.mult, ALU.add).then_inc(ms_ready, 1)

            def make_diag(r):
                for t in range(NT):
                    m = dve.tensor_scalar(diag[:, t, :], ident, r[:, t:t + 1], None, ALU.mult)
                m.then_inc(diag_ready, 1)

            def turn_rest(kind, m, t_value):
                _, dh, dl, gain = turn_of(kind)
                bank = turn_bank(kind, m)
                dve.wait_ge(turn_hi, t_value + 1)
                if gain is None:
                    z = dve.tensor_tensor(dl[:, 2 * m:2 * m + 2, :].rearrange("p c s -> p (c s)"), bank,
                                          dh[:, 2 * m:2 * m + 2, :].rearrange("p c s -> p (c s)").bitcast(F32), ALU.subtract)
                else:
                    for j in range(2):
                        c = 2 * m + j
                        z = dve.scalar_tensor_tensor(dl[:, c, :], bank[:, 256 * j:256 * j + 256], gain(c),
                                                     dh[:, c, :].bitcast(F32), ALU.mult, ALU.subtract)
                z.then_inc(turn_lo, 1)

            def spread(count):
                dve.wait_ge(row_ready, count)
                dve.tensor_copy(rbc[:, 0, :], psT[:, 0:S])
                sync()

            def by_token(tiles):
                return rbc[:, :, :].broadcast_to([P, tiles, S])

            def chunks_of(ps, tiles):
                return ps[:, 0:S * tiles].rearrange("p (j s) -> p j s", j=tiles)

            def scaled(dst, ps):
                for t in range(NT):
                    m = dve.tensor_scalar(dst(t), ps[:, 512 * t:512 * t + 512], rs[:, t:t + 1], None, ALU.mult)
                return m

            def rotate(dst, cos, sin, k, r, tiles, raw_t, norm):
                rw = chunks_of(raw_t, tiles)
                ps = chunks_of(acc[k % 2], tiles)
                if norm:
                    dve.tensor_tensor(rw, ps, by_token(tiles), ALU.mult).then_inc(rot_in, 1)
                else:
                    dve.tensor_copy(rw, ps).then_inc(rot_in, 1)
                dve.wait_ge(rot_done, r + 1)
                cb = cos.unsqueeze(1).broadcast_to([P, tiles, S])
                sb_ = sin.unsqueeze(1).broadcast_to([P, tiles, S])
                dve.tensor_tensor(dst, ps, sb_, ALU.mult)
                dve.tensor_tensor(rw, rw, cb, ALU.mult)
                sync()
                return dve.tensor_tensor(dst, dst, rw, ALU.add)

            def masked(hh, pr, mask, scale):
                dve.wait_ge(scores_ready, hh + 1)
                dve.scalar_tensor_tensor(pr, psS[:, 0:384], scale, mask, ALU.mult, ALU.add)
                sync()
                dve.tensor_reduce(negmax[:, 0:1], pr[:, 0:256], AX_X, ALU.max, negate=True)
                return dve.tensor_reduce(negmax[:, 2:3], pr[:, 256:384], AX_X, ALU.max, negate=True)

            for i, signal in enumerate((acc_free[0], acc_free[1], act_read, negmax_ready, head_read)):
                dve.memset(rinv[:, 0:1], 0.0).then_inc(signal, 1)
                sync()
            dve.memset(stat[:, :], 1.0)
            dve.wait_ge(bias_ps, 1)
            dve.tensor_copy(o[0:DH, 1, 0:384], psT[0:DH, 0:384]).then_inc(bias_sb, 1)
            for m in range(PRO_T):
                if m % 3 == 0:
                    dve.wait_ge(x_loaded[m // 3], 16)
                turn_rest("x", m, m)
                if m in (1, 2, 4, 5):
                    squares(x, {1: 0, 2: 1, 4: 2, 5: 3}[m])
            for j in range(4):
                dve.wait_ge(bias_flip, j + 1)
                dve.tensor_copy(bias[:, 2 * j:2 * j + 2, :].rearrange("p a b -> p (a b)"),
                                (psO, psT)[j % 2][:, 0:512]).then_inc(bias_done, 1)
            sync()
            dve.wait_ge(bsmall_loaded, 16)
            dve.tensor_tensor(par("mix"), par("mix"), par("final1"), ALU.mult)
            sync()
            at_next = LAYER_COLS["next_norm"][0]
            dve.tensor_copy(lsmall[:, DEPTH - 1, at_next:at_next + DC], par("mix"))
            dve.wait_ge(pos_loaded, 16)
            TWO_PI = 2 * math.pi
            magic = 1.5 * 2.0 ** 23
            c1 = 6.28125
            c2 = float(np.float32((TWO_PI - c1) * 2 ** 19 // 1 / 2 ** 19))
            c3 = TWO_PI - c1 - c2
            ang = junk[:, 0:256]
            turns = junk[:, 256:768].rearrange("p (a s) -> p a s", a=2)
            r = pos_t[:, 1:3, :]
            dve.tensor_copy(ang, pos_i[:, :])
            sync()
            dve.tensor_scalar(ang, ang, par("inv_freq"), None, ALU.mult)
            sync()
            for which, shift in ((0, 0.0), (1, 0.25)):
                dve.tensor_scalar(turns[:, which, :], ang, 1.0 / TWO_PI, shift, ALU.mult, ALU.add)
            sync()
            dve.tensor_scalar(turns, turns, magic, None, ALU.add)
            sync()
            dve.tensor_scalar(turns, turns, magic, None, ALU.subtract)
            sync()
            dve.scalar_tensor_tensor(r, turns, -c1, ang.unsqueeze(1).broadcast_to([P, 2, S]), ALU.mult, ALU.add)
            sync()
            dve.scalar_tensor_tensor(r, turns, -c2, r, ALU.mult, ALU.add)
            sync()
            dve.scalar_tensor_tensor(r, turns, -c3, r, ALU.mult, ALU.add)
            sync()
            dve.tensor_scalar(pos_t[:, 2, :], pos_t[:, 2, :], math.pi / 2, None, ALU.add)
            sync()
            dve.tensor_scalar(r, r, 3.1415925, -3.1415925, ALU.min, ALU.max).then_inc(angle_ready, 1)
            dve.wait_ge(masks_loaded, 16)
            dve.wait_ge(table_ready, 1)
            sync()

            with dve.Fori(0, DEPTH) as l:
                tb = l * LAYER.t + PRO_T
                uses = l * (LAYER.k // 2)
                dve.tensor_copy(lcur[:, :], lsmall[:, bass.ds(l, 1), 0:LAYER_OWN].rearrange("p a w -> p (a w)"))
                sync()
                own = lambda a, w: lsmall[:, bass.ds(l, 1), a:a + w].rearrange("p a w -> p (a w)")
                dve.tensor_copy(junk[:, 256:512], own(LAYER_COLS["lambda"][0], 256))
                sync()
                for i in range(2):
                    dve.tensor_tensor_reduce(out=junk[:, 64 * i:64 * i + 64], in0=junk[:, 256 + 128 * i:320 + 128 * i],
                                             in1=junk[:, 320 + 128 * i:384 + 128 * i], scale=1.0, scalar=0.0,
                                             op0=ALU.mult, op1=ALU.add, accum_out=lam[:, i:i + 1])
                sync()
                dve.tensor_scalar(subg[:, :], own(LAYER_COLS["subln"][0], P), lay("one_minus"), None, ALU.mult).then_inc(lam_in, 1)
                for what, d in LAYER.items:
                    if what == "root":
                        mean_of_quarters(1e-6)
                        dve.wait_ge(root_ready, l * LAYER_S + 1)
                        dve.reciprocal(rs[:, 0:NT], stat[:, 32:32 + NT]).then_inc(r_ready, 1)
                        sync()
                        make_diag(rs)
                        dve.wait_ge(lam_exp, l + 1)
                        dve.tensor_tensor(lam[:, 4:5], lam[:, 3:4], lam[:, 2:3], ALU.subtract)
                        sync()
                        dve.tensor_tensor(lam[:, 5:6], lam[:, 4:5], lay("lam_init"), ALU.subtract)
                        sync()
                    elif what == "spread":
                        spread(l + 1)
                    elif what == "cstats":
                        at_ = c_at + 512 * d["c"]
                        sync()
                        for t in range(NT):
                            a = o[:, t, at_:at_ + 512]
                            dve.tensor_tensor_reduce(out=junk[:, 512 * t:512 * t + 512], in0=a, in1=a, scale=1.0,
                                                     scalar=0.0, op0=ALU.mult, op1=ALU.add, accum_out=stat[:, t:t + 1])
                        sync()
                        dve.tensor_scalar(stat[:, 16:18], stat[:, 0:2], 1.0 / 512, 1e-6, ALU.mult, ALU.add)\
                            .then_inc(ms_ready, 1)
                        dve.wait_ge(root_ready, l * LAYER_S + (2 + d["c"]))
                        dve.reciprocal(stat[:, 48:50], stat[:, 32:34])
                        sync()
                        make_diag(stat[:, 48:50])
                    elif what == "cturn":
                        c, k, name = d["c"], d["k"], {"cq": "q_norm", "ckv": "kv_norm"}[d["kind"]]
                        dve.wait_ge(cturn_hi, l * 2 + (c + 1))
                        for j in range(4):
                            m = dve.scalar_tensor_tensor(cl[:, 4 * c + j, :], acc[k % 2][:, 256 * j:256 * j + 256],
                                                         lay(name, j, j + 1), ch[:, 4 * c + j, :].bitcast(F32),
                                                         ALU.mult, ALU.subtract)
                        m.then_inc(acc_free[k % 2], 1)
                    elif what == "turn":
                        turn_rest(d["kind"], d["m"], tb + d["t"])
                    elif what == "evac":
                        kind, n, k = d["kind"], d["n"], d["k"]
                        ps = acc[k % 2]
                        free = acc_free[k % 2]
                        two = ps[:, :].rearrange("p (t n) -> p t n", t=NT)
                        cols = slice(512 * n, 512 * n + 512)
                        if kind in ("kr", "qr"):
                            sync()
                        if kind != "z":
                            dve.wait_ge(w_used, l * LAYER.g + d["g"])
                        if kind in ("q", "k"):
                            dst = qT if kind == "q" else kT
                            dve.tensor_tensor(dst[:, 4 * n:4 * n + 4, :], chunks_of(ps, 4), by_token(4), ALU.mult)\
                                .then_inc(free, 1)
                        elif kind in ("qn", "kn"):
                            dst = qT if kind == "qn" else kT
                            dve.tensor_copy(dst[:, 4 * n:4 * n + 4, :].rearrange("p c s -> p (c s)"), ps[:, :])\
                                .then_inc(free, 1)
                        elif kind == "v":
                            scaled(lambda t: v[:, t, cols], ps).then_inc(free, 1)
                        elif kind == "vb":
                            dve.tensor_copy(v[:, :, cols], two).then_inc(free, 1)
                        elif kind in ("cq", "ckv"):
                            at_ = c_at if kind == "cq" else c_at + 512
                            scaled(lambda t: o[:, t, at_:at_ + 512], ps).then_inc(free, 1)
                        elif kind == "kr":
                            rotate(kr[:, :].unsqueeze(1), cst("cos"), cst("sin"), k, l * 2, 1, unrot, True)\
                                .then_inc(free, 1)
                        elif kind == "qr":
                            rotate(qr[:, :, :], cst("cos"), cst("sin"), k, l * 2 + 1, 4, unrot, False)\
                                .then_inc(free, 1)
                        elif kind == "z":
                            moved(dve, k, uses)
                            dve.tensor_tensor(o[:, :, cols], o[:, :, cols], act_out[:, :, :], ALU.mult)\
                                .then_inc(act_read, 1)
                        elif kind == "out":
                            dve.tensor_tensor(x[:, :, cols], x[:, :, cols], two, ALU.add).then_inc(free, 1)
                            squares(x, n)
                    elif what == "head_scores":
                        h = d["h"]
                        hh = l * HEADS + h
                        if h < DH:
                            dve.wait_ge(scores_ready, hh + 1)
                            pss = psS[:, :].rearrange("p (m n) -> p m n", m=2)
                            b_all = bias[:, h, :].unsqueeze(1).broadcast_to([P, 2, 256])
                            b_diag = bias[:, h, 128:256].unsqueeze(1).broadcast_to([P, 2, 128])
                            dve.scalar_tensor_tensor(prob[:, :, 0:256], pss[:, :, 0:256], 64 ** -0.5, b_all,
                                                     ALU.mult, ALU.add)
                            dve.scalar_tensor_tensor(prob[:, :, 256:384], pss[:, :, 256:384], 64 ** -0.5, b_diag,
                                                     ALU.mult, ALU.add)
                            sync()
                            dve.tensor_reduce(negmax[:, 0:2], prob[:, :, 0:256], AX_X, ALU.max, negate=True)
                            dve.tensor_reduce(negmax[:, 2:4], prob[:, :, 256:384], AX_X, ALU.max, negate=True)\
                                .then_inc(negmax_ready, 1)
                        else:
                            masked(hh, prob[:, 0, :], cst("causal"), 192 ** -0.5).then_inc(negmax_ready, 1)
                    elif what == "head_weights":
                        h = d["h"]
                        sync()
                        dve.wait_ge(exp_ready, l * HEADS + h + 1)
                        if h < DH:
                            dve.reciprocal(rinv[:, :], sums[:, :])
                            sync()
                            for j in (1, 3):
                                dve.tensor_scalar(rinv[:, j:j + 1], rinv[:, j:j + 1], lam[:, 5:6], None, ALU.mult)
                            sync()
                            parts = ((0, 256, 0), (256, 384, 2))
                            for a, b, j in parts:
                                dve.tensor_scalar(prob[:, 1, a:b], prob[:, 1, a:b], rinv[:, j + 1:j + 2], None, ALU.mult)
                            sync()
                            for a, b, j in parts:
                                m = dve.scalar_tensor_tensor(prob[:, 0, a:b], prob[:, 0, a:b], rinv[:, j:j + 1],
                                                             prob[:, 1, a:b], ALU.mult, ALU.add)
                            m.then_inc(weights_ready, 1)
                        else:
                            for j in (0, 2):
                                dve.reciprocal(rinv[:, j:j + 1], sums[:, j:j + 1])
                            sync()
                    elif what == "head_out":
                        h = d["h"]
                        dve.wait_ge(pv_ready, l * HEADS + h + 1)
                        pso = psO[:, 0:256].rearrange("p (t n) -> p t n", t=NT)
                        if h < DH:
                            dve.tensor_copy(o[:, :, P * h:P * h + P], pso).then_inc(head_read, 1)
                        else:
                            dve.tensor_scalar(o[:, 0, P * h:P * h + P], pso[:, 0, :], rinv[:, 2:3], None, ALU.mult)
                            dve.tensor_scalar(o[:, 1, P * h:P * h + P], pso[:, 1, :], rinv[:, 0:1], None, ALU.mult)\
                                .then_inc(head_read, 1)
                    elif what == "subln":
                        sync()
                        for t in range(NT):
                            oa = o[:, t, 0:1024]
                            dve.tensor_tensor(junk[:, :], oa, oa, ALU.mult)
                            sync()
                            dve.tensor_reduce(stat[:, 8 * t:8 * t + 8], junk[:, :].rearrange("p (h n) -> p h n", h=DH),
                                              AX_X, ALU.add)
                            sync()
                        dve.tensor_scalar(stat[:, 16:32], stat[:, 0:16], 1.0 / P, 1e-6, ALU.mult, ALU.add)\
                            .then_inc(ms_ready, 1)
                        dve.wait_ge(root_ready, l * LAYER_S + LAYER_S)
                        dve.reciprocal(stat[:, 48:64], stat[:, 32:48])
                        sync()
                        for t in range(NT):
                            oa = o[:, t, 0:1024].rearrange("p (h n) -> p h n", h=DH)
                            dve.tensor_tensor(oa, oa, stat[:, 48 + 8 * t:56 + 8 * t].unsqueeze(2).to_broadcast([P, DH, P]),
                                              ALU.mult)
                        sync()
                        for t in range(NT):
                            oa = o[:, t, 0:1024].rearrange("p (h n) -> p h n", h=DH)
                            dve.tensor_tensor(oa, oa, subg[:, :].unsqueeze(1).broadcast_to([P, DH, P]), ALU.mult)
                        sync()
                sync()

            HB = DEPTH * HEADS
            by_head = lambda a, n=SSM_P: a.rearrange("p (h n) -> p h n", n=n)
            for what, d in B2.items:
                kind = d.get("kind")
                if what == "root":
                    mean_of_quarters(1e-5 if kind == "y" else 1e-6)
                    dve.wait_ge(root_ready, S2 + {"x1": 1, "y": 3, "f": 4}[kind])
                    if kind == "y":
                        dve.reciprocal(rs[:, 2:4], stat[:, 32:34])
                    elif kind == "x1":
                        dve.reciprocal(rs[:, 0:2], stat[:, 32:34])
                    else:
                        dve.reciprocal(rs[:, 0:2], stat[:, 32:34]).then_inc(r_ready, 1)
                    sync()
                    if kind == "f":
                        make_diag(rs)
                elif what == "second_norm":
                    dve.wait_ge(gain1_loaded, 16)
                    dve.wait_ge(turned, T2 + 2)
                    for t in range(NT):
                        m = dve.scalar_tensor_tensor(x[:, t, :], x[:, t, :], rs[:, t:t + 1], gain1[:, :], ALU.mult, ALU.mult)
                    m.then_inc(final1_ready, 1)
                    for n in range(4):
                        squares(x, n)
                    mean_of_quarters(1e-6)
                    dve.wait_ge(root_ready, S2 + 2)
                    dve.reciprocal(stat[:, 48:50], stat[:, 32:34])
                    sync()
                    dve.tensor_tensor(rs[:, 0:2], rs[:, 0:2], stat[:, 48:50], ALU.mult).then_inc(r_ready, 1)
                    sync()
                    make_diag(rs)
                    dve.memset(stage[:, :, 0:TAPS - 1], 0.0)
                elif what == "spread":
                    spread(DEPTH + (1 if kind == "u" else 2))
                elif what == "turn":
                    turn_rest(kind, d["m"], T2 + d["t"])
                elif what == "evac":
                    n, k = d["n"], d["k"]
                    ps = acc[k % 2]
                    free = acc_free[k % 2]
                    two = ps[:, :].rearrange("p (t n) -> p t n", t=NT)
                    cols = slice(512 * n, 512 * n + 512)
                    if kind in ("q", "kv", "ssd_br", "xbc"):
                        sync()
                    if kind in ("q", "kv", "xbc", "dt", "attn_br", "ssd_br", "w_o"):
                        dve.wait_ge(w_used, G2 + d["g"])
                    if kind == "q":
                        rotate(q2[:, 4 * n:4 * n + 4, :], cos2[:, :], sin2[:, :], k, DEPTH * 2 + n, 4, attn[:, 0, :], True)\
                            .then_inc(free, 1)
                    elif kind == "kv":
                        for t in range(NT):
                            dve.tensor_scalar(v2[:, t, :], ps[:, 512 + 256 * t:768 + 256 * t], rs[:, t:t + 1], None, ALU.mult)
                        rotate(k2[:, :, :], cos2[:, :], sin2[:, :], k, DEPTH * 2 + 2, 2, attn[:, 0, :], True)\
                            .then_inc(free, 1)
                    elif kind == "xbc":
                        dve.tensor_tensor(stage[:, :, TAPS - 1:], chunks_of(ps, 4), by_token(4), ALU.mult).then_inc(free, 1)
                        sync()
                        if n >= 1:
                            dve.wait_ge(conv_done, n)
                        if n >= 3:
                            dve.wait_ge(back_ready, n - 1)
                        for tap in range(TAPS):
                            for j in range(4):
                                w = par("conv_w", (4 * n + j) * TAPS + tap, (4 * n + j) * TAPS + tap + 1)
                                a = stage[:, j, tap:tap + S]
                                if tap == 0:
                                    m = dve.tensor_scalar(conv[:, j, :], a, w, par("conv_b", 4 * n + j, 4 * n + j + 1),
                                                          ALU.mult, ALU.add)
                                else:
                                    m = dve.scalar_tensor_tensor(conv[:, j, :], a, w, conv[:, j, :], ALU.mult, ALU.add)
                            if tap < TAPS - 1:
                                sync()
                        m.then_inc(conv_sum, 1)
                    elif kind == "dt":
                        for t in range(NT):
                            m = dve.scalar_tensor_tensor(dts[:, 0, SSM_H * t:SSM_H * t + SSM_H], two[:, t, 0:SSM_H],
                                                         rs[:, t:t + 1], par("dt_bias"), ALU.mult, ALU.add)
                        m.then_inc(free, 1)
                        sync()
                        dve.tensor_scalar(dts[:, 1, :], dts[:, 0, :], -1.0, None, ALU.mult)
                        sync()
                        dve.tensor_tensor(dts[:, 1, :], dts[:, 1, :], dts[:, 0, :], ALU.min).then_inc(dt_step, 1)
                        dve.wait_ge(dt_act, 1)
                        dve.tensor_scalar(dts[:, 3, :], dts[:, 2, :], 1.0, None, ALU.add).then_inc(dt_step, 1)
                        sync()
                        dve.tensor_scalar(dts[:, 9, :], dts[:, 3, :], 1.0, None, ALU.subtract)
                        sync()
                        dve.tensor_scalar(dts[:, 10, :], dts[:, 9, :], 1e-30, None, ALU.max)
                        dve.tensor_scalar(dts[:, 11, :], dts[:, 9, :], 0.0, None, ALU.is_equal)
                        sync()
                        dve.reciprocal(dts[:, 10, :], dts[:, 10, :])
                        dve.tensor_tensor(dts[:, 11, :], dts[:, 11, :], dts[:, 2, :], ALU.mult)
                        dve.wait_ge(dt_act, 2)
                        dve.tensor_tensor(dts[:, 9, :], dts[:, 4, :], dts[:, 2, :], ALU.mult)
                        sync()
                        dve.tensor_tensor(dts[:, 9, :], dts[:, 9, :], dts[:, 10, :], ALU.mult)
                        sync()
                        dve.tensor_tensor(dts[:, 9, :], dts[:, 9, :], dts[:, 11, :], ALU.add)
                        sync()
                        dve.scalar_tensor_tensor(dts[:, 5, :], dts[:, 0, :], 0.0, dts[:, 9, :], ALU.max, ALU.add)
                        sync()
                        dve.scalar_tensor_tensor(dts[:, 6, :].rearrange("p (t n) -> p t n", t=NT),
                                                 dts[:, 5, :].rearrange("p (t n) -> p t n", t=NT), -1.0,
                                                 dts[:, 8, 0:SSM_H].unsqueeze(1).broadcast_to([P, NT, SSM_H]),
                                                 ALU.mult, ALU.mult).then_inc(dt_step, 1)
                    elif kind == "z":
                        moved(dve, K2 + k)
                        dve.tensor_tensor(ys[:, :, cols], ys[:, :, cols], act_out[:, :, :], ALU.mult).then_inc(act_read, 1)
                        squares(ys, n)
                    elif kind == "attn_br":
                        dve.tensor_tensor(ga[:, :, cols], ga[:, :, cols], two, ALU.mult).then_inc(free, 1)
                    elif kind == "ssd_br":
                        for t in range(NT):
                            m = dve.scalar_tensor_tensor(act_out[:, t, :], two[:, t, :], rs[:, 2 + t:3 + t], x[:, t, cols],
                                                         ALU.mult, ALU.mult)
                        if n == 3:
                            m.then_inc(merged_free, 1)
                        sync()
                        dve.tensor_tensor(ga[:, :, cols], ga[:, :, cols], act_out[:, :, :], ALU.add).then_inc(free, 1)
                    elif kind == "w_o":
                        if n == 0:
                            dve.wait_ge(refetched, 16)
                        dve.tensor_tensor(x[:, :, cols], x[:, :, cols], two, ALU.add).then_inc(free, 1)
                        squares(x, n)
                elif what == "back":
                    n, k = d["n"], d["k"]
                    dve.wait_ge(back_ready, n + 1)
                    if n == 0:
                        m = dve.tensor_copy(bt[:, :], acc[k % 2][:, 0:512])
                    else:
                        m = dve.tensor_copy(ys[:, :, 512 * (n - 1):512 * n],
                                            acc[k % 2][:, :].rearrange("p (t n) -> p t n", t=NT))
                    m.then_inc(acc_free[k % 2], 1)
                elif what == "head_scores":
                    if d["h"] == 0:
                        dve.wait_ge(near_loaded, 16)
                    dve.wait_ge(scores_ready, HB + d["h"] + 1)
                    dve.scalar_tensor_tensor(prob2[:, :], psS[:, 0:384], HD ** -0.5, cst("causal"), ALU.mult, ALU.add)
                    sync()
                    dve.tensor_reduce(negmax[:, 1:2], prob2[:, 0:256], AX_X, ALU.max)
                    dve.tensor_reduce(negmax[:, 3:4], prob2[:, 256:384], AX_X, ALU.max)
                    sync()
                    sink = par("sinks", d["h"], d["h"] + 1)
                    dve.tensor_scalar(negmax[:, 0:1], negmax[:, 1:2], sink, -1.0, ALU.max, ALU.mult)
                    dve.tensor_scalar(negmax[:, 2:3], negmax[:, 3:4], sink, -1.0, ALU.max, ALU.mult)\
                        .then_inc(negmax_ready, 1)
                elif what == "head_weights":
                    dve.wait_ge(exp_ready, HB + d["h"] + 1)
                    sync()
                    for j in (0, 2):
                        dve.tensor_tensor(rinv[:, j:j + 1], sums[:, j:j + 1], sums[:, j + 1:j + 2], ALU.add)
                    sync()
                    for j in (0, 2):
                        dve.reciprocal(rinv[:, j:j + 1], rinv[:, j:j + 1])
                    sync()
                elif what == "head_out":
                    h = d["h"]
                    dve.wait_ge(pv_ready, HB + h + 1)
                    dve.tensor_scalar(attn[:, 0, HD * h:HD * h + HD], psO[:, 0:HD], rinv[:, 2:3], None, ALU.mult)
                    dve.tensor_scalar(attn[:, 1, HD * h:HD * h + HD], psO[:, HD:2 * HD], rinv[:, 0:1], None, ALU.mult)\
                        .then_inc(head_read, 1)
                elif what == "decay":
                    dve.wait_ge(acs_ready, 1)
                    dve.tensor_copy(dts[:, 7, :], psO[:, 0:64])
                    sync()
                    dve.tensor_tensor(dts[:, 10, 0:32], psO[:, 64:96], dts[:, 7, 0:32], ALU.subtract)
                    dve.tensor_copy(dts[:, 10, 32:64], psO[:, 32:64]).then_inc(decay_in, 1)
                    for c in range(NT):
                        dve.tensor_tensor(by_head(xd[:, c, :]), by_head(ys[:, c, :]),
                                          dts[:, 5, 32 * c:32 * c + 32].unsqueeze(2).to_broadcast([P, SSM_H, SSM_P]),
                                          ALU.mult)
                    sync()
                    for c in range(NT):
                        dve.tensor_tensor(by_head(ys[:, c, :]), by_head(ys[:, c, :]),
                                          par("d_skip").unsqueeze(2).to_broadcast([P, SSM_H, SSM_P]), ALU.mult)
                    dve.wait_ge(decay_ready, 1)
                    sync()
                elif what == "group_cb":
                    grp = d["grp"]
                    dve.wait_ge(cb_ready, grp + 1)
                    dve.tensor_tensor(cbm[:, :, :], psS[:, 0:256].rearrange("p (c n) -> p c n", c=NT),
                                      tri.unsqueeze(1).broadcast_to([P, NT, P]), ALU.mult).then_inc(cb_read, 1)
                    wait(dve, state_ps, grp)
                    dve.tensor_tensor(by_head(xw[:, :]), by_head(xd[:, 0, 512 * grp:512 * grp + 512]),
                                      dts[:, 9, 8 * grp:8 * grp + 8].unsqueeze(2).to_broadcast([P, 8, SSM_P]),
                                      ALU.mult).then_inc(xw_ready, 1)
                elif what == "group_off":
                    grp = d["grp"]
                    dve.wait_ge(off_ready, grp + 1)
                    dve.tensor_tensor(by_head(act_out[:, 0, :]), by_head(psS[:, 512:1024]),
                                      dts[:, 9, 32 + 8 * grp:40 + 8 * grp].unsqueeze(2).to_broadcast([P, 8, SSM_P]),
                                      ALU.mult).then_inc(off_read, 1)
                    sync()
                    y1 = ys[:, 1, 512 * grp:512 * grp + 512]
                    dve.tensor_tensor(y1, y1, act_out[:, 0, :], ALU.add)
                    sync()
                elif what == "unit_rows":
                    u, c, h0 = d["u"], d["c"], d["h0"]
                    dve.wait_ge(rows_ready, u + 1)
                    if u >= 2:
                        dve.wait_ge(diag_out, u - 1)
                    for j in range(4):
                        col = 32 * c + h0 + j
                        m = dve.tensor_scalar(decay[:, u % 2, P * j:P * j + P], psT[:, P * j:P * j + P],
                                              dts[:, 7, col:col + 1], 0.0, ALU.subtract, ALU.min)
                    m.then_inc(diff_ready, 1)
                elif what == "unit_mask":
                    u, c = d["u"], d["c"]
                    dve.wait_ge(unit_exp, u + 1)
                    dd = decay[:, u % 2, :].rearrange("p (j n) -> p j n", j=4)
                    dve.tensor_tensor(dd, dd, cbm[:, c, :].unsqueeze(1).broadcast_to([P, 4, P]), ALU.mult)\
                        .then_inc(unit_ready, 1)
                elif what == "unit_out":
                    u, c, h0 = d["u"], d["c"], d["h0"]
                    dve.wait_ge(diag_out, u + 1)
                    yy = ys[:, c, 64 * h0:64 * h0 + 256]
                    dve.tensor_tensor(yy, yy, psO[:, 0:256], ALU.add).then_inc(diag_read, 1)
                    if u == 15:
                        sync()

            flat = act_out[:, :, :].rearrange("p t n -> p (t n)")
            for f in FFN_PARTS:
                with dve.Fori(0, f["hbs"]) as i:
                    sync()
                    dve.wait_ge(w_used, 16 * i + (f["g_up"] + 8))
                    dve.tensor_tensor(chunks_of(flat, 4), chunks_of(acc[GATE], 4), by_token(4), ALU.mult)\
                        .then_inc(acc_free[GATE], 1)
                    dve.wait_ge(w_used, 16 * i + (f["g_up"] + 16))
                    dve.tensor_tensor(chunks_of(junk, 4), chunks_of(acc[UP], 4), by_token(4), ALU.mult)\
                        .then_inc(acc_free[UP], 1)
                    sync()
                    dve.wait_ge(gate_done, i + (f["done"] + 1))
                    dve.tensor_tensor(flat, flat, junk[:, :], ALU.mult).then_inc(hid_ready, 1)
                    sync()
                    dve.wait_ge(hid_hi, i + (f["done"] + 1))
                    dve.tensor_tensor(fl[:, bass.ds(4 * i, 4), :].rearrange("p c s -> p (c s)"), flat,
                                      fh[:, bass.ds(4 * i, 4), :].rearrange("p c s -> p (c s)").bitcast(F32),
                                      ALU.subtract).then_inc(hid_lo, 1)
                per = 2 * f["hbs"]
                if f is FFN_PARTS[0]:
                    dve.wait_ge(p_hi, 1)
                    dve.tensor_tensor(pl[:, :, :], praw[:, :, :], ph[:, :, :].bitcast(F32), ALU.subtract).then_inc(p_lo, 1)
                if f is not FFN_PARTS[-1]:
                    with dve.Fori(0, 2) as i:
                        for side in range(2):
                            k = f["k_dn"] + side
                            xc = x[:, :, bass.ds(1024 * i + 512 * side, 512)]
                            dve.wait_ge(w_used, 2 * per * i + (f["g_dn"] + per * (side + 1)))
                            dve.tensor_tensor(xc, xc, acc[k % 2][:, :].rearrange("p (t n) -> p t n", t=NT),
                                              ALU.add).then_inc(acc_free[k % 2], 1)
                    sync()
            for what, d in DOWN.items:
                if what == "turn":
                    turn_rest("ple", d["m"], T_DOWN + d["t"])
                elif what == "evac":
                    n, k = d["n"], K_DOWN + d["k"]
                    cols = slice(512 * n, 512 * n + 512)
                    dve.wait_ge(w_used, G_DOWN + d["g"])
                    dve.tensor_tensor(x[:, :, cols], x[:, :, cols], acc[k % 2][:, :].rearrange("p (t n) -> p t n", t=NT),
                                      ALU.add).then_inc(acc_free[k % 2], 1)
                    squares(x, n)

            def last_gain(n):
                sync()
                for t in range(NT):
                    xc = x[:, t, 512 * n:512 * n + 512]
                    dve.tensor_tensor(xc, xc, gain2[:, 512 * n:512 * n + 512], ALU.mult)

            for what, d in PLE.items:
                if what == "root":
                    mean_of_quarters(1e-6)
                    dve.wait_ge(root_ready, S2 + 5)
                    dve.reciprocal(rs[:, 0:2], stat[:, 32:34]).then_inc(r_ready, 1)
                elif what == "turn":
                    turn_rest("ple", d["m"], T_PLE + d["t"])
                elif what == "evac" and d["kind"] == "proj":
                    n, k = d["n"], K_PLE + d["k"]
                    cols = slice(512 * n, 512 * n + 512)
                    if n:
                        last_gain(n - 1)
                    sync()
                    moved(dve, k - 1)
                    dve.wait_ge(w_used, G_PLE + d["g"])
                    dve.tensor_tensor(flat, flat, acc[k % 2][:, :], ALU.mult).then_inc(acc_free[k % 2], 1)
                    sync()
                    dve.tensor_tensor(x[:, :, cols], x[:, :, cols], act_out[:, :, :], ALU.add).then_inc(act_read, 1)
                    squares(x, n)
                    if n == 0:
                        dve.wait_ge(gain2_loaded, 16)
            mean_of_quarters(1e-6)
            last_gain(3)
            dve.wait_ge(root_ready, S2 + 6)
            dve.reciprocal(rs[:, 0:2], stat[:, 32:34]).then_inc(r_ready, 1)
            sync()
            dve.tensor_scalar(x[:, 1, :], x[:, 1, :], rs[:, 1:2], None, ALU.mult).then_inc(result_ready[1], 1)


def _pack(table, width, parts, rows=P):
    a = np.zeros((rows, width), np.float32)
    for name, v in parts.items():
        at, w = table[name]
        a[:, at:at + w] = v
    return a


def _columns(v):
    return np.asarray(v).reshape(-1, P).T


def _granules(w, cols, chunks=2):
    w = w[:, cols]
    k, n = w.shape
    return w.reshape(k // P // chunks, chunks, P, n).transpose(0, 2, 1, 3).reshape(-1, P, chunks * n)


def _constants():
    i = np.arange(P)
    rot = np.zeros((P, P), np.float32)
    for d in range(P):
        if d % 64 < 32:
            rot[d + 32, d] = -1.0
        else:
            rot[d - 32, d] = 1.0
    diag = np.where(i[None, :] > i[:, None], NEG, 0.0)
    none = np.zeros((P, P))
    near = np.where(i[None, :] > i[:, None], 0.0, NEG)
    inv = (1.0 / (np.float32(10000.0) ** (np.arange(0, 64, 2, dtype=np.float32) / np.float32(64)))).astype(np.float32)
    ang = (np.arange(S, dtype=np.float32)[None, :] * inv[i % 32][:, None]).astype(np.float32).astype(np.float64)
    return _pack(CONST_COLS, CONST_W, dict(
        ident=np.eye(P), rot=rot, tri=(i[:, None] <= i[None, :]), flip=np.eye(P)[::-1],
        causal=np.concatenate([none, diag, diag], 1), near=near,
        cos=np.cos(ang), sin=np.sin(ang)))


def _bias_onehot():
    dist = 255 - np.arange(383)
    n = np.maximum(dist, 0)
    nf = np.maximum(n, 1).astype(np.float32)
    large = 16 + (np.log(nf / np.float32(16)) / np.float32(math.log(8)) * np.float32(16)).astype(np.int32)
    bucket = np.where(n < 16, n, np.minimum(large, 31))
    a = np.zeros((33, 384), np.float32)
    a[bucket[dist >= 0], np.nonzero(dist >= 0)[0]] = 1.0
    a[32, :383] = np.where(dist < 0, NEG, 0.0)
    return a


def _weights(i):
    blocks = []
    add = lambda w, cols, chunks=2: blocks.append(_granules(w, cols, chunks))
    span = lambda a, n=512: np.arange(a, a + n)
    for l in range(DEPTH):
        w = i["w_in"][l]
        for at in (0, 512, 1024, 1536, 2048, 2560, 4096, 4608):
            add(w, span(at))
        add(w, np.concatenate([span(5120, 64)] * 2), 8)
        uq, ukv = i["w_uq"][l], i["w_ukv"][l]
        for half in range(2):
            add(uq, np.concatenate([span(192 * h, 128) for h in range(4 * half, 4 * half + 4)]))
        add(uq, np.concatenate([span(192 * h + 128, 64) for h in range(MH)]))
        for off in (0, 128):
            for half in range(2):
                add(ukv, np.concatenate([span(256 * h + off, 128) for h in range(4 * half, 4 * half + 4)]))
        for at in (3072, 3584, 5184, 5696):
            add(w, span(at))
        for n in range(4):
            add(i["w_out"][l], span(512 * n))
    w = i["w_in_2"][0]
    for at in (0, 512, 1024, 5632, 6144, 3584, 4096, 4608, 5120):
        add(w, span(at))
    dt = np.zeros((D, 64), np.float32)
    dt[:, :SSM_H] = w[:, 6656:6688]
    add(dt, span(0, 64), 16)
    for first in (6688, 8736, 1536):
        for n in range(4):
            add(w, span(first + 512 * n))
    for name in ("w_attn_br_2", "w_ssd_br_2", "w_o_2"):
        for n in range(4):
            add(i[name][0], span(512 * n))
    for f in FFN_PARTS:
        a, b = f["done"], f["done"] + f["hbs"]
        for hb in range(a, b):
            add(i["w_gate_2"][0], span(512 * hb))
            add(i["w_up_2"][0], span(512 * hb))
        for n in range(4):
            add(i["w_down_2"][0][512 * a:512 * b], span(512 * n))
    for n in range(4):
        add(i["w_ple_gate_2"][0], span(512 * n))
        add(i["w_ple_proj_2"][0], span(512 * n))
    return np.concatenate(blocks, 0)


def kernel(**inputs):
    import concourse.bacc as bacc
    from concourse.bass_utils import run_bass_kernel_spmd

    i = {k: np.asarray(v) for k, v in inputs.items()}
    row = lambda v: np.broadcast_to(np.asarray(v).reshape(1, -1), (P, np.asarray(v).size))
    layer_small = []
    for l in range(DEPTH):
        lambda_init = 0.8 - 0.6 * math.exp(-0.3 * l)
        layer_small.append(_pack(LAYER_COLS, LAYER_W, {
            "norm": _columns(i["norm_g"][l]),
            "next_norm": _columns(i["norm_g"][l + 1]) if l + 1 < DEPTH else 0.0, "q_norm": _columns(i["mla_q_norm_g"][l]),
            "kv_norm": _columns(i["mla_kv_norm_g"][l]), "lam_init": lambda_init, "one_minus": 1.0 - lambda_init,
            "lambda": row(i["diff_lambda"][l]), "subln": row(i["diff_subln_g"][l])}))
    order = np.concatenate([np.arange(2048, 3072), np.arange(0, 2048)])
    conv_w = i["conv_w_2"][0][:, order].reshape(TAPS, 24, P).transpose(2, 1, 0).reshape(P, 24 * TAPS)
    inv = (np.float32(10000.0) ** (-np.arange(32, dtype=np.float32) * np.float32(2.0) / np.float32(64))).astype(np.float32)
    block2_small = _pack(BLOCK2_COLS, BLOCK2_W, {
        "final1": _columns(i["final_norm_g"]),
        "mix": _columns(i["g_mix_2"][0]), "ffn": _columns(i["g_ffn_2"][0]), "ple": _columns(i["g_ple_2"][0]),
        "ssd": _columns(i["g_ssd_2"][0]), "conv_w": conv_w, "conv_b": _columns(i["conv_b_2"][0][order]),
        "dt_bias": row(i["dt_bias_2"][0]), "a_log": row(i["a_log_2"][0]), "d_skip": row(i["d_skip_2"][0]),
        "sinks": row(i["sinks_2"][0]), "inv_freq": inv[np.arange(P) % 32][:, None]})
    bias_rows = np.concatenate([i["rel_bias_table"], np.ones((1, DH), np.float32)], 0)
    arrays = {
        "wstream": _weights(i), "x_in": np.ascontiguousarray(i["x"][0]),
        "p_in": np.ascontiguousarray(i["p_2"][0, 0].T.reshape(2, P, S).transpose(1, 0, 2)),
        "positions": np.ascontiguousarray(i["positions_2"].reshape(S)),
        "layer_small": np.stack(layer_small), "block2_small": block2_small, "const_in": _constants(),
        "bias_rows": bias_rows, "bias_onehot": _bias_onehot(),
        "gain_final1": np.ascontiguousarray(row(i["final_norm_g"])),
        "gain_final2": np.ascontiguousarray(row(i["g_final_2"])),
    }
    nc = bacc.Bacc("TRN2", target_bir_lowering=False, num_devices=1)
    args = [nc.dram_tensor(n, a.shape, mybir.dt.from_np(a.dtype), kind="ExternalInput").ap()
            for n, a in arrays.items()]
    args.append(nc.dram_tensor("out", (S, D), F32, kind="ExternalOutput").ap())
    build(nc, *args)
    r = run_bass_kernel_spmd(nc, [arrays], core_ids=[0])
    return r.results[0]["out"].reshape(1, S, D)
```

```python
import math
from contextlib import ExitStack

import concourse.bass as bass
import numpy as np
from concourse import mybir

F32 = mybir.dt.float32
F32R = mybir.dt.float32r
I32 = mybir.dt.int32
ALU = mybir.AluOpType
ACT = mybir.ActivationFunctionType
AX_X = mybir.AxisListType.X

P = 128
S = 256
NT = S // P
D = 2048
DC = D // P
DEPTH = 2
GW = 1024
RING = 4
LOOK = RING
NEG = -1e30

DH, MH = 8, 8
SWA_H, KV_H, HD = 16, 4, 64
SSM_H, SSM_G, SSM_N, SSM_P = 32, 4, 128, 64
TAPS = 4
FFN = 5632
HIDDEN_BLOCKS = FFN // 512
PARTS = (4, 4, 3)
PAIRS = DC // 2

LAYER_COLS = {}
BLOCK2_COLS = {}
CONST_COLS = {}


def _lay(table, widths):
    at = 0
    for name, w in widths:
        table[name] = (at, w)
        at += w
    return at


LAYER_W = _lay(LAYER_COLS, [("norm", DC), ("next_norm", DC), ("q_norm", 4), ("kv_norm", 4), ("lam_init", 1), ("one_minus", 1),
                            ("lambda", 256), ("subln", 128)])
BLOCK2_W = _lay(BLOCK2_COLS, [("final1", DC), ("mix", DC), ("ffn", DC), ("ple", DC), ("ssd", DC), ("conv_w", 24 * TAPS),
                              ("conv_b", 24), ("dt_bias", SSM_H), ("a_log", SSM_H), ("d_skip", SSM_H),
                              ("sinks", SWA_H), ("inv_freq", 1)])
CONST_W = _lay(CONST_COLS, [("ident", P), ("rot", P), ("tri", P), ("flip", P), ("causal", 384),
                            ("cos", S), ("sin", S), ("near", P)])
RESIDENT = CONST_W - P
LAYER_OWN = LAYER_COLS["lambda"][0]


class Plan:

    def __init__(self):
        self.items, self.later = [], []
        self.g = self.k = self.t = 0

    def item(self, what, **d):
        self.items.append((what, d))

    def at(self, when, what, **d):
        self.later.append((when, what, d))
        self.later.sort(key=lambda x: x[0])

    def flush(self, upto=10 ** 9):
        while self.later and self.later[0][0] <= upto:
            _, what, d = self.later.pop(0)
            if what == "turn":
                self.turn(**d)
            else:
                self.item(what, **d)

    def turn(self, kind, m):
        self.item("turn", kind=kind, m=m, t=self.t)
        self.t += 1

    def product(self, kind, n, granules, evac_after=0, rotated=()):
        d = dict(kind=kind, n=n, of=granules, k=self.k)
        end = self.g + granules
        for i in range(granules):
            self.item("gran", i=i, g=self.g, **d)
            self.g += 1
            self.flush(self.g)
        if evac_after:
            self.at(end + evac_after, "evac", g=end, **d)
        else:
            self.item("evac", g=end, **d)
        if kind in rotated:
            self.at(end + evac_after + 1, "swap", **d)
        self.k += 1

    def heads(self, first, count, spacing, start):
        for h in range(first, first + count + 1):
            gap = start + spacing * (h - first)
            if h > first:
                self.at(gap, "head_turn", h=h - 1)
            if h < first + count:
                self.at(gap, "head_scores", h=h)
            if h > first:
                self.at(gap + 1, "head_out", h=h - 1)
            if h < first + count:
                self.at(gap + 1, "head_exp", h=h)
                self.at(gap + 1, "head_weights", h=h)


def layer_plan():
    p = Plan()
    p.item("root", kind="x")
    p.at(4, "inverse", kind="x")
    p.at(2, "turn", kind="x_last", m=6)
    p.at(4, "turn", kind="x_last", m=7)
    p.at(7, "spread", kind="x")
    for kind in ("q", "k"):
        for n in range(2):
            p.product(kind, n, 8)
    p.product("v", 0, 8)
    p.heads(0, DH, 3, p.g + 1)
    p.product("v", 1, 8)
    for c, kind in enumerate(("cq", "ckv")):
        p.product(kind, 0, 8)
        p.item("root", kind=kind)
        p.at(p.g + 1, "inverse", kind=kind)
    p.product("kr", 0, 2, rotated=("kr",))
    p.at(p.g + 2, "root", kind="subln")
    for j, (kind, m) in enumerate((("cq", 0), ("cq", 1), ("ckv", 0), ("ckv", 1))):
        p.at(p.g + 2 + j, "turn", kind=kind, m=m)
    p.at(p.g + 6, "inverse", kind="subln")
    p.product("z", 0, 8)
    for n in range(2):
        p.product("qn", n, 2)
    p.product("qr", 0, 2, rotated=("qr",))
    for n in range(2):
        p.product("kn", n, 2)
    for n in range(2):
        p.product("vb", n, 2)
    p.at(p.g + 2, "turn", kind="o", m=0)
    p.at(p.g + 4, "turn", kind="o", m=1)
    p.heads(DH, MH, 2, p.g + 1)
    for n in range(1, 4):
        p.product("z", n, 8)
        p.at(p.g + 3, "turn", kind="o", m=2 * n)
        p.at(p.g + 5, "turn", kind="o", m=2 * n + 1)
    for n in range(4):
        p.product("out", n, 8)
        if n < 3:
            p.at(p.g + 2, "turn", kind="x_next", m=2 * n)
            p.at(p.g + 4, "turn", kind="x_next", m=2 * n + 1)
    assert not p.later
    return p


def block2_plan():
    p = Plan()
    p.item("root", kind="x1")
    p.at(1, "inverse", kind="x1")
    p.at(1, "turn", kind="u_last", m=6)
    p.at(3, "turn", kind="u_last", m=7)
    p.at(4, "second_norm")
    p.at(8, "inverse", kind="u")
    p.at(9, "spread", kind="u")
    p.product("q", 0, 8, evac_after=2, rotated=("q",))
    p.product("q", 1, 8, rotated=("q",))
    p.product("kv", 0, 8, rotated=("kv",))
    p.at(p.g + 2, "key_halves")
    p.heads(0, SWA_H, 2, p.g + 5)
    b = 0
    for n in range(6):
        p.product("xbc", n, 8)
        for tap in range(TAPS):
            p.at(p.g + tap, "tap", n=n, tap=tap)
        p.at(p.g + TAPS, "conv_silu", n=n)
        for c in range((1, 0, 2, 2, 2, 2)[n]):
            p.at(p.g + TAPS + 2 + c, "back", n=n, c=c, b=b)
            b += 1
    p.product("dt", 0, 1)
    for after, what in ((1, "dt_turn"), (2, "dt_exp"), (3, "dt_u"), (4, "dt_log"), (5, "dt_end"), (8, "decay"),
                        (9, "decay_exp")):
        p.at(p.g + after, what)
    gap = p.g + 12
    for grp in range(SSM_G):
        p.at(gap, "group_cb", grp=grp)
        p.at(gap + 1, "group_state", grp=grp)
        p.at(gap + 2, "group_off", grp=grp)
        gap += 2
        for c in range(NT):
            for half in range(2):
                u = (grp * NT + c) * 2 + half
                d = dict(u=u, grp=grp, c=c, h0=grp * 8 + half * 4)
                p.at(gap, "unit_rows", **d)
                p.at(gap + 1, "unit_mask", **d)
                p.at(gap + 3, "unit_out", **d)
                gap += 2
    for n in range(4):
        p.product("ga", n, 8)
    for n in range(4):
        p.product("gs", n, 8)
    p.flush()
    for n in range(4):
        if n < 2:
            p.at(p.g + 6, "turn", kind="attn", m=2 * n)
            p.at(p.g + 7, "turn", kind="attn", m=2 * n + 1)
        p.product("z", n, 8)
        p.at(p.g + 3, "turn", kind="y", m=2 * n)
        p.at(p.g + 5, "turn", kind="y", m=2 * n + 1)
    p.item("root", kind="y")
    p.at(p.g + 1, "inverse", kind="y")
    for n in range(4):
        p.product("attn_br", n, 4)
    p.flush()
    for n in range(4):
        p.product("ssd_br", n, 8)
        p.at(p.g + 2, "turn", kind="merged", m=2 * n)
        p.at(p.g + 4, "turn", kind="merged", m=2 * n + 1)
    for n in range(4):
        p.product("w_o", n, 8)
        if n < 3:
            p.at(p.g + 2, "turn", kind="f", m=2 * n)
            p.at(p.g + 4, "turn", kind="f", m=2 * n + 1)
    p.item("root", kind="f")
    p.turn("f", 6)
    p.item("inverse", kind="f")
    p.turn("f", 7)
    p.item("spread", kind="f")
    assert not p.later
    return p


def down_plan():
    p = Plan()
    for n in range(4):
        p.product("down", n, 2 * PARTS[-1])
        if n < 3:
            p.at(p.g + 2, "turn", kind="ple", m=2 * n)
            p.at(p.g + 4, "turn", kind="ple", m=2 * n + 1)
    return p


def embedding_plan():
    p = Plan()
    p.item("root", kind="ple")
    p.at(1, "inverse", kind="ple")
    p.at(1, "turn", kind="ple", m=6)
    p.at(3, "turn", kind="ple", m=7)
    for n in range(4):
        p.product("gate", n, 8)
        p.product("proj", n, 1)
    return p


def freed(pair, k):
    return (k - pair) // 2 + 1


LAYER, B2, DOWN, PLE = layer_plan(), block2_plan(), down_plan(), embedding_plan()
LAYER_STEP = {(d["kind"], d["n"]): d["k"] for what, d in LAYER.items if what == "evac"}
BACKS = sum(what == "back" for what, d in B2.items)
PRO_T = 6
G2 = DEPTH * LAYER.g
K2 = DEPTH * LAYER.k
T2 = PRO_T + DEPTH * LAYER.t
LAYER_S = 4
S2 = DEPTH * LAYER_S
G_FFN, K_FFN = G2 + B2.g, K2 + B2.k
FFN_PARTS = []
_g, _k, _b = G_FFN, K_FFN, 0
for _hbs in PARTS:
    FFN_PARTS.append(dict(g_up=_g, k_up=_k, hbs=_hbs, g_dn=_g + 16 * _hbs, k_dn=_k + 2 * _hbs, done=_b))
    _g += 16 * _hbs + 8 * _hbs
    _k += 2 * _hbs + 4
    _b += _hbs
G_PLE, K_PLE = _g, _k
G_ALL = G_PLE + PLE.g
T_DOWN = T2 + B2.t
T_PLE = T_DOWN + DOWN.t
assert LAYER.g % RING == 0 and LAYER.k % 2 == 0
HEADS = DH + MH
B2_STEP = {(d["kind"], d["n"]): d["k"] for what, d in B2.items if what == "evac"}
TURN = {(name, d["kind"], d["m"]): d["t"] for name, plan in (("layer", LAYER), ("block2", B2))
        for what, d in plan.items if what == "turn"}
DG2 = DEPTH
ROOT = {"x": 0, "cq": 1, "ckv": 2, "subln": 3,
        "x1": 0, "u": 1, "y": 2, "f": 3, "ple": 4}
G_DOWN, K_DOWN = FFN_PARTS[-1]["g_dn"], FFN_PARTS[-1]["k_dn"]
GATE, UP = K_FFN % 2, 1 - K_FFN % 2
assert all(p["k_up"] % 2 == GATE for p in FFN_PARTS) and K_PLE % 2 == GATE


def build(nc, wstream, x_in, p_in, positions, layer_small, block2_small, const_in, bias_rows, bias_onehot,
          gain_final1, gain_final2, out):
    rev = nc.dram_tensor("bias_by_distance", (DH, 384), F32, kind="Internal")
    spill = nc.dram_tensor("residual_spill", (S, D), F32, kind="Internal").ap()

    place = {"at": (nc.sbuf_base + 31) // 32 * 32}

    def sb(name, shape, dt=F32, at=None):
        size = 4 * int(np.prod(shape[1:]))
        where = place["at"] if at is None else at
        if at is None:
            place["at"] += (size + 31) // 32 * 32
        assert where + size <= 229344, name
        return nc.alloc_sbuf_tensor_at(name, shape, dt, offset=where)

    ctx = ExitStack()
    with ctx:
        def psum(name, cols):
            return ctx.enter_context(nc.psum_tensor(name, [P, cols], F32))

        def sem(name):
            return ctx.enter_context(nc.semaphore(name))

        raw = sb("raw", [P, RING, GW])
        whi = sb("whi", [P, RING, GW], F32R)
        wlo = sb("wlo", [P, RING, GW], F32R)
        x = sb("x", [P, NT, D])
        xh = sb("xh", [P, DC, S], F32R)
        xl = sb("xl", [P, DC, S], F32R)
        const = sb("const", [P, RESIDENT])
        cos2 = sb("cos2", [P, S])
        sin2 = sb("sin2", [P, S])
        lsmall = sb("lsmall", [P, DEPTH, LAYER_W])
        lcur = sb("lcur", [P, LAYER_OWN])
        bsmall = sb("bsmall", [P, BLOCK2_W])
        diag = sb("diag", [P, NT, P])
        act_out = sb("act_out", [P, NT, 512])
        rs = sb("rs", [P, 8])
        rbc = sb("rbc", [P, 1, S])
        stat = sb("stat", [P, 64])
        lam = sb("lam", [P, 8])
        subg = sb("subg", [P, P])
        negmax = sb("negmax", [P, 4])
        sums = sb("sums", [P, 4])
        rinv = sb("rinv", [P, 4])
        region = place["at"]

        K = 1024
        at = lambda kib: region + kib * K
        bh = sb("bh", [P, DC, S], F32R, at=at(16))
        bl = sb("bl", [P, DC, S], F32R, at=at(32))
        bias = sb("bias", [P, DH, 256], at=at(0))
        v = sb("v", [P, NT, 1024], at=at(8))
        ch = sb("ch", [P, 8, S], F32R, at=at(16))
        cl = sb("cl", [P, 8, S], F32R, at=at(32))
        qT = sb("qT", [P, 8, S], at=at(24))
        kT = sb("kT", [P, 8, S], at=at(40))
        qr = sb("qr", [P, 4, S], at=at(48))
        kr = sb("kr", [P, S], at=at(52))
        o = sb("o", [P, NT, 2 * 1024], at=at(53))
        c_at = 1024
        unrot = sb("unrot", [P, 1024], at=at(69))
        prob = sb("prob", [P, 2, 384], at=at(73))
        probT = sb("probT", [P, 384], at=at(76))
        pos_i = sb("pos_i", [P, S], I32, at=at(73))
        pos_t = sb("pos_t", [P, 3, S], at=at(74))
        gain1 = sb("gain1", [P, D], at=at(80))
        junk = sb("junk", [P, 1024], at=at(88))

        xd = sb("xd", [P, NT, D], at=at(0))
        q2 = sb("q2", [P, 8, S], at=at(0))
        kk2 = sb("kk2", [P, KV_H, S], at=at(8))
        k2 = sb("k2", [P, 2, S], at=at(12))
        v2 = sb("v2", [P, NT, 256], at=at(14))
        ah = sb("ah", [P, 8, S], F32R, at=at(0))
        al = sb("al", [P, 8, S], F32R, at=at(8))
        bcT = sb("bcT", [P, 8, S], at=at(16))
        stage = sb("stage", [P, 4, S + TAPS - 1], at=at(24))
        conv = sb("conv", [P, 4, S], at=at(28) + 64)
        decay = sb("decay", [P, 2, 512], at=at(24))
        xw = sb("xw", [P, 512], at=at(28))
        state = sb("state", [P, 512], at=at(30))
        bt = sb("bt", [P, 512], at=at(33))
        cbm = sb("cbm", [P, NT, P], at=at(35))
        prob2 = sb("prob2", [P, 384], at=at(36))
        probT2 = sb("probT2", [P, 384], at=at(38))
        dts = sb("dts", [P, 12, 64], at=at(40))
        dtT = sb("dtT", [P, S], at=at(43))
        ys = sb("ys", [P, NT, D], at=at(48))
        attn = sb("attn", [P, NT, 1024], at=at(64))
        ga = sb("ga", [P, NT, D], at=at(72))

        gain2 = sb("gain2", [P, D], at=at(0))
        fh = sb("fh", [P, 4 * max(PARTS), S], F32R, at=at(48))
        fl = sb("fl", [P, 4 * max(PARTS), S], F32R, at=at(64))
        praw = sb("praw", [P, 2, S], at=at(80))
        ph = sb("ph", [P, 2, S], F32R, at=at(82))
        pl = sb("pl", [P, 2, S], F32R, at=at(84))

        acc = [psum("acc0", 1024), psum("acc1", 1024)]
        psS = psum("psS", 1024)
        psT = psum("psT", 512)
        psO = psum("psO", 512)

        def cst(name, rows=P):
            at, w = CONST_COLS[name]
            return const[0:rows, at:at + w]

        def lay(name, a=0, b=None):
            at, w = LAYER_COLS[name]
            return lcur[:, at + a:at + (w if b is None else b)]

        def par(name, a=0, b=None):
            at, w = BLOCK2_COLS[name]
            return bsmall[:, at + a:at + (w if b is None else b)]

        ident, rot, tri = cst("ident"), cst("rot"), cst("tri")

        w_loaded = [sem(f"w_loaded{i}") for i in range(RING)]
        hi_ready = sem("hi_ready")
        lo_ready = sem("lo_ready")
        w_used = sem("w_used")
        acc_free = [sem(f"acc_free{i}") for i in range(2)]
        act_read = sem("act_read")
        negmax_ready = sem("negmax_ready")
        head_read = sem("head_read")
        turned = sem("turned")
        turn_hi = sem("turn_hi")
        turn_lo = sem("turn_lo")
        ms_ready = sem("ms_ready")
        root_ready = sem("root_ready")
        r_ready = sem("r_ready")
        diag_ready = sem("diag_ready")
        c_ready = sem("c_ready")
        row_ready = sem("row_ready")
        rot_in = sem("rot_in")
        rot_done = sem("rot_done")
        scores_ready = sem("scores_ready")
        exp_ready = sem("exp_ready")
        weights_ready = sem("weights_ready")
        probT_in_psum = sem("probT_in_psum")
        probT_ready = sem("probT_ready")
        pv_ready = sem("pv_ready")
        const_loaded = sem("const_loaded")
        masks_loaded = sem("masks_loaded")
        lsmall_loaded = sem("lsmall_loaded")
        bsmall_loaded = sem("bsmall_loaded")
        gain1_loaded = sem("gain1_loaded")
        x_loaded = [sem(f"x_loaded{i}") for i in range(2)]
        bias_loaded = sem("bias_loaded")
        bias_ps = sem("bias_ps")
        bias_sb = sem("bias_sb")
        bias_out = sem("bias_out")
        bias_in = sem("bias_in")
        bias_flip = sem("bias_flip")
        bias_done = sem("bias_done")
        pos_loaded = sem("pos_loaded")
        angle_ready = sem("angle_ready")
        table_ready = sem("table_ready")
        lam_in = sem("lam_in")
        lam_exp = sem("lam_exp")
        final1_ready = sem("final1_ready")
        spilled = sem("spilled")
        near_loaded = sem("near_loaded")
        refetched = sem("refetched")
        gain2_loaded = sem("gain2_loaded")
        k_spread = sem("k_spread")
        conv_sum = sem("conv_sum")
        conv_done = sem("conv_done")
        back_ready = sem("back_ready")
        back_read = sem("back_read")
        dt_turned = sem("dt_turned")
        dt_step = sem("dt_step")
        dt_act = sem("dt_act")
        acs_ready = sem("acs_ready")
        decay_in = sem("decay_in")
        decay_ready = sem("decay_ready")
        cb_ready = sem("cb_ready")
        xw_ready = sem("xw_ready")
        cb_read = sem("cb_read")
        state_ps = sem("state_ps")
        state_ready = sem("state_ready")
        off_ready = sem("off_ready")
        off_read = sem("off_read")
        rows_ready = sem("rows_ready")
        diff_ready = sem("diff_ready")
        unit_exp = sem("unit_exp")
        unit_ready = sem("unit_ready")
        diag_out = sem("diag_out")
        diag_read = sem("diag_read")
        merged_free = sem("merged_free")
        gate_done = sem("gate_done")
        hid_ready = sem("hid_ready")
        hid_hi = sem("hid_hi")
        hid_lo = sem("hid_lo")
        p_loaded = sem("p_loaded")
        p_hi = sem("p_hi")
        p_lo = sem("p_lo")
        result_ready = [sem(f"result_ready{t}") for t in range(NT)]
        stored = sem("stored")

        block = ctx.enter_context(nc.Block())

        def moved(eng, k, more=0):
            eng.wait_ge(acc_free[k % 2], more + (k // 2 + 2))

        def wait(eng, signal, value):
            if not (isinstance(value, int) and value <= 0):
                eng.wait_ge(signal, value)

        @block.sync
        def _(sp):
            def load(g, slot):
                sp.dma_start(raw[:, slot, :], wstream[g, :, :]).then_inc(w_loaded[slot], 16)

            sp.dma_start(bias[0:33, 0, 0:DH], bias_rows).then_inc(bias_loaded, 16)
            sp.dma_start(bias[0:33, 2:4, :].rearrange("p a b -> p (a b)")[:, 0:384], bias_onehot).then_inc(bias_loaded, 16)
            sp.dma_start(const[:, 0:4 * P], const_in[:, 0:4 * P]).then_inc(const_loaded, 16)
            sp.dma_start(lsmall[:, :, :], layer_small.rearrange("l p w -> p l w")).then_inc(lsmall_loaded, 16)
            sp.dma_start(bsmall[:, :], block2_small).then_inc(bsmall_loaded, 16)
            sp.dma_start(pos_i[:, :], positions.partition_broadcast(P)).then_inc(pos_loaded, 16)

            def load_x(half):
                cols = slice(1024 * half, 1024 * half + 1024)
                sp.dma_start(x[:, :, cols], x_in.rearrange("(t p) d -> p t d", p=P)[:, :, cols])\
                    .then_inc(x_loaded[half], 16)

            load_x(0)
            sp.wait_ge(bias_sb, 1)
            sp.dma_start(rev.ap(), o[0:DH, 1, 0:384]).then_inc(bias_out, 16)
            load(0, 0)
            sp.wait_ge(bias_out, 16)
            sp.dma_start(o[:, 0, :].rearrange("p (h n) -> p h n", h=DH),
                         bass.AP(rev, 0, [[1, P], [384, DH], [1, 256]])).then_inc(bias_in, 16)
            load_x(1)
            for g in range(1, RING):
                load(g, g)
            sp.dma_start(const[:, 4 * P:], const_in[:, 4 * P:RESIDENT]).then_inc(masks_loaded, 16)
            sp.dma_start(gain1[:, :], gain_final1).then_inc(gain1_loaded, 16)

            with sp.Fori(1, G_ALL // RING) as i:
                for j in range(RING):
                    sp.wait_ge(lo_ready, RING * i + (j + 1 - RING))
                    sp.dma_start(raw[:, j, :], wstream[bass.ds(RING * i + j, 1), :, :]
                                 .rearrange("a p n -> p (a n)")).then_inc(w_loaded[j], 16)
            for g in range(G_ALL // RING * RING, G_ALL):
                sp.wait_ge(lo_ready, g + 1 - RING)
                load(g, g % RING)
            for t in range(NT):
                sp.wait_ge(result_ready[t], 1)
                sp.dma_start(out[P * t:P * t + P, :], x[:, t, :]).then_inc(stored, 16)
            sp.wait_ge(stored, 16 * NT)

        @block.gpsimd
        def _(pool):
            def rest(g, j, first):
                pool.wait_ge(hi_ready, g + 1)
                if not first:
                    pool.wait_ge(w_used, g + 1 - RING)
                pool.tensor_tensor(wlo[:, j, :], raw[:, j, :], whi[:, j, :].bitcast(F32),
                                   ALU.subtract).then_inc(lo_ready, 1)

            for g in range(RING):
                rest(g, g, True)
            with pool.Fori(1, G_ALL // RING) as i:
                for j in range(RING):
                    rest(RING * i + j, j, False)
            for g in range(G_ALL // RING * RING, G_ALL):
                rest(g, g % RING, False)

        def turn_of(kind):
            return {
                "x": (x, xh, xl, lambda c: lsmall[:, 0, c:c + 1]),
                "x_last": (x, xh, xl, lambda c: lay("norm", c, c + 1)),
                "x_next": (x, xh, xl, lambda c: lay("next_norm", c, c + 1)),
                "u_last": (x, xh, xl, lambda c: par("mix", c, c + 1)),
                "o": (o, bh, bl, None),
                "cq": (o[:, :, c_at:c_at + 512], ch, cl, lambda c: lay("q_norm", c, c + 1)),
                "ckv": (o[:, :, c_at + 512:c_at + 1024], ch[:, 4:8, :], cl[:, 4:8, :], lambda c: lay("kv_norm", c, c + 1)),
                "attn": (attn, ah, al, None),
                "y": (ys, bh, bl, lambda c: par("ssd", c, c + 1)),
                "merged": (ga, xh, xl, None),
                "f": (x, bh, bl, lambda c: par("ffn", c, c + 1)),
                "ple": (x, xh, xl, lambda c: par("ple", c, c + 1)),
            }[kind]

        def turn_bank(kind, m):
            b = 1 if kind == "o" else m % 2
            return psS[:, 512 * b:512 * b + 512]

        @block.tensor
        def _(pe):
            def claim(k, more=0):
                pe.wait_ge(acc_free[k % 2], more + (k // 2 + 1))

            def granule(g, slot, out_ps, form, ah_, al_, chunk0, chunks, first, last_one, width=512):
                pe.wait_ge(lo_ready, g + 1)
                wh = whi[:, slot, :].rearrange("p (c n) -> p c n", c=chunks)
                wl = wlo[:, slot, :].rearrange("p (c n) -> p c n", c=chunks)
                m = None
                for c in range(chunks):
                    begin = first and c == 0
                    end = last_one and c == chunks - 1
                    kc = chunk0 + c
                    if form in ("B", "KV", "KR", "DT"):
                        for j in range({"B": 4, "KV": 2, "KR": 1, "DT": 1}[form]):
                            wide = 64 if form == "DT" else 128
                            dst = out_ps[0:wide, 256 * j:256 * j + 256]
                            js = slice(128 * j, 128 * j + wide)
                            pe.matmul(dst, wh[:, c, js], ah_[:, kc, :], start=begin and j % 2 == 0, stop=False,
                                      skip_group_check=True)
                            pe.matmul(dst, wh[:, c, js], al_[:, kc, :], start=False, stop=False,
                                      skip_group_check=True)
                            m = pe.matmul(dst, wl[:, c, js], ah_[:, kc, :], start=False, stop=end,
                                          skip_group_check=True)
                    if form in ("A", "KV"):
                        for t in range(NT):
                            lo, step = (0, 512) if form == "A" else (512, 256)
                            dst = out_ps[:, lo + step * t:lo + step * t + width]
                            cols = slice(0, width) if form == "A" else slice(256, 512)
                            ts = slice(P * t, P * t + P)
                            shared = form == "KV"
                            pe.matmul(dst, ah_[:, kc, ts], wh[:, c, cols], start=begin and not (shared and t),
                                      stop=False, skip_group_check=shared)
                            pe.matmul(dst, ah_[:, kc, ts], wl[:, c, cols], start=False, stop=False,
                                      skip_group_check=shared)
                            m = pe.matmul(dst, al_[:, kc, ts], wh[:, c, cols], start=False, stop=end,
                                          skip_group_check=shared)
                m.then_inc(w_used, 1)

            def turn(kind, m, t_value):
                src = turn_of(kind)[0]
                wait(pe, turn_lo, t_value if kind == "o" else t_value - 1)
                bank = turn_bank(kind, m)
                for j in range(2):
                    for t in range(NT):
                        c = 2 * m + j
                        dst, a = bank[:, 256 * j + P * t:256 * j + P * t + P], src[:, t, c * P:c * P + P]
                        z = pe.transpose(dst, a, ident)
                z.then_inc(turned, 1)

            def spread():
                for t in range(NT):
                    m = pe.matmul(psT[:, P * t:P * t + P], tri[:, P - 1:P].to_broadcast([P, P]), diag[:, t, :],
                                  start=True, stop=True)
                m.then_inc(row_ready, 1)

            FORMS = dict(q="B", k="B", v="A", cq="A", ckv="A", kr="KR", qn="B", qr="B", kn="B", vb="A",
                         z="A", out="A", kv="KV", xbc="B", dt="DT", ga="A", gs="A", attn_br="A", ssd_br="A", w_o="A")

            def scores(hh, tiles):
                pe.wait_ge(negmax_ready, hh + 1)
                for at_, qs, ks in ((0, slice(P, S), slice(0, S)), (256, slice(0, P), slice(0, P))):
                    for part in range(len(tiles[0])):
                        for n, parts in enumerate(tiles):
                            qa, ka = parts[part]
                            dst = psS[:, 512 * n + at_:512 * n + at_ + ks.stop]
                            m = pe.matmul(dst, qa[:, qs], ka[:, ks], start=part == 0, stop=part == len(parts) - 1)
                m.then_inc(scores_ready, 1)

            def head_turn(src):
                for j in range(3):
                    m = pe.transpose(psT[:, P * j:P * j + P], src[:, P * j:P * j + P], ident)
                m.then_inc(probT_in_psum, 1)

            def head_out(hh, pt, vv, w):
                pe.wait_ge(probT_ready, hh + 1)
                pe.wait_ge(head_read, hh + 1)
                pe.matmul(psO[:, w:2 * w], pt[:, 0:P], vv(0), start=True, stop=False)
                pe.matmul(psO[:, w:2 * w], pt[:, P:2 * P], vv(1), start=False, stop=True)
                m = pe.matmul(psO[:, 0:w], pt[:, 2 * P:3 * P], vv(0), start=True, stop=True)
                m.then_inc(pv_ready, 1)

            pe.wait_ge(bias_loaded, 32)
            pe.matmul(psT[0:DH, 0:384], bias[0:33, 0, 0:DH],
                      bias[0:33, 2:4, :].rearrange("p a b -> p (a b)")[:, 0:384], start=True, stop=True)\
                .then_inc(bias_ps, 1)
            pe.wait_ge(const_loaded, 16)
            pe.wait_ge(x_loaded[0], 16)
            for m in range(4):
                turn("x", m, m)
            pe.wait_ge(bias_in, 16)
            for j in range(4):
                if j == 2:
                    pe.wait_ge(x_loaded[1], 16)
                    for m in (4, 5):
                        turn("x", m, m)
                if j >= 2:
                    pe.wait_ge(bias_done, j - 1)
                pe.matmul((psO, psT)[j % 2][:, 0:512], cst("flip"), o[:, 0, 512 * j:512 * j + 512],
                          start=True, stop=True).then_inc(bias_flip, 1)

            with pe.Fori(0, DEPTH) as l:
                uses = l * (LAYER.k // 2)
                tb = l * LAYER.t + PRO_T

                def read_upto(step):
                    for b in range(2):
                        pe.wait_ge(acc_free[b], uses + (1 + freed(b, LAYER_STEP[step])))

                for what, d in LAYER.items:
                    if what == "gran":
                        kind, n, i = d["kind"], d["n"], d["i"]
                        if i == 0:
                            claim(d["k"], uses)
                        if kind == "q" and n == 0:
                            pe.wait_ge(turn_lo, tb + (i - 5))
                        operand = {"qn": "cq", "kn": "ckv", "out": "o"}.get(kind)
                        if operand and n == 0:
                            pe.wait_ge(turn_lo, tb + (TURN["layer", operand, i] + 1))
                        a, b, c0 = xh, xl, 2 * i
                        chunks = 8 if kind == "kr" else 2
                        if kind == "kr":
                            c0 = 8 * i
                        if kind in ("qn", "qr"):
                            a, b = ch, cl
                        if kind in ("kn", "vb"):
                            a, b, c0 = ch, cl, 4 + 2 * i
                        if kind == "out":
                            a, b = bh, bl
                        granule(l * LAYER.g + d["g"], d["g"] % RING, acc[d["k"] % 2], FORMS[kind], a, b, c0,
                                chunks, i == 0, i == d["of"] - 1)
                    elif what == "turn":
                        kind, m = d["kind"], d["m"]
                        if kind == "x_last":
                            pe.wait_ge(acc_free[1], uses + 1)
                        elif kind == "o":
                            pe.wait_ge(act_read, l * 4 + (m // 2 + 2))
                        elif kind in ("cq", "ckv"):
                            if m == 0:
                                pe.wait_ge(c_ready, l * 2 + (1 if kind == "cq" else 2))
                            if kind == "cq":
                                pe.wait_ge(negmax_ready, l * HEADS + (DH + 1))
                        else:
                            moved(pe, LAYER_STEP["out", m // 2], uses)
                            if m == 0:
                                pe.wait_ge(negmax_ready, l * HEADS + (HEADS + 1))
                        turn(kind, m, tb + d["t"])
                    elif what == "spread":
                        pe.wait_ge(bias_done, 4)
                        pe.wait_ge(diag_ready, l + 1)
                        spread()
                    elif what == "swap":
                        r = 0 if d["kind"] == "kr" else 1
                        pe.wait_ge(rot_in, l * 2 + r + 1)
                        for j in range(1 if r == 0 else 4):
                            m = pe.matmul(acc[d["k"] % 2][:, 256 * j:256 * j + 256], rot,
                                          unrot[:, 256 * j:256 * j + 256], start=True, stop=True)
                        m.then_inc(rot_done, 1)
                    elif what == "head_scores":
                        h = d["h"]
                        if h < DH:
                            if h == 0:
                                read_upto(("k", 1))
                            scores(l * HEADS + h, [[(qT[64 * m:64 * m + 64, h, :], kT[64 * m:64 * m + 64, h, :])]
                                                   for m in range(2)])
                        else:
                            e = h - DH
                            if e == 0:
                                read_upto(("vb", 1))
                            half = slice(64 * (e % 2), 64 * (e % 2) + 64)
                            scores(l * HEADS + h, [[(qT[:, e, :], kT[:, e, :]), (qr[half, e // 2, :], kr[half, :])]])
                    elif what == "head_turn":
                        h = d["h"]
                        if h < DH:
                            pe.wait_ge(weights_ready, l * DH + h + 1)
                        else:
                            pe.wait_ge(exp_ready, l * HEADS + h + 1)
                        head_turn(prob[:, 0, :])
                    elif what == "head_out":
                        h = d["h"]
                        e = h % DH
                        if h in (0, 4):
                            read_upto(("v", h // 4))
                        head_out(l * HEADS + h, probT, lambda c, e=e: v[:, c, e * P:e * P + P], P)

            HB = DEPTH * HEADS
            for what, d in B2.items:
                if what == "gran":
                    kind, n, i = d["kind"], d["n"], d["i"]
                    if i == 0:
                        claim(K2 + d["k"])
                    if n == 0 and kind == "q":
                        pe.wait_ge(turn_lo, T2 + i - 5)
                    operand = {"attn_br": "attn", "ssd_br": "y", "w_o": "merged"}.get(kind)
                    if n == 0 and operand:
                        pe.wait_ge(turn_lo, T2 + TURN["block2", operand, i] + 1)
                    a, b = {"attn_br": (ah, al), "ssd_br": (bh, bl)}.get(kind, (xh, xl))
                    chunks = 16 if kind == "dt" else 2
                    granule(G2 + d["g"], (G2 + d["g"]) % RING, acc[d["k"] % 2], FORMS[kind], a, b, 2 * i,
                            chunks, i == 0, i == d["of"] - 1, width=256 if kind == "kv" else 512)
                elif what == "turn":
                    kind, m = d["kind"], d["m"]
                    if kind == "u_last":
                        moved(pe, K2 - 1)
                    elif kind == "attn":
                        if m == 0:
                            pe.wait_ge(head_read, HB + SWA_H + 1)
                            pe.wait_ge(cb_read, SSM_G)
                            pe.wait_ge(off_read, SSM_G)
                    elif kind == "y":
                        pe.wait_ge(act_read, DEPTH * 4 + m // 2 + 2)
                    else:
                        moved(pe, K2 + B2_STEP["ssd_br" if kind == "merged" else "w_o", m // 2])
                    turn(kind, m, T2 + d["t"])
                elif what == "spread":
                    pe.wait_ge(diag_ready, DG2 + (1 if d["kind"] == "u" else 2))
                    spread()
                elif what == "swap":
                    r = DEPTH * 2 + (d["n"] if d["kind"] == "q" else 2)
                    pe.wait_ge(rot_in, r + 1)
                    for j in range(4 if d["kind"] == "q" else 2):
                        m = pe.matmul(acc[d["k"] % 2][:, 256 * j:256 * j + 256], rot,
                                      attn[:, 0, 256 * j:256 * j + 256], start=True, stop=True)
                    m.then_inc(rot_done, 1)
                elif what == "back":
                    n, c, b = d["n"], d["c"], d["b"]
                    pe.wait_ge(conv_done, n + 1)
                    wait(pe, back_read, b)
                    for j in range(4):
                        src = bcT[:, j, 0:P] if n == 0 else conv[:, j, P * c:P * c + P]
                        m = pe.transpose(psS[:, 512 + P * j:512 + P * j + P], src, ident)
                    m.then_inc(back_ready, 1)
                elif what == "head_scores":
                    h = d["h"]
                    if h == 0:
                        pe.wait_ge(k_spread, 16 * KV_H * 2)
                    half = slice(64 * (h % 2), 64 * (h % 2) + 64)
                    scores(HB + h, [[(q2[half, h // 2, :], kk2[half, h // (SWA_H // KV_H), :])]])
                elif what == "head_turn":
                    pe.wait_ge(exp_ready, HB + d["h"] + 1)
                    head_turn(prob2[:, :])
                elif what == "head_out":
                    h = d["h"]
                    kvh = h // (SWA_H // KV_H)
                    head_out(HB + h, probT2, lambda c, e=kvh: v2[:, c, e * HD:e * HD + HD], HD)
                elif what == "dt_turn":
                    moved(pe, K2 + B2_STEP["dt", 0])
                    for t in range(NT):
                        m = pe.transpose(psT[:, 64 * t:64 * t + 64], dtT[0:64, P * t:P * t + P], ident[0:64, 0:64])
                    m.then_inc(dt_turned, 1)
                elif what == "decay":
                    pe.wait_ge(dt_step, 3)
                    pe.wait_ge(head_read, HB + SWA_H + 1)
                    pe.matmul(psO[:, 0:64], tri, dts[:, 6, :], start=True, stop=True)
                    pe.matmul(psO[:, 64:128], tri[:, P - 1:P].to_broadcast([P, P]), dts[:, 6, :], start=True,
                              stop=True).then_inc(acs_ready, 1)
                elif what == "group_cb":
                    grp = d["grp"]
                    if grp == 0:
                        pe.wait_ge(negmax_ready, HB + SWA_H + 1)
                        pe.wait_ge(conv_done, 6)
                    wait(pe, cb_read, grp)
                    for c in range(NT):
                        m = pe.matmul(psS[:, P * c:P * c + P], bcT[:, grp, P * c:P * c + P],
                                      bcT[:, 4 + grp, P * c:P * c + P], start=True, stop=True)
                    m.then_inc(cb_ready, 1)
                elif what == "group_state":
                    grp = d["grp"]
                    pe.wait_ge(xw_ready, grp + 1)
                    if grp == 0:
                        pe.wait_ge(back_read, BACKS)
                    wait(pe, off_read, grp)
                    pe.matmul(psS[:, 512:1024], bt[:, P * grp:P * grp + P], xw[:, :], start=True, stop=True)\
                        .then_inc(state_ps, 1)
                elif what == "group_off":
                    grp = d["grp"]
                    pe.wait_ge(state_ready, grp + 1)
                    pe.matmul(psS[:, 512:1024], bcT[:, 4 + grp, P:S], state[:, :], start=True, stop=True)\
                        .then_inc(off_ready, 1)
                elif what == "unit_rows":
                    u, c, h0 = d["u"], d["c"], d["h0"]
                    if u == 0:
                        pe.wait_ge(probT_ready, HB + SWA_H)
                    wait(pe, diff_ready, u)
                    for j in range(4):
                        a = dts[:, 6, 32 * c + h0 + j:32 * c + h0 + j + 1].to_broadcast([P, P])
                        m = pe.matmul(psT[:, P * j:P * j + P], a, tri, start=True, stop=True)
                    m.then_inc(rows_ready, 1)
                elif what == "unit_out":
                    u, c, h0 = d["u"], d["c"], d["h0"]
                    pe.wait_ge(unit_ready, u + 1)
                    wait(pe, diag_read, u)
                    if u == 0:
                        pe.wait_ge(decay_in, 1)
                    for j in range(4):
                        m = pe.matmul(psO[:, 64 * j:64 * j + 64], decay[:, u % 2, P * j:P * j + P],
                                      xd[:, c, 64 * (h0 + j):64 * (h0 + j) + 64], start=True, stop=True)
                    m.then_inc(diag_out, 1)

            pe.wait_ge(turn_lo, T_DOWN)
            for f in FFN_PARTS:
                with pe.Fori(0, f["hbs"]) as i:
                    for side in range(2):
                        claim(f["k_up"] + side, i)
                        for j in range(8):
                            g = f["g_up"] + 8 * side + j
                            granule(16 * i + g, g % RING, acc[(GATE, UP)[side]], "B", bh, bl, 2 * j, 2, j == 0, j == 7)
                per = 2 * f["hbs"]
                if f is FFN_PARTS[-1]:
                    continue
                with pe.Fori(0, 2) as i:
                    for side in range(2):
                        k = f["k_dn"] + side
                        claim(k, i)
                        for j in range(per):
                            g = f["g_dn"] + per * side + j
                            if side == 0 and j in (0, per - 2):
                                pe.wait_ge(hid_lo, f["done"] + f["hbs"] - (1 if j == 0 else 0))
                            granule(2 * per * i + g, g % RING, acc[k % 2], "A", fh, fl, 2 * j, 2, j == 0, j == per - 1)
            for what, d in DOWN.items:
                if what == "gran":
                    k, g, i = K_DOWN + d["k"], G_DOWN + d["g"], d["i"]
                    if i == 0:
                        claim(k)
                    if d["n"] == 0 and i in (0, d["of"] - 2):
                        pe.wait_ge(hid_lo, HIDDEN_BLOCKS - (1 if i == 0 else 0))
                    granule(g, g % RING, acc[k % 2], "A", fh, fl, 2 * i, 2, i == 0, i == d["of"] - 1)
                elif what == "turn":
                    moved(pe, K_DOWN + d["m"] // 2)
                    turn("ple", d["m"], T_DOWN + d["t"])
            for what, d in PLE.items:
                if what == "gran":
                    k, g, i = K_PLE + d["k"], G_PLE + d["g"], d["i"]
                    if i == 0:
                        claim(k)
                    if d["kind"] == "gate" and d["n"] == 0:
                        pe.wait_ge(turn_lo, T_PLE + i - 5)
                    if d["kind"] == "proj" and d["n"] == 0:
                        pe.wait_ge(p_lo, 1)
                    a, b = (xh, xl) if d["kind"] == "gate" else (ph, pl)
                    granule(g, g % RING, acc[k % 2], "A", a, b, 2 * i, 2, i == 0, i == d["of"] - 1)
                elif what == "turn":
                    moved(pe, K_DOWN + 3)
                    turn("ple", d["m"], T_PLE + d["t"])

        @block.scalar
        def _(act):
            def upper(g, slot, first=False):
                act.wait_ge(w_loaded[slot], 16 * (g // RING + 1))
                if not first:
                    act.wait_ge(w_used, g + 1 - RING)
                act.activation(whi[:, slot, :], raw[:, slot, :], ACT.Copy).then_inc(hi_ready, 1)

            def ahead(g):
                if g + LOOK < G_ALL:
                    upper(g + LOOK, g % RING)

            def turn_round(kind, m, t_value):
                _, dh, _, gain = turn_of(kind)
                act.wait_ge(turned, t_value + 1)
                bank = turn_bank(kind, m)
                if gain is None:
                    z = act.activation(dh[:, 2 * m:2 * m + 2, :].rearrange("p c s -> p (c s)"), bank, ACT.Copy)
                else:
                    for j in range(2):
                        z = act.activation(dh[:, 2 * m + j, :], bank[:, 256 * j:256 * j + 256], ACT.Copy,
                                           scale=gain(2 * m + j))
                z.then_inc(turn_hi, 1)

            def root(s_value):
                act.wait_ge(ms_ready, s_value + 1)
                act.activation(stat[:, 32:48], stat[:, 16:32], ACT.Sqrt).then_inc(root_ready, 1)

            def exps(hh, pr, maps):
                act.wait_ge(negmax_ready, hh + 2)
                for m in range(maps):
                    act.activation(pr(m)[:, 0:256], pr(m)[:, 0:256], ACT.Exp, bias=negmax[:, m:m + 1],
                                   accum_out=sums[:, m:m + 1])
                    z = act.activation(pr(m)[:, 256:384], pr(m)[:, 256:384], ACT.Exp, bias=negmax[:, 2 + m:3 + m],
                                       accum_out=sums[:, 2 + m:3 + m])
                return z

            def copy_probT(hh, pt):
                act.wait_ge(probT_in_psum, hh + 1)
                act.activation(pt[:, :], psT[:, 0:384], ACT.Copy).then_inc(probT_ready, 1)

            def scaled(dst, k, g_value, func):
                act.wait_ge(w_used, g_value)
                for t in range(NT):
                    z = act.activation(dst[:, t, :], acc[k % 2][:, 512 * t:512 * t + 512], func, scale=rs[:, t:t + 1])
                z.then_inc(acc_free[k % 2], 1)

            act.wait_ge(lsmall_loaded, 16)
            for m in range(4):
                turn_round("x", m, m)
            upper(0, 0, first=True)
            for m in (4, 5):
                turn_round("x", m, m)
            for g in range(1, RING):
                upper(g, g, first=True)
            act.wait_ge(angle_ready, 1)
            act.activation(sin2[:, :], pos_t[:, 1, :], ACT.Sin)
            act.activation(cos2[:, :], pos_t[:, 2, :], ACT.Sin).then_inc(table_ready, 1)
            with act.Fori(0, DEPTH) as l:
                base = l * LAYER.g
                tb = l * LAYER.t + PRO_T
                for what, d in LAYER.items:
                    if what == "gran":
                        g = d["g"]
                        act.wait_ge(w_loaded[g % RING], 16 * (l * (LAYER.g // RING) + (g + LOOK) // RING + 1))
                        act.wait_ge(w_used, base + (g + 1))
                        act.activation(whi[:, g % RING, :], raw[:, g % RING, :], ACT.Copy).then_inc(hi_ready, 1)
                    elif what == "turn":
                        if d["kind"] == "x_last":
                            act.wait_ge(lam_in, l + 1)
                        turn_round(d["kind"], d["m"], tb + d["t"])
                    elif what == "inverse":
                        root(l * LAYER_S + ROOT[d["kind"]])
                        if d["kind"] == "x":
                            act.wait_ge(lam_in, l + 1)
                            act.activation(lam[:, 2:4], lam[:, 0:2], ACT.Exp).then_inc(lam_exp, 1)
                    elif what == "head_exp":
                        h = d["h"]
                        exps(l * HEADS + h, lambda m: prob[:, m, :], 2 if h < DH else 1).then_inc(exp_ready, 1)
                    elif what == "head_turn":
                        copy_probT(l * HEADS + d["h"], probT)
                    elif what == "evac" and d["kind"] == "z":
                        act.wait_ge(act_read, l * 4 + (d["n"] + 1))
                        act.wait_ge(r_ready, l + 1)
                        scaled(act_out, d["k"], base + d["g"], ACT.Silu)

            HB = DEPTH * HEADS
            for what, d in B2.items:
                kind = d.get("kind")
                if what == "gran":
                    ahead(G2 + d["g"])
                elif what == "turn":
                    turn_round(kind, d["m"], T2 + d["t"])
                elif what == "inverse":
                    root(S2 + ROOT[kind])
                    if kind != "u":
                        continue
                    act.wait_ge(final1_ready, 1)
                    act.dma_start(spill.rearrange("(t p) d -> p t d", p=P), x[:, :, :]).then_inc(spilled, 16)
                    act.dma_start(cst("causal")[:, 0:P], const_in[:, RESIDENT:]).then_inc(near_loaded, 16)
                elif what == "head_exp":
                    h = d["h"]
                    exps(HB + h, lambda m: prob2[:, :], 1)
                    act.activation(sums[:, 3:4], par("sinks", h, h + 1), ACT.Exp, bias=negmax[:, 2:3])
                    act.activation(sums[:, 1:2], par("sinks", h, h + 1), ACT.Exp, bias=negmax[:, 0:1])\
                        .then_inc(exp_ready, 1)
                elif what == "head_turn":
                    copy_probT(HB + d["h"], probT2)
                elif what == "key_halves":
                    moved(act, K2 + B2_STEP["kv", 0])
                    for i in range(KV_H):
                        for half in range(2):
                            act.dma_start(kk2[64 * half:64 * half + 64, i, :],
                                          k2[64 * (i % 2):64 * (i % 2) + 64, i // 2, :]).then_inc(k_spread, 16)
                elif what == "conv_silu":
                    n = d["n"]
                    act.wait_ge(conv_sum, n + 1)
                    dst = bcT[:, 4 * n:4 * n + 4, :] if n < 2 else conv[:, :, :]
                    act.activation(dst, conv[:, :, :], ACT.Silu).then_inc(conv_done, 1)
                elif what == "evac" and kind in ("ga", "gs"):
                    if d["n"] == 0:
                        act.wait_ge(r_ready, DEPTH + 1)
                        if kind == "gs":
                            act.wait_ge(spilled, 16)
                    cols = slice(512 * d["n"], 512 * d["n"] + 512)
                    scaled((ga if kind == "ga" else x)[:, :, cols], d["k"], G2 + d["g"], ACT.Sigmoid)
                elif what == "evac" and kind == "z":
                    act.wait_ge(act_read, DEPTH * 4 + d["n"] + 1)
                    scaled(act_out, d["k"], G2 + d["g"], ACT.Silu)
                elif what == "dt_exp":
                    act.wait_ge(dt_step, 1)
                    act.activation(dts[:, 8, 0:SSM_H], par("a_log"), ACT.Exp)
                    act.activation(dts[:, 2, :], dts[:, 1, :], ACT.Exp).then_inc(dt_act, 1)
                elif what == "dt_log":
                    act.wait_ge(dt_step, 2)
                    act.activation(dts[:, 4, :], dts[:, 3, :], ACT.Ln).then_inc(dt_act, 1)
                elif what == "decay_exp":
                    act.wait_ge(decay_in, 1)
                    act.activation(dts[:, 9, :], dts[:, 10, :], ACT.Exp).then_inc(decay_ready, 1)
                elif what == "group_state":
                    grp = d["grp"]
                    act.wait_ge(state_ps, grp + 1)
                    act.activation(state[:, :], psS[:, 512:1024], ACT.Copy).then_inc(state_ready, 1)
                elif what == "unit_mask":
                    u = d["u"]
                    act.wait_ge(diff_ready, u + 1)
                    act.activation(decay[:, u % 2, :], decay[:, u % 2, :], ACT.Exp).then_inc(unit_exp, 1)
                elif what == "evac" and kind == "ssd_br" and d["n"] == 3:
                    act.wait_ge(merged_free, 1)
                    act.dma_start(x[:, :, :], spill.rearrange("(t p) d -> p t d", p=P)).then_inc(refetched, 16)
            act.dma_start(praw[:, :, :], p_in).then_inc(p_loaded, 16)
            act.dma_start(gain2[:, :], gain_final2).then_inc(gain2_loaded, 16)

            for f in FFN_PARTS:
                def stream(g_static, i, stride, many):
                    for j in range(many):
                        g = g_static + j
                        act.wait_ge(w_loaded[g % RING], 16 * (stride // RING * i + (g + LOOK) // RING + 1))
                        act.wait_ge(w_used, stride * i + (g + 1))
                        act.activation(whi[:, g % RING, :], raw[:, g % RING, :], ACT.Copy).then_inc(hi_ready, 1)

                flat = act_out[:, :, :].rearrange("p t n -> p (t n)")
                with act.Fori(0, f["hbs"]) as i:
                    stream(f["g_up"], i, 16, 8)
                    moved(act, f["k_up"], i)
                    act.activation(flat, flat, ACT.Silu).then_inc(gate_done, 1)
                    stream(f["g_up"] + 8, i, 16, 8)
                    act.wait_ge(hid_ready, i + (f["done"] + 1))
                    act.activation(fh[:, bass.ds(4 * i, 4), :].rearrange("p c s -> p (c s)"), flat, ACT.Copy)\
                        .then_inc(hid_hi, 1)
                if f is FFN_PARTS[0]:
                    act.wait_ge(p_loaded, 16)
                    act.activation(ph[:, :, :], praw[:, :, :], ACT.Copy).then_inc(p_hi, 1)
                per = 2 * f["hbs"]
                if f is not FFN_PARTS[-1]:
                    with act.Fori(0, 2) as i:
                        stream(f["g_dn"], i, 2 * per, 2 * per)
            for what, d in DOWN.items:
                if what == "gran":
                    ahead(G_DOWN + d["g"])
                elif what == "turn":
                    turn_round("ple", d["m"], T_DOWN + d["t"])
            for what, d in PLE.items:
                if what == "gran":
                    ahead(G_PLE + d["g"])
                elif what == "turn":
                    turn_round("ple", d["m"], T_PLE + d["t"])
                elif what == "inverse":
                    root(S2 + ROOT["ple"])
                elif what == "evac" and d["kind"] == "gate":
                    act.wait_ge(act_read, DEPTH * 4 + 4 + d["n"] + 1)
                    act.wait_ge(r_ready, DEPTH + 3)
                    scaled(act_out, K_PLE + d["k"], G_PLE + d["g"], ACT.Sigmoid)
            root(S2 + 5)
            act.wait_ge(r_ready, DEPTH + 4)
            act.activation(x[:, 0, :], x[:, 0, :], ACT.Copy, scale=rs[:, 0:1]).then_inc(result_ready[0], 1)

        @block.vector
        def _(dve):
            def sync():
                dve.drain()

            def squares(src, n):
                sync()
                for t in range(NT):
                    a = src[:, t, 512 * n:512 * n + 512]
                    m = dve.tensor_tensor_reduce(out=junk[:, 512 * t:512 * t + 512], in0=a, in1=a, scale=1.0, scalar=0.0,
                                                 op0=ALU.mult, op1=ALU.add, accum_out=stat[:, 4 * t + n:4 * t + n + 1])
                return m

            def mean_of_quarters(eps):
                sync()
                dve.tensor_reduce(stat[:, 8:10], stat[:, 0:8].rearrange("p (t n) -> p t n", t=NT), AX_X, ALU.add)
                sync()
                dve.tensor_scalar(stat[:, 16:18], stat[:, 8:10], 1.0 / D, eps, ALU.mult, ALU.add).then_inc(ms_ready, 1)

            def make_diag():
                for t in range(NT):
                    m = dve.tensor_scalar(diag[:, t, :], ident, rs[:, t:t + 1], None, ALU.mult)
                m.then_inc(diag_ready, 1)

            def turn_rest(kind, m, t_value):
                _, dh, dl, gain = turn_of(kind)
                bank = turn_bank(kind, m)
                dve.wait_ge(turn_hi, t_value + 1)
                if gain is None:
                    z = dve.tensor_tensor(dl[:, 2 * m:2 * m + 2, :].rearrange("p c s -> p (c s)"), bank,
                                          dh[:, 2 * m:2 * m + 2, :].rearrange("p c s -> p (c s)").bitcast(F32), ALU.subtract)
                else:
                    for j in range(2):
                        c = 2 * m + j
                        z = dve.scalar_tensor_tensor(dl[:, c, :], bank[:, 256 * j:256 * j + 256], gain(c),
                                                     dh[:, c, :].bitcast(F32), ALU.mult, ALU.subtract)
                z.then_inc(turn_lo, 1)

            def spread(count):
                dve.wait_ge(row_ready, count)
                dve.tensor_copy(rbc[:, 0, :], psT[:, 0:S])
                sync()

            def by_token(tiles):
                return rbc[:, :, :].broadcast_to([P, tiles, S])

            def chunks_of(ps, tiles):
                return ps[:, 0:S * tiles].rearrange("p (j s) -> p j s", j=tiles)

            def scaled(dst, ps):
                for t in range(NT):
                    m = dve.tensor_scalar(dst(t), ps[:, 512 * t:512 * t + 512], rs[:, t:t + 1], None, ALU.mult)
                return m

            def rotate_in(raw_t, k, tiles, norm):
                rw = chunks_of(raw_t, tiles)
                ps = chunks_of(acc[k % 2], tiles)
                if norm:
                    dve.tensor_tensor(rw, ps, by_token(tiles), ALU.mult).then_inc(rot_in, 1)
                else:
                    dve.tensor_copy(rw, ps).then_inc(rot_in, 1)

            def rotate(dst, cos, sin, k, r, tiles, raw_t):
                rw = chunks_of(raw_t, tiles)
                dve.wait_ge(rot_done, r + 1)
                cb = cos.unsqueeze(1).broadcast_to([P, tiles, S])
                sb_ = sin.unsqueeze(1).broadcast_to([P, tiles, S])
                first = dve.tensor_tensor(dst, chunks_of(acc[k % 2], tiles), sb_, ALU.mult)
                dve.tensor_tensor(rw, rw, cb, ALU.mult)
                sync()
                return first, dve.tensor_tensor(dst, dst, rw, ALU.add)

            def masked(hh, pr, mask, scale):
                dve.wait_ge(scores_ready, hh + 1)
                dve.scalar_tensor_tensor(pr, psS[:, 0:384], scale, mask, ALU.mult, ALU.add)
                sync()
                dve.tensor_reduce(negmax[:, 0:1], pr[:, 0:256], AX_X, ALU.max, negate=True)
                return dve.tensor_reduce(negmax[:, 2:3], pr[:, 256:384], AX_X, ALU.max, negate=True)

            for i, signal in enumerate((acc_free[0], acc_free[1], act_read, negmax_ready, head_read)):
                dve.memset(rinv[:, 0:1], 0.0).then_inc(signal, 1)
                sync()
            dve.memset(stat[:, :], 1.0)
            dve.wait_ge(bias_ps, 1)
            dve.tensor_copy(o[0:DH, 1, 0:384], psT[0:DH, 0:384]).then_inc(bias_sb, 1)
            dve.wait_ge(bsmall_loaded, 16)
            dve.wait_ge(pos_loaded, 16)
            TWO_PI = 2 * math.pi
            magic = 1.5 * 2.0 ** 23
            c1 = 6.28125
            c2 = float(np.float32((TWO_PI - c1) * 2 ** 19 // 1 / 2 ** 19))
            c3 = TWO_PI - c1 - c2
            ang = junk[:, 0:256]
            turns = junk[:, 256:768].rearrange("p (a s) -> p a s", a=2)
            r = pos_t[:, 1:3, :]
            dve.tensor_copy(ang, pos_i[:, :])
            sync()
            dve.tensor_scalar(ang, ang, par("inv_freq"), None, ALU.mult)
            sync()
            for which, shift in ((0, 0.0), (1, 0.25)):
                dve.tensor_scalar(turns[:, which, :], ang, 1.0 / TWO_PI, shift, ALU.mult, ALU.add)
            sync()
            dve.tensor_scalar(turns, turns, magic, None, ALU.add)
            sync()
            dve.tensor_scalar(turns, turns, magic, None, ALU.subtract)
            sync()
            dve.scalar_tensor_tensor(r, turns, -c1, ang.unsqueeze(1).broadcast_to([P, 2, S]), ALU.mult, ALU.add)
            sync()
            dve.scalar_tensor_tensor(r, turns, -c2, r, ALU.mult, ALU.add)
            sync()
            dve.scalar_tensor_tensor(r, turns, -c3, r, ALU.mult, ALU.add)
            sync()
            dve.tensor_scalar(pos_t[:, 2, :], pos_t[:, 2, :], math.pi / 2, None, ALU.add)
            sync()
            dve.tensor_scalar(r, r, 3.1415925, -3.1415925, ALU.min, ALU.max).then_inc(angle_ready, 1)
            dve.wait_ge(lsmall_loaded, 16)
            for m in range(4):
                turn_rest("x", m, m)
            for j in range(4):
                dve.wait_ge(bias_flip, j + 1)
                dve.tensor_copy(bias[:, 2 * j:2 * j + 2, :].rearrange("p a b -> p (a b)"),
                                (psO, psT)[j % 2][:, 0:512]).then_inc(bias_done, 1)
                if j == 1:
                    for m in (4, 5):
                        turn_rest("x", m, m)
            for half in range(2):
                dve.wait_ge(x_loaded[half], 16)
                squares(x, 2 * half)
                squares(x, 2 * half + 1)
            sync()
            dve.tensor_tensor(par("mix"), par("mix"), par("final1"), ALU.mult)
            sync()
            at_next = LAYER_COLS["next_norm"][0]
            dve.tensor_copy(lsmall[:, DEPTH - 1, at_next:at_next + DC], par("mix"))
            dve.wait_ge(masks_loaded, 16)
            dve.wait_ge(table_ready, 1)
            sync()

            with dve.Fori(0, DEPTH) as l:
                tb = l * LAYER.t + PRO_T
                uses = l * (LAYER.k // 2)
                dve.tensor_copy(lcur[:, :], lsmall[:, bass.ds(l, 1), 0:LAYER_OWN].rearrange("p a w -> p (a w)"))
                sync()
                own = lambda a, w: lsmall[:, bass.ds(l, 1), a:a + w].rearrange("p a w -> p (a w)")
                dve.tensor_copy(junk[:, 256:512], own(LAYER_COLS["lambda"][0], 256))
                sync()
                for i in range(2):
                    dve.tensor_tensor_reduce(out=junk[:, 64 * i:64 * i + 64], in0=junk[:, 256 + 128 * i:320 + 128 * i],
                                             in1=junk[:, 320 + 128 * i:384 + 128 * i], scale=1.0, scalar=0.0,
                                             op0=ALU.mult, op1=ALU.add, accum_out=lam[:, i:i + 1])
                sync()
                dve.tensor_scalar(subg[:, :], own(LAYER_COLS["subln"][0], P), lay("one_minus"), None, ALU.mult).then_inc(lam_in, 1)
                for what, d in LAYER.items:
                    if what == "root" and d["kind"] == "x":
                        mean_of_quarters(1e-6)
                    elif what == "root" and d["kind"] != "subln":
                        at_ = c_at + (0 if d["kind"] == "cq" else 512)
                        sync()
                        for t in range(NT):
                            a = o[:, t, at_:at_ + 512]
                            dve.tensor_tensor_reduce(out=junk[:, 512 * t:512 * t + 512], in0=a, in1=a, scale=1.0,
                                                     scalar=0.0, op0=ALU.mult, op1=ALU.add, accum_out=stat[:, t:t + 1])
                        sync()
                        dve.tensor_scalar(stat[:, 16:18], stat[:, 0:2], 1.0 / 512, 1e-6, ALU.mult, ALU.add)\
                            .then_inc(ms_ready, 1)
                    elif what == "root":
                        sync()
                        for t in range(NT):
                            oa = o[:, t, 0:1024]
                            dve.tensor_tensor(junk[:, :], oa, oa, ALU.mult)
                            sync()
                            dve.tensor_reduce(stat[:, 8 * t:8 * t + 8], junk[:, :].rearrange("p (h n) -> p h n", h=DH),
                                              AX_X, ALU.add)
                            sync()
                        dve.tensor_scalar(stat[:, 16:32], stat[:, 0:16], 1.0 / P, 1e-6, ALU.mult, ALU.add)\
                            .then_inc(ms_ready, 1)
                    elif what == "inverse":
                        kind = d["kind"]
                        sync()
                        dve.wait_ge(root_ready, l * LAYER_S + (ROOT[kind] + 1))
                        if kind == "x":
                            dve.reciprocal(rs[:, 0:NT], stat[:, 32:32 + NT]).then_inc(r_ready, 1)
                            sync()
                            make_diag()
                            dve.wait_ge(lam_exp, l + 1)
                            dve.tensor_tensor(lam[:, 4:5], lam[:, 3:4], lam[:, 2:3], ALU.subtract)
                            sync()
                            dve.tensor_tensor(lam[:, 5:6], lam[:, 4:5], lay("lam_init"), ALU.subtract)
                            sync()
                        elif kind != "subln":
                            dve.reciprocal(stat[:, 48:50], stat[:, 32:34])
                            sync()
                            at_ = c_at + (0 if kind == "cq" else 512)
                            for t in range(NT):
                                c = o[:, t, at_:at_ + 512]
                                m = dve.tensor_scalar(c, c, stat[:, 48 + t:49 + t], None, ALU.mult)
                            m.then_inc(c_ready, 1)
                        else:
                            dve.reciprocal(stat[:, 48:64], stat[:, 32:48])
                            sync()
                            for t in range(NT):
                                oa = o[:, t, 0:1024].rearrange("p (h n) -> p h n", h=DH)
                                r = stat[:, 48 + 8 * t:56 + 8 * t].unsqueeze(2).to_broadcast([P, DH, P])
                                dve.tensor_tensor(oa, oa, r, ALU.mult)
                            sync()
                            for t in range(NT):
                                oa = o[:, t, 0:1024].rearrange("p (h n) -> p h n", h=DH)
                                dve.tensor_tensor(oa, oa, subg[:, :].unsqueeze(1).broadcast_to([P, DH, P]), ALU.mult)
                            sync()
                    elif what == "spread":
                        spread(l + 1)
                    elif what == "swap":
                        k = d["k"]
                        if d["kind"] == "kr":
                            first, _ = rotate(kr[:, :].unsqueeze(1), cst("cos"), cst("sin"), k, l * 2, 1, unrot)
                        else:
                            first, _ = rotate(qr[:, :, :], cst("cos"), cst("sin"), k, l * 2 + 1, 4, unrot)
                        first.then_inc(acc_free[k % 2], 1)
                    elif what == "turn":
                        turn_rest(d["kind"], d["m"], tb + d["t"])
                    elif what == "evac":
                        kind, n, k = d["kind"], d["n"], d["k"]
                        ps = acc[k % 2]
                        free = acc_free[k % 2]
                        two = ps[:, :].rearrange("p (t n) -> p t n", t=NT)
                        cols = slice(512 * n, 512 * n + 512)
                        if kind in ("kr", "qr"):
                            sync()
                        if kind != "z":
                            dve.wait_ge(w_used, l * LAYER.g + d["g"])
                        if kind in ("q", "k"):
                            dst = qT if kind == "q" else kT
                            dve.tensor_tensor(dst[:, 4 * n:4 * n + 4, :], chunks_of(ps, 4), by_token(4), ALU.mult)\
                                .then_inc(free, 1)
                        elif kind in ("qn", "kn"):
                            dst = qT if kind == "qn" else kT
                            dve.tensor_copy(dst[:, 4 * n:4 * n + 4, :].rearrange("p c s -> p (c s)"), ps[:, :])\
                                .then_inc(free, 1)
                        elif kind == "v":
                            scaled(lambda t: v[:, t, cols], ps).then_inc(free, 1)
                        elif kind == "vb":
                            dve.tensor_copy(v[:, :, cols], two).then_inc(free, 1)
                        elif kind in ("cq", "ckv"):
                            at_ = c_at if kind == "cq" else c_at + 512
                            scaled(lambda t: o[:, t, at_:at_ + 512], ps).then_inc(free, 1)
                        elif kind in ("kr", "qr"):
                            rotate_in(unrot, k, 1 if kind == "kr" else 4, kind == "kr")
                        elif kind == "z":
                            moved(dve, k, uses)
                            dve.tensor_tensor(o[:, :, cols], o[:, :, cols], act_out[:, :, :], ALU.mult)\
                                .then_inc(act_read, 1)
                        elif kind == "out":
                            dve.tensor_tensor(x[:, :, cols], x[:, :, cols], two, ALU.add).then_inc(free, 1)
                            squares(x, n)
                    elif what == "head_scores":
                        h = d["h"]
                        hh = l * HEADS + h
                        if h < DH:
                            dve.wait_ge(scores_ready, hh + 1)
                            pss = psS[:, :].rearrange("p (m n) -> p m n", m=2)
                            b_all = bias[:, h, :].unsqueeze(1).broadcast_to([P, 2, 256])
                            b_diag = bias[:, h, 128:256].unsqueeze(1).broadcast_to([P, 2, 128])
                            dve.scalar_tensor_tensor(prob[:, :, 0:256], pss[:, :, 0:256], 64 ** -0.5, b_all,
                                                     ALU.mult, ALU.add)
                            dve.scalar_tensor_tensor(prob[:, :, 256:384], pss[:, :, 256:384], 64 ** -0.5, b_diag,
                                                     ALU.mult, ALU.add)
                            sync()
                            dve.tensor_reduce(negmax[:, 0:2], prob[:, :, 0:256], AX_X, ALU.max, negate=True)
                            dve.tensor_reduce(negmax[:, 2:4], prob[:, :, 256:384], AX_X, ALU.max, negate=True)\
                                .then_inc(negmax_ready, 1)
                        else:
                            masked(hh, prob[:, 0, :], cst("causal"), 192 ** -0.5).then_inc(negmax_ready, 1)
                    elif what == "head_weights":
                        h = d["h"]
                        sync()
                        dve.wait_ge(exp_ready, l * HEADS + h + 1)
                        if h < DH:
                            dve.reciprocal(rinv[:, :], sums[:, :])
                            sync()
                            for j in (1, 3):
                                dve.tensor_scalar(rinv[:, j:j + 1], rinv[:, j:j + 1], lam[:, 5:6], None, ALU.mult)
                            sync()
                            parts = ((0, 256, 0), (256, 384, 2))
                            for a, b, j in parts:
                                dve.tensor_scalar(prob[:, 1, a:b], prob[:, 1, a:b], rinv[:, j + 1:j + 2], None, ALU.mult)
                            sync()
                            for a, b, j in parts:
                                m = dve.scalar_tensor_tensor(prob[:, 0, a:b], prob[:, 0, a:b], rinv[:, j:j + 1],
                                                             prob[:, 1, a:b], ALU.mult, ALU.add)
                            m.then_inc(weights_ready, 1)
                        else:
                            for j in (0, 2):
                                dve.reciprocal(rinv[:, j:j + 1], sums[:, j:j + 1])
                            sync()
                    elif what == "head_out":
                        h = d["h"]
                        dve.wait_ge(pv_ready, l * HEADS + h + 1)
                        pso = psO[:, 0:256].rearrange("p (t n) -> p t n", t=NT)
                        if h < DH:
                            dve.tensor_copy(o[:, :, P * h:P * h + P], pso).then_inc(head_read, 1)
                        else:
                            dve.tensor_scalar(o[:, 0, P * h:P * h + P], pso[:, 0, :], rinv[:, 2:3], None, ALU.mult)
                            dve.tensor_scalar(o[:, 1, P * h:P * h + P], pso[:, 1, :], rinv[:, 0:1], None, ALU.mult)\
                                .then_inc(head_read, 1)
                sync()

            HB = DEPTH * HEADS
            by_head = lambda a, n=SSM_P: a.rearrange("p (h n) -> p h n", n=n)
            for what, d in B2.items:
                kind = d.get("kind")
                if what == "root":
                    mean_of_quarters(1e-5 if kind == "y" else 1e-6)
                elif what == "inverse":
                    sync()
                    dve.wait_ge(root_ready, S2 + ROOT[kind] + 1)
                    if kind == "u":
                        dve.reciprocal(stat[:, 48:50], stat[:, 32:34])
                        sync()
                        dve.tensor_tensor(rs[:, 0:2], rs[:, 0:2], stat[:, 48:50], ALU.mult).then_inc(r_ready, 1)
                    elif kind == "f":
                        dve.reciprocal(rs[:, 0:2], stat[:, 32:34]).then_inc(r_ready, 1)
                    else:
                        dve.reciprocal(rs[:, 2:4] if kind == "y" else rs[:, 0:2], stat[:, 32:34])
                    sync()
                    if kind in ("u", "f"):
                        make_diag()
                elif what == "second_norm":
                    dve.wait_ge(gain1_loaded, 16)
                    dve.wait_ge(turned, T2 + 2)
                    for t in range(NT):
                        m = dve.scalar_tensor_tensor(x[:, t, :], x[:, t, :], rs[:, t:t + 1], gain1[:, :], ALU.mult, ALU.mult)
                    m.then_inc(final1_ready, 1)
                    for n in range(4):
                        squares(x, n)
                    mean_of_quarters(1e-6)
                    dve.memset(stage[:, :, 0:TAPS - 1], 0.0)
                elif what == "spread":
                    spread(DEPTH + (1 if kind == "u" else 2))
                elif what == "turn":
                    turn_rest(kind, d["m"], T2 + d["t"])
                elif what == "evac":
                    n, k = d["n"], d["k"]
                    ps = acc[k % 2]
                    free = acc_free[k % 2]
                    two = ps[:, :].rearrange("p (t n) -> p t n", t=NT)
                    cols = slice(512 * n, 512 * n + 512)
                    if kind in ("q", "kv", "ssd_br", "xbc"):
                        sync()
                    if kind in ("q", "kv", "xbc", "dt", "attn_br", "ssd_br", "w_o"):
                        dve.wait_ge(w_used, G2 + d["g"])
                    if kind == "q":
                        rotate_in(attn[:, 0, :], k, 4, True)
                    elif kind == "kv":
                        for t in range(NT):
                            dve.tensor_scalar(v2[:, t, :], ps[:, 512 + 256 * t:768 + 256 * t], rs[:, t:t + 1], None, ALU.mult)
                        rotate_in(attn[:, 0, :], k, 2, True)
                    elif kind == "xbc":
                        dve.tensor_tensor(stage[:, :, TAPS - 1:], chunks_of(ps, 4), by_token(4), ALU.mult).then_inc(free, 1)
                    elif kind == "dt":
                        dve.tensor_tensor(dtT[0:64, :], ps[0:64, 0:S], rbc[0:64, 0, :], ALU.mult).then_inc(free, 1)
                    elif kind == "z":
                        moved(dve, K2 + k)
                        dve.tensor_tensor(ys[:, :, cols], ys[:, :, cols], act_out[:, :, :], ALU.mult).then_inc(act_read, 1)
                        squares(ys, n)
                    elif kind == "attn_br":
                        dve.tensor_tensor(ga[:, :, cols], ga[:, :, cols], two, ALU.mult).then_inc(free, 1)
                    elif kind == "ssd_br":
                        for t in range(NT):
                            m = dve.scalar_tensor_tensor(act_out[:, t, :], two[:, t, :], rs[:, 2 + t:3 + t], x[:, t, cols],
                                                         ALU.mult, ALU.mult)
                        if n == 3:
                            m.then_inc(merged_free, 1)
                        sync()
                        dve.tensor_tensor(ga[:, :, cols], ga[:, :, cols], act_out[:, :, :], ALU.add).then_inc(free, 1)
                    elif kind == "w_o":
                        if n == 0:
                            dve.wait_ge(refetched, 16)
                        dve.tensor_tensor(x[:, :, cols], x[:, :, cols], two, ALU.add).then_inc(free, 1)
                        squares(x, n)
                elif what == "tap":
                    n, tap = d["n"], d["tap"]
                    sync()
                    if tap == 0 and n >= 1:
                        dve.wait_ge(conv_done, n)
                    if tap == 0 and n >= 3:
                        dve.wait_ge(back_ready, 2 * n - 3)
                    for j in range(4):
                        w = par("conv_w", (4 * n + j) * TAPS + tap, (4 * n + j) * TAPS + tap + 1)
                        a = stage[:, j, tap:tap + S]
                        if tap == 0:
                            m = dve.tensor_scalar(conv[:, j, :], a, w, par("conv_b", 4 * n + j, 4 * n + j + 1),
                                                  ALU.mult, ALU.add)
                        else:
                            m = dve.scalar_tensor_tensor(conv[:, j, :], a, w, conv[:, j, :], ALU.mult, ALU.add)
                    if tap == TAPS - 1:
                        m.then_inc(conv_sum, 1)
                elif what == "dt_turn":
                    dve.wait_ge(dt_turned, 1)
                    dve.tensor_tensor(dts[:, 0, :].rearrange("p (t n) -> p t n", t=NT),
                                      psT[:, 0:2 * 64].rearrange("p (t n) -> p t n", t=NT)[:, :, 0:SSM_H],
                                      par("dt_bias").unsqueeze(1).broadcast_to([P, NT, SSM_H]), ALU.add)
                    sync()
                    dve.tensor_scalar(dts[:, 1, :], dts[:, 0, :], -1.0, None, ALU.mult)
                    sync()
                    dve.tensor_tensor(dts[:, 1, :], dts[:, 1, :], dts[:, 0, :], ALU.min).then_inc(dt_step, 1)
                elif what == "dt_u":
                    dve.wait_ge(dt_act, 1)
                    dve.tensor_scalar(dts[:, 3, :], dts[:, 2, :], 1.0, None, ALU.add).then_inc(dt_step, 1)
                elif what == "dt_end":
                    sync()
                    dve.tensor_scalar(dts[:, 9, :], dts[:, 3, :], 1.0, None, ALU.subtract)
                    sync()
                    dve.tensor_scalar(dts[:, 10, :], dts[:, 9, :], 1e-30, None, ALU.max)
                    dve.tensor_scalar(dts[:, 11, :], dts[:, 9, :], 0.0, None, ALU.is_equal)
                    sync()
                    dve.reciprocal(dts[:, 10, :], dts[:, 10, :])
                    dve.tensor_tensor(dts[:, 11, :], dts[:, 11, :], dts[:, 2, :], ALU.mult)
                    dve.wait_ge(dt_act, 2)
                    dve.tensor_tensor(dts[:, 9, :], dts[:, 4, :], dts[:, 2, :], ALU.mult)
                    sync()
                    dve.tensor_tensor(dts[:, 9, :], dts[:, 9, :], dts[:, 10, :], ALU.mult)
                    sync()
                    dve.tensor_tensor(dts[:, 9, :], dts[:, 9, :], dts[:, 11, :], ALU.add)
                    sync()
                    dve.scalar_tensor_tensor(dts[:, 5, :], dts[:, 0, :], 0.0, dts[:, 9, :], ALU.max, ALU.add)
                    sync()
                    dve.scalar_tensor_tensor(dts[:, 6, :].rearrange("p (t n) -> p t n", t=NT),
                                             dts[:, 5, :].rearrange("p (t n) -> p t n", t=NT), -1.0,
                                             dts[:, 8, 0:SSM_H].unsqueeze(1).broadcast_to([P, NT, SSM_H]),
                                             ALU.mult, ALU.mult).then_inc(dt_step, 1)
                elif what == "swap":
                    n, k = d["n"], d["k"]
                    if kind == "q":
                        first, _ = rotate(q2[:, 4 * n:4 * n + 4, :], cos2[:, :], sin2[:, :], k, DEPTH * 2 + n, 4, attn[:, 0, :])
                        first.then_inc(acc_free[k % 2], 1)
                    else:
                        _, last = rotate(k2[:, :, :], cos2[:, :], sin2[:, :], k, DEPTH * 2 + 2, 2, attn[:, 0, :])
                        last.then_inc(acc_free[k % 2], 1)
                elif what == "back":
                    n, c = d["n"], d["c"]
                    dve.wait_ge(back_ready, d["b"] + 1)
                    dst = bt[:, :] if n == 0 else ys[:, c, 512 * (n - 2):512 * (n - 1)]
                    dve.tensor_copy(dst, psS[:, 512:1024]).then_inc(back_read, 1)
                elif what == "head_scores":
                    if d["h"] == 0:
                        dve.wait_ge(near_loaded, 16)
                    dve.wait_ge(scores_ready, HB + d["h"] + 1)
                    dve.scalar_tensor_tensor(prob2[:, :], psS[:, 0:384], HD ** -0.5, cst("causal"), ALU.mult, ALU.add)
                    sync()
                    dve.tensor_reduce(negmax[:, 1:2], prob2[:, 0:256], AX_X, ALU.max)
                    dve.tensor_reduce(negmax[:, 3:4], prob2[:, 256:384], AX_X, ALU.max)
                    sync()
                    sink = par("sinks", d["h"], d["h"] + 1)
                    dve.tensor_scalar(negmax[:, 0:1], negmax[:, 1:2], sink, -1.0, ALU.max, ALU.mult)
                    dve.tensor_scalar(negmax[:, 2:3], negmax[:, 3:4], sink, -1.0, ALU.max, ALU.mult)\
                        .then_inc(negmax_ready, 1)
                elif what == "head_weights":
                    dve.wait_ge(exp_ready, HB + d["h"] + 1)
                    sync()
                    for j in (0, 2):
                        dve.tensor_tensor(rinv[:, j:j + 1], sums[:, j:j + 1], sums[:, j + 1:j + 2], ALU.add)
                    sync()
                    for j in (0, 2):
                        dve.reciprocal(rinv[:, j:j + 1], rinv[:, j:j + 1])
                    sync()
                elif what == "head_out":
                    h = d["h"]
                    dve.wait_ge(pv_ready, HB + h + 1)
                    dve.tensor_scalar(attn[:, 0, HD * h:HD * h + HD], psO[:, 0:HD], rinv[:, 2:3], None, ALU.mult)
                    dve.tensor_scalar(attn[:, 1, HD * h:HD * h + HD], psO[:, HD:2 * HD], rinv[:, 0:1], None, ALU.mult)\
                        .then_inc(head_read, 1)
                elif what == "decay":
                    dve.wait_ge(acs_ready, 1)
                    dve.tensor_copy(dts[:, 7, :], psO[:, 0:64])
                    sync()
                    dve.tensor_tensor(dts[:, 10, 0:32], psO[:, 64:96], dts[:, 7, 0:32], ALU.subtract)
                    dve.tensor_copy(dts[:, 10, 32:64], psO[:, 32:64]).then_inc(decay_in, 1)
                    for c in range(NT):
                        dve.tensor_tensor(by_head(xd[:, c, :]), by_head(ys[:, c, :]),
                                          dts[:, 5, 32 * c:32 * c + 32].unsqueeze(2).to_broadcast([P, SSM_H, SSM_P]),
                                          ALU.mult)
                    sync()
                    for c in range(NT):
                        dve.tensor_tensor(by_head(ys[:, c, :]), by_head(ys[:, c, :]),
                                          par("d_skip").unsqueeze(2).to_broadcast([P, SSM_H, SSM_P]), ALU.mult)
                elif what == "decay_exp":
                    sync()
                    dve.wait_ge(decay_ready, 1)
                elif what == "group_cb":
                    grp = d["grp"]
                    sync()
                    dve.wait_ge(cb_ready, grp + 1)
                    dve.tensor_tensor(cbm[:, :, :], psS[:, 0:256].rearrange("p (c n) -> p c n", c=NT),
                                      tri.unsqueeze(1).broadcast_to([P, NT, P]), ALU.mult).then_inc(cb_read, 1)
                    wait(dve, state_ps, grp)
                    dve.tensor_tensor(by_head(xw[:, :]), by_head(xd[:, 0, 512 * grp:512 * grp + 512]),
                                      dts[:, 9, 8 * grp:8 * grp + 8].unsqueeze(2).to_broadcast([P, 8, SSM_P]),
                                      ALU.mult).then_inc(xw_ready, 1)
                elif what == "group_off":
                    grp = d["grp"]
                    dve.wait_ge(off_ready, grp + 1)
                    dve.tensor_tensor(by_head(act_out[:, 0, :]), by_head(psS[:, 512:1024]),
                                      dts[:, 9, 32 + 8 * grp:40 + 8 * grp].unsqueeze(2).to_broadcast([P, 8, SSM_P]),
                                      ALU.mult).then_inc(off_read, 1)
                    sync()
                    y1 = ys[:, 1, 512 * grp:512 * grp + 512]
                    dve.tensor_tensor(y1, y1, act_out[:, 0, :], ALU.add)
                    sync()
                elif what == "unit_rows":
                    u, c, h0 = d["u"], d["c"], d["h0"]
                    dve.wait_ge(rows_ready, u + 1)
                    if u >= 2:
                        dve.wait_ge(diag_out, u - 1)
                    for j in range(4):
                        col = 32 * c + h0 + j
                        m = dve.tensor_scalar(decay[:, u % 2, P * j:P * j + P], psT[:, P * j:P * j + P],
                                              dts[:, 7, col:col + 1], 0.0, ALU.subtract, ALU.min)
                    m.then_inc(diff_ready, 1)
                elif what == "unit_mask":
                    u, c = d["u"], d["c"]
                    dve.wait_ge(unit_exp, u + 1)
                    dd = decay[:, u % 2, :].rearrange("p (j n) -> p j n", j=4)
                    dve.tensor_tensor(dd, dd, cbm[:, c, :].unsqueeze(1).broadcast_to([P, 4, P]), ALU.mult)\
                        .then_inc(unit_ready, 1)
                elif what == "unit_out":
                    u, c, h0 = d["u"], d["c"], d["h0"]
                    dve.wait_ge(diag_out, u + 1)
                    yy = ys[:, c, 64 * h0:64 * h0 + 256]
                    dve.tensor_tensor(yy, yy, psO[:, 0:256], ALU.add).then_inc(diag_read, 1)
                    if u == 15:
                        sync()

            flat = act_out[:, :, :].rearrange("p t n -> p (t n)")
            for f in FFN_PARTS:
                with dve.Fori(0, f["hbs"]) as i:
                    sync()
                    dve.wait_ge(w_used, 16 * i + (f["g_up"] + 8))
                    dve.tensor_tensor(chunks_of(flat, 4), chunks_of(acc[GATE], 4), by_token(4), ALU.mult)\
                        .then_inc(acc_free[GATE], 1)
                    dve.wait_ge(w_used, 16 * i + (f["g_up"] + 16))
                    dve.tensor_tensor(chunks_of(junk, 4), chunks_of(acc[UP], 4), by_token(4), ALU.mult)\
                        .then_inc(acc_free[UP], 1)
                    sync()
                    dve.wait_ge(gate_done, i + (f["done"] + 1))
                    dve.tensor_tensor(flat, flat, junk[:, :], ALU.mult).then_inc(hid_ready, 1)
                    sync()
                    dve.wait_ge(hid_hi, i + (f["done"] + 1))
                    dve.tensor_tensor(fl[:, bass.ds(4 * i, 4), :].rearrange("p c s -> p (c s)"), flat,
                                      fh[:, bass.ds(4 * i, 4), :].rearrange("p c s -> p (c s)").bitcast(F32),
                                      ALU.subtract).then_inc(hid_lo, 1)
                per = 2 * f["hbs"]
                if f is FFN_PARTS[0]:
                    dve.wait_ge(p_hi, 1)
                    dve.tensor_tensor(pl[:, :, :], praw[:, :, :], ph[:, :, :].bitcast(F32), ALU.subtract).then_inc(p_lo, 1)
                if f is not FFN_PARTS[-1]:
                    with dve.Fori(0, 2) as i:
                        for side in range(2):
                            k = f["k_dn"] + side
                            xc = x[:, :, bass.ds(1024 * i + 512 * side, 512)]
                            dve.wait_ge(w_used, 2 * per * i + (f["g_dn"] + per * (side + 1)))
                            dve.tensor_tensor(xc, xc, acc[k % 2][:, :].rearrange("p (t n) -> p t n", t=NT),
                                              ALU.add).then_inc(acc_free[k % 2], 1)
                    sync()
            for what, d in DOWN.items:
                if what == "turn":
                    turn_rest("ple", d["m"], T_DOWN + d["t"])
                elif what == "evac":
                    n, k = d["n"], K_DOWN + d["k"]
                    cols = slice(512 * n, 512 * n + 512)
                    dve.wait_ge(w_used, G_DOWN + d["g"])
                    dve.tensor_tensor(x[:, :, cols], x[:, :, cols], acc[k % 2][:, :].rearrange("p (t n) -> p t n", t=NT),
                                      ALU.add).then_inc(acc_free[k % 2], 1)
                    squares(x, n)

            def last_gain(n):
                sync()
                for t in range(NT):
                    xc = x[:, t, 512 * n:512 * n + 512]
                    dve.tensor_tensor(xc, xc, gain2[:, 512 * n:512 * n + 512], ALU.mult)

            for what, d in PLE.items:
                if what == "root":
                    mean_of_quarters(1e-6)
                elif what == "inverse":
                    dve.wait_ge(root_ready, S2 + ROOT["ple"] + 1)
                    dve.reciprocal(rs[:, 0:2], stat[:, 32:34]).then_inc(r_ready, 1)
                elif what == "turn":
                    turn_rest("ple", d["m"], T_PLE + d["t"])
                elif what == "evac" and d["kind"] == "proj":
                    n, k = d["n"], K_PLE + d["k"]
                    cols = slice(512 * n, 512 * n + 512)
                    if n:
                        last_gain(n - 1)
                    sync()
                    moved(dve, k - 1)
                    dve.wait_ge(w_used, G_PLE + d["g"])
                    dve.tensor_tensor(flat, flat, acc[k % 2][:, :], ALU.mult).then_inc(acc_free[k % 2], 1)
                    sync()
                    dve.tensor_tensor(x[:, :, cols], x[:, :, cols], act_out[:, :, :], ALU.add).then_inc(act_read, 1)
                    squares(x, n)
                    if n == 0:
                        dve.wait_ge(gain2_loaded, 16)
            mean_of_quarters(1e-6)
            last_gain(3)
            dve.wait_ge(root_ready, S2 + 6)
            dve.reciprocal(rs[:, 0:2], stat[:, 32:34]).then_inc(r_ready, 1)
            sync()
            dve.tensor_scalar(x[:, 1, :], x[:, 1, :], rs[:, 1:2], None, ALU.mult).then_inc(result_ready[1], 1)


def _pack(table, width, parts, rows=P):
    a = np.zeros((rows, width), np.float32)
    for name, v in parts.items():
        at, w = table[name]
        a[:, at:at + w] = v
    return a


def _columns(v):
    return np.asarray(v).reshape(-1, P).T


def _granules(w, cols, chunks=2):
    w = w[:, cols]
    k, n = w.shape
    return w.reshape(k // P // chunks, chunks, P, n).transpose(0, 2, 1, 3).reshape(-1, P, chunks * n)


def _constants():
    i = np.arange(P)
    rot = np.zeros((P, P), np.float32)
    for d in range(P):
        if d % 64 < 32:
            rot[d + 32, d] = -1.0
        else:
            rot[d - 32, d] = 1.0
    diag = np.where(i[None, :] > i[:, None], NEG, 0.0)
    none = np.zeros((P, P))
    near = np.where(i[None, :] > i[:, None], 0.0, NEG)
    inv = (1.0 / (np.float32(10000.0) ** (np.arange(0, 64, 2, dtype=np.float32) / np.float32(64)))).astype(np.float32)
    ang = (np.arange(S, dtype=np.float32)[None, :] * inv[i % 32][:, None]).astype(np.float32).astype(np.float64)
    return _pack(CONST_COLS, CONST_W, dict(
        ident=np.eye(P), rot=rot, tri=(i[:, None] <= i[None, :]), flip=np.eye(P)[::-1],
        causal=np.concatenate([none, diag, diag], 1), near=near,
        cos=np.cos(ang), sin=np.sin(ang)))


def _bias_onehot():
    dist = 255 - np.arange(383)
    n = np.maximum(dist, 0)
    nf = np.maximum(n, 1).astype(np.float32)
    large = 16 + (np.log(nf / np.float32(16)) / np.float32(math.log(8)) * np.float32(16)).astype(np.int32)
    bucket = np.where(n < 16, n, np.minimum(large, 31))
    a = np.zeros((33, 384), np.float32)
    a[bucket[dist >= 0], np.nonzero(dist >= 0)[0]] = 1.0
    a[32, :383] = np.where(dist < 0, NEG, 0.0)
    return a


def _weights(i):
    blocks = []
    add = lambda w, cols, chunks=2: blocks.append(_granules(w, cols, chunks))
    span = lambda a, n=512: np.arange(a, a + n)
    for l in range(DEPTH):
        w = i["w_in"][l]
        for at in (0, 512, 1024, 1536, 2048, 2560, 4096, 4608):
            add(w, span(at))
        add(w, np.concatenate([span(5120, 64)] * 2), 8)
        add(w, span(3072))
        uq, ukv = i["w_uq"][l], i["w_ukv"][l]
        for half in range(2):
            add(uq, np.concatenate([span(192 * h, 128) for h in range(4 * half, 4 * half + 4)]))
        add(uq, np.concatenate([span(192 * h + 128, 64) for h in range(MH)]))
        for off in (0, 128):
            for half in range(2):
                add(ukv, np.concatenate([span(256 * h + off, 128) for h in range(4 * half, 4 * half + 4)]))
        for at in (3584, 5184, 5696):
            add(w, span(at))
        for n in range(4):
            add(i["w_out"][l], span(512 * n))
    w = i["w_in_2"][0]
    for at in (0, 512, 1024, 5632, 6144, 3584, 4096, 4608, 5120):
        add(w, span(at))
    dt = np.zeros((D, 64), np.float32)
    dt[:, :SSM_H] = w[:, 6656:6688]
    add(dt, span(0, 64), 16)
    for first in (6688, 8736, 1536):
        for n in range(4):
            add(w, span(first + 512 * n))
    for name in ("w_attn_br_2", "w_ssd_br_2", "w_o_2"):
        for n in range(4):
            add(i[name][0], span(512 * n))
    for f in FFN_PARTS:
        a, b = f["done"], f["done"] + f["hbs"]
        for hb in range(a, b):
            add(i["w_gate_2"][0], span(512 * hb))
            add(i["w_up_2"][0], span(512 * hb))
        for n in range(4):
            add(i["w_down_2"][0][512 * a:512 * b], span(512 * n))
    for n in range(4):
        add(i["w_ple_gate_2"][0], span(512 * n))
        add(i["w_ple_proj_2"][0], span(512 * n))
    return np.concatenate(blocks, 0)


def kernel(**inputs):
    import concourse.bacc as bacc
    from concourse.bass_utils import run_bass_kernel_spmd

    i = {k: np.asarray(v) for k, v in inputs.items()}
    row = lambda v: np.broadcast_to(np.asarray(v).reshape(1, -1), (P, np.asarray(v).size))
    layer_small = []
    for l in range(DEPTH):
        lambda_init = 0.8 - 0.6 * math.exp(-0.3 * l)
        layer_small.append(_pack(LAYER_COLS, LAYER_W, {
            "norm": _columns(i["norm_g"][l]),
            "next_norm": _columns(i["norm_g"][l + 1]) if l + 1 < DEPTH else 0.0, "q_norm": _columns(i["mla_q_norm_g"][l]),
            "kv_norm": _columns(i["mla_kv_norm_g"][l]), "lam_init": lambda_init, "one_minus": 1.0 - lambda_init,
            "lambda": row(i["diff_lambda"][l]), "subln": row(i["diff_subln_g"][l])}))
    order = np.concatenate([np.arange(2048, 3072), np.arange(0, 2048)])
    conv_w = i["conv_w_2"][0][:, order].reshape(TAPS, 24, P).transpose(2, 1, 0).reshape(P, 24 * TAPS)
    inv = (np.float32(10000.0) ** (-np.arange(32, dtype=np.float32) * np.float32(2.0) / np.float32(64))).astype(np.float32)
    block2_small = _pack(BLOCK2_COLS, BLOCK2_W, {
        "final1": _columns(i["final_norm_g"]),
        "mix": _columns(i["g_mix_2"][0]), "ffn": _columns(i["g_ffn_2"][0]), "ple": _columns(i["g_ple_2"][0]),
        "ssd": _columns(i["g_ssd_2"][0]), "conv_w": conv_w, "conv_b": _columns(i["conv_b_2"][0][order]),
        "dt_bias": row(i["dt_bias_2"][0]), "a_log": row(i["a_log_2"][0]), "d_skip": row(i["d_skip_2"][0]),
        "sinks": row(i["sinks_2"][0]), "inv_freq": inv[np.arange(P) % 32][:, None]})
    bias_rows = np.concatenate([i["rel_bias_table"], np.ones((1, DH), np.float32)], 0)
    arrays = {
        "wstream": _weights(i), "x_in": np.ascontiguousarray(i["x"][0]),
        "p_in": np.ascontiguousarray(i["p_2"][0, 0].T.reshape(2, P, S).transpose(1, 0, 2)),
        "positions": np.ascontiguousarray(i["positions_2"].reshape(S)),
        "layer_small": np.stack(layer_small), "block2_small": block2_small, "const_in": _constants(),
        "bias_rows": bias_rows, "bias_onehot": _bias_onehot(),
        "gain_final1": np.ascontiguousarray(row(i["final_norm_g"])),
        "gain_final2": np.ascontiguousarray(row(i["g_final_2"])),
    }
    nc = bacc.Bacc("TRN2", target_bir_lowering=False, num_devices=1)
    args = [nc.dram_tensor(n, a.shape, mybir.dt.from_np(a.dtype), kind="ExternalInput").ap()
            for n, a in arrays.items()]
    args.append(nc.dram_tensor("out", (S, D), F32, kind="ExternalOutput").ap())
    build(nc, *args)
    r = run_bass_kernel_spmd(nc, [arrays], core_ids=[0])
    return r.results[0]["out"].reshape(1, S, D)
```
